# Optimizing a Trainium2 kernel written in Bass

```python
import math
import jax
import jax.numpy as jnp
from jax import lax
import numpy as np
import jax, jax.numpy as jnp

D_MODEL = 1024
BATCH = 1
SEQ = 512
DEPTH = 2

GRID_W = 64
CTX_LEN = 256
N_MIXERS = 2
N_MLA = (DEPTH + 1) // 2
N_HYENA = DEPTH // 2

MLA_HEADS = 16
QK_NOPE = 64
QK_ROPE = 32
QK_DIM = QK_NOPE + QK_ROPE
V_HEAD = 64
Q_LORA = 512
KV_LORA = 256
ROPE_THETA = 10000.0
Q_BLOCK = 128

HY_BANDS = 16
HY_POS_DIM = 1 + 2 * HY_BANDS
HY_FILTER_HIDDEN = 64
HY_DECAY_SLOW = math.log(100.0) / 1.5
HY_DECAY_FAST = math.log(100.0) / 0.3
HY_FILTER_INIT = 0.02

D_FF = 2816

EPS = 1e-6
F32 = jnp.float32


def rmsnorm(x, g):
    xf = x.astype(F32)
    y = xf * lax.rsqrt(jnp.mean(xf * xf, axis=-1, keepdims=True) + EPS)
    return (y * g.astype(F32)).astype(x.dtype)

def modulate(h, shift, scale):
    return h * (1 + scale) + shift

def dwconv3(x, w, b):
    xp = jnp.pad(x, ((0, 0), (1, 1), (0, 0)))
    return xp[:, :-2] * w[0] + xp[:, 1:-1] * w[1] + xp[:, 2:] * w[2] + b

def axial_rope_tables(rows):
    row = jnp.repeat(jnp.arange(rows, dtype=F32), GRID_W)
    col = jnp.tile(jnp.arange(GRID_W, dtype=F32), rows)
    half = QK_ROPE // 2
    inv_freq = ROPE_THETA ** (-jnp.arange(0, half, 2, dtype=F32) / half)
    ang_r = row[:, None] * inv_freq
    ang_c = col[:, None] * inv_freq
    ang = jnp.concatenate([ang_r, ang_r, ang_c, ang_c], axis=-1)
    return jnp.cos(ang), jnp.sin(ang)

def apply_axial_rope(x, cos, sin):
    q = QK_ROPE // 4
    xf = x.astype(F32)
    rot = jnp.concatenate([-xf[..., q:2 * q], xf[..., :q], -xf[..., 3 * q:], xf[..., 2 * q:3 * q]], axis=-1)
    return (xf * cos + rot * sin).astype(x.dtype)

def mla_queries(h, w_dq, g_q, w_uq, cos, sin):
    B, L, _ = h.shape
    cq = rmsnorm(h @ w_dq, g_q)
    q = (cq @ w_uq).reshape(B, L, MLA_HEADS, QK_DIM)
    q_nope, q_pe = q[..., :QK_NOPE], q[..., QK_NOPE:]
    if cos is not None:
        q_pe = apply_axial_rope(q_pe, cos[None, :, None, :], sin[None, :, None, :])
    return jnp.concatenate([q_nope, q_pe], axis=-1)

def mla_keys_values(h, w_dkv, g_kv, w_uk, w_uv, cos, sin):
    B, L, _ = h.shape
    kv = h @ w_dkv
    ckv = rmsnorm(kv[..., :KV_LORA], g_kv)
    k_pe = kv[..., KV_LORA:]
    if cos is not None:
        k_pe = apply_axial_rope(k_pe, cos[None], sin[None])
    k_nope = (ckv @ w_uk).reshape(B, L, MLA_HEADS, QK_NOPE)
    v = (ckv @ w_uv).reshape(B, L, MLA_HEADS, V_HEAD)
    k_pe = jnp.broadcast_to(k_pe[:, :, None, :], (B, L, MLA_HEADS, QK_ROPE))
    return jnp.concatenate([k_nope, k_pe], axis=-1), v

def block_attention(q, k, v):
    B, Lq, H, dk = q.shape
    nblk = Lq // Q_BLOCK
    scale = 1.0 / math.sqrt(dk)
    qb = q.reshape(B, nblk, Q_BLOCK, H, dk).transpose(1, 0, 2, 3, 4)

    def one_block(qblk):
        s = jnp.einsum('bqhd,bkhd->bhqk', qblk, k).astype(F32) * scale
        p = jax.nn.softmax(s, axis=-1).astype(v.dtype)
        return jnp.einsum('bhqk,bkhd->bqhd', p, v)

    o = lax.map(one_block, qb)
    return o.transpose(1, 0, 2, 3, 4).reshape(B, Lq, H * v.shape[-1])

def hyena_pos_features(L):
    t = jnp.linspace(0.0, 1.0, L, dtype=F32)
    w = 2.0 * math.pi * jnp.arange(L, dtype=F32) / L
    f = jnp.linspace(1e-4, HY_BANDS - 1, HY_BANDS, dtype=F32)
    z = jnp.concatenate([t[:, None], jnp.cos(w[:, None] * f), -jnp.sin(w[:, None] * f)], axis=-1)
    return t, z

def hyena_filters(L, f_w1, f_b1, f_freq1, f_w2, f_b2, f_freq2, f_w3, decay):
    t, z = hyena_pos_features(L)
    h = jnp.sin(f_freq1.astype(F32) * (z @ f_w1.astype(F32) + f_b1.astype(F32)))
    h = jnp.sin(f_freq2.astype(F32) * (h @ f_w2.astype(F32) + f_b2.astype(F32)))
    h = h @ f_w3.astype(F32)
    window = jnp.exp(-t[:, None] * jnp.abs(decay.astype(F32))[None, :])
    d = h.shape[1] // 2
    return h[:, :d] * window, h[:, d:] * window

def two_sided_fftconv(u, h_fwd, h_bwd):
    L = u.shape[1]
    filt = jnp.concatenate([h_fwd, jnp.zeros((1, h_fwd.shape[1]), F32), h_bwd[1:][::-1]], axis=0)
    filt_f = jnp.fft.rfft(filt, n=2 * L, axis=0)
    u_f = jnp.fft.rfft(u.astype(F32), n=2 * L, axis=1)
    y = jnp.fft.irfft(u_f * filt_f[None], n=2 * L, axis=1)[:, :L]
    return y.astype(u.dtype)

def hyena_mixer(u, w_in, b_in, conv_w, conv_b, f_w1, f_b1, f_freq1, f_w2, f_b2, f_freq2, f_w3, decay, d_bias, w_out, b_out):
    L = u.shape[1]
    z = dwconv3(u @ w_in + b_in, conv_w, conv_b)
    x1, x2, v = jnp.split(z, 3, axis=-1)
    h_fwd, h_bwd = hyena_filters(L, f_w1, f_b1, f_freq1, f_w2, f_b2, f_freq2, f_w3, decay)
    v = v * x2
    y = (two_sided_fftconv(v, h_fwd, h_bwd) + v * d_bias) * x1
    return y @ w_out + b_out

def conv_ffn(h, w_up, conv_w, conv_b, w_down):
    z = dwconv3(h @ w_up, conv_w, conv_b)
    a, g = jnp.split(z, 2, axis=-1)
    return (jax.nn.silu(g) * a) @ w_down

def first_inputs(seed: int = 0) -> dict:
    key = jax.random.key(seed)
    ks = jax.random.split(key, 40)
    D = D_MODEL

    def nrm(i, shape, scale):
        return jax.random.normal(ks[i], shape, F32) * scale

    def gain(i, shape):
        return 1.0 + nrm(i, shape, 0.05)

    decay_base = jnp.linspace(HY_DECAY_SLOW, HY_DECAY_FAST, D, dtype=F32)
    return {
        'x': nrm(0, (BATCH, SEQ, D), 1.0),
        'c': nrm(1, (BATCH, D), 1.0),
        'ctx': nrm(2, (BATCH, CTX_LEN, D), 1.0),
        'c_ctx': nrm(3, (D,), 1.0),
        'mod_w': nrm(4, (DEPTH, D, 6 * D), D ** -0.5),
        'mod_b': nrm(5, (DEPTH, 6 * D), 0.02),
        'norm_mix_g': gain(6, (DEPTH, D)),
        'norm_ffn_g': gain(7, (DEPTH, D)),
        'mla_w_dq': nrm(8, (N_MLA, D, Q_LORA), D ** -0.5),
        'mla_g_q': gain(9, (N_MLA, Q_LORA)),
        'mla_w_uq': nrm(10, (N_MLA, Q_LORA, MLA_HEADS * QK_DIM), Q_LORA ** -0.5),
        'mla_w_dkv': nrm(11, (N_MLA, D, KV_LORA + QK_ROPE), D ** -0.5),
        'mla_g_kv': gain(12, (N_MLA, KV_LORA)),
        'mla_w_uk': nrm(13, (N_MLA, KV_LORA, MLA_HEADS * QK_NOPE), KV_LORA ** -0.5),
        'mla_w_uv': nrm(14, (N_MLA, KV_LORA, MLA_HEADS * V_HEAD), KV_LORA ** -0.5),
        'mla_w_o': nrm(15, (N_MLA, MLA_HEADS * V_HEAD, D), (MLA_HEADS * V_HEAD) ** -0.5),
        'hy_w_in': nrm(16, (N_HYENA, D, 3 * D), D ** -0.5),
        'hy_b_in': nrm(17, (N_HYENA, 3 * D), 0.02),
        'hy_conv_w': nrm(18, (N_HYENA, 3, 3 * D), 3 ** -0.5),
        'hy_conv_b': nrm(19, (N_HYENA, 3 * D), 0.02),
        'hy_f_w1': nrm(20, (N_HYENA, HY_POS_DIM, HY_FILTER_HIDDEN), HY_POS_DIM ** -0.5),
        'hy_f_b1': nrm(21, (N_HYENA, HY_FILTER_HIDDEN), 0.1),
        'hy_f_freq1': gain(22, (N_HYENA, HY_FILTER_HIDDEN)),
        'hy_f_w2': nrm(23, (N_HYENA, HY_FILTER_HIDDEN, HY_FILTER_HIDDEN), HY_FILTER_HIDDEN ** -0.5),
        'hy_f_b2': nrm(24, (N_HYENA, HY_FILTER_HIDDEN), 0.1),
        'hy_f_freq2': gain(25, (N_HYENA, HY_FILTER_HIDDEN)),
        'hy_f_w3': nrm(26, (N_HYENA, HY_FILTER_HIDDEN, 2 * D), HY_FILTER_INIT),
        'hy_decay': decay_base[None, :] * (1.0 + nrm(27, (N_HYENA, D), 0.05)),
        'hy_d_bias': nrm(28, (N_HYENA, D), 1.0),
        'hy_w_out': nrm(29, (N_HYENA, D, D), D ** -0.5),
        'hy_b_out': nrm(30, (N_HYENA, D), 0.02),
        'ffn_w_up': nrm(31, (DEPTH, D, 2 * D_FF), D ** -0.5),
        'ffn_conv_w': nrm(32, (DEPTH, 3, 2 * D_FF), 3 ** -0.5),
        'ffn_conv_b': nrm(33, (DEPTH, 2 * D_FF), 0.02),
        'ffn_w_down': nrm(34, (DEPTH, D_FF, D), D_FF ** -0.5),
        'final_g': gain(35, (D,)),
    }

def first_block(x, c, ctx, c_ctx, mod_w, mod_b, norm_mix_g, norm_ffn_g,
              mla_w_dq, mla_g_q, mla_w_uq, mla_w_dkv, mla_g_kv, mla_w_uk, mla_w_uv, mla_w_o,
              hy_w_in, hy_b_in, hy_conv_w, hy_conv_b, hy_f_w1, hy_f_b1, hy_f_freq1, hy_f_w2, hy_f_b2,
              hy_f_freq2, hy_f_w3, hy_decay, hy_d_bias, hy_w_out, hy_b_out,
              ffn_w_up, ffn_conv_w, ffn_conv_b, ffn_w_down, final_g):
    L = x.shape[1]
    ROWS = L // GRID_W
    cos, sin = axial_rope_tables(ROWS)
    silu_c = jax.nn.silu(c)
    silu_cc = jax.nn.silu(c_ctx)
    h_ctx = ctx
    for i in range(DEPTH):
        last = i == DEPTH - 1
        j = i // N_MIXERS
        mod_x = silu_c @ mod_w[i] + mod_b[i]
        mod_c = silu_cc @ mod_w[i] + mod_b[i]
        sh1, sc1, g1, sh2, sc2, g2 = [m[:, None, :] for m in jnp.split(mod_x, 6, axis=-1)]
        csh1, csc1, cg1, csh2, csc2, cg2 = jnp.split(mod_c, 6, axis=-1)
        hx = modulate(rmsnorm(x, norm_mix_g[i]), sh1, sc1)
        if i % N_MIXERS == 0:
            hc = modulate(rmsnorm(h_ctx, norm_mix_g[i]), csh1, csc1)
            qx = mla_queries(hx, mla_w_dq[j], mla_g_q[j], mla_w_uq[j], cos, sin)
            kx, vx = mla_keys_values(hx, mla_w_dkv[j], mla_g_kv[j], mla_w_uk[j], mla_w_uv[j], cos, sin)
            kc, vc = mla_keys_values(hc, mla_w_dkv[j], mla_g_kv[j], mla_w_uk[j], mla_w_uv[j], None, None)
            ox = block_attention(qx, jnp.concatenate([kc, kx], axis=1), jnp.concatenate([vc, vx], axis=1))
            x = x + g1 * (ox @ mla_w_o[j])
            if not last:
                qc = mla_queries(hc, mla_w_dq[j], mla_g_q[j], mla_w_uq[j], None, None)
                oc = block_attention(qc, kc, vc)
                h_ctx = h_ctx + cg1 * (oc @ mla_w_o[j])
        else:
            hy = (hy_w_in[j], hy_b_in[j], hy_conv_w[j], hy_conv_b[j], hy_f_w1[j], hy_f_b1[j], hy_f_freq1[j],
                  hy_f_w2[j], hy_f_b2[j], hy_f_freq2[j], hy_f_w3[j], hy_decay[j], hy_d_bias[j],
                  hy_w_out[j], hy_b_out[j])
            x = x + g1 * hyena_mixer(hx, *hy)
            if not last:
                hc = modulate(rmsnorm(h_ctx, norm_mix_g[i]), csh1, csc1)
                h_ctx = h_ctx + cg1 * hyena_mixer(hc, *hy)
        ffn = (ffn_w_up[i], ffn_conv_w[i], ffn_conv_b[i], ffn_w_down[i])
        x = x + g2 * conv_ffn(modulate(rmsnorm(x, norm_ffn_g[i]), sh2, sc2), *ffn)
        if not last:
            h_ctx = h_ctx + cg2 * conv_ffn(modulate(rmsnorm(h_ctx, norm_ffn_g[i]), csh2, csc2), *ffn)
    return rmsnorm(x, final_g)


DEPTH_2 = 1

SSM_WIDTH = D_MODEL // 2
SSM_GROUP_SIZE = 16
SSM_GROUPS = SSM_WIDTH // SSM_GROUP_SIZE
SSM_STATE = 64
DT_MIN = 1e-3
DT_MAX = 1e-1
POOL_WIDTH = D_MODEL // 2
POOL_WINDOWS = (2, 4, 8, 16)
POOL_GROUPS = len(POOL_WINDOWS)
POOL_GROUP = POOL_WIDTH // POOL_GROUPS
N_IN = 2 * SSM_WIDTH + 2 * POOL_WIDTH + 2 * D_MODEL
SPLITS = (SSM_WIDTH, 2 * SSM_WIDTH, 2 * SSM_WIDTH + POOL_WIDTH,
          2 * SSM_WIDTH + 2 * POOL_WIDTH, 2 * SSM_WIDTH + 2 * POOL_WIDTH + D_MODEL)


def _rmsnorm(x, g):
    x32 = x.astype(jnp.float32)
    y = x32 * lax.rsqrt(jnp.mean(x32 * x32, axis=-1, keepdims=True) + EPS)
    return y.astype(x.dtype) * g

def _complex_linear_combine(left, right):
    a1r, a1i, b1r, b1i = left
    a2r, a2i, b2r, b2i = right
    ar = a2r * a1r - a2i * a1i
    ai = a2r * a1i + a2i * a1r
    br = a2r * b1r - a2i * b1i + b2r
    bi = a2r * b1i + a2i * b1r + b2i
    return ar, ai, br, bi

def _s5_branch(u, log_dt, lam_re, lam_im, b_re, b_im, c_re, c_im, d_skip, w_glu, b_glu):
    bsz, seq, _ = u.shape
    ug = u.reshape(bsz, seq, SSM_GROUPS, SSM_GROUP_SIZE)
    dt = jnp.exp(log_dt)[:, None]
    mag = jnp.exp(lam_re * dt)
    ang = lam_im * dt
    abar_re = mag * jnp.cos(ang)
    abar_im = mag * jnp.sin(ang)
    num_re = abar_re - 1.0
    num_im = abar_im
    den = lam_re * lam_re + lam_im * lam_im
    coef_re = (num_re * lam_re + num_im * lam_im) / den
    coef_im = (num_im * lam_re - num_re * lam_im) / den
    bbar_re = coef_re[..., None] * b_re - coef_im[..., None] * b_im
    bbar_im = coef_re[..., None] * b_im + coef_im[..., None] * b_re
    bu_re = jnp.einsum('blgc,gpc->blgp', ug, bbar_re)
    bu_im = jnp.einsum('blgc,gpc->blgp', ug, bbar_im)
    a_re = jnp.broadcast_to(abar_re, bu_re.shape)
    a_im = jnp.broadcast_to(abar_im, bu_im.shape)
    _, _, s_re, s_im = lax.associative_scan(_complex_linear_combine,
                                            (a_re, a_im, bu_re, bu_im), axis=1)
    y = (jnp.einsum('blgp,gcp->blgc', s_re, c_re)
         - jnp.einsum('blgp,gcp->blgc', s_im, c_im))
    y = y.reshape(bsz, seq, SSM_WIDTH) + d_skip * u
    y = jax.nn.gelu(y)
    return y * jax.nn.sigmoid(y @ w_glu + b_glu)

def _pool_branch(u, w_group, scale):
    bsz, seq, _ = u.shape
    u32 = u.astype(jnp.float32)
    cs = jnp.cumsum(u32, axis=1)
    pos = jnp.arange(seq)
    outs = []
    for gi, win in enumerate(POOL_WINDOWS):
        csg = cs[:, :, gi * POOL_GROUP:(gi + 1) * POOL_GROUP]
        shifted = jnp.pad(csg, ((0, 0), (win, 0), (0, 0)))[:, :seq]
        count = jnp.minimum(pos + 1, win).astype(jnp.float32)[None, :, None]
        mean = (csg - shifted) / count
        outs.append(mean - u32[:, :, gi * POOL_GROUP:(gi + 1) * POOL_GROUP])
    pooled = jnp.stack(outs, axis=2).astype(u.dtype)
    mixed = jnp.einsum('blgc,gcd->blgd', pooled, w_group).reshape(bsz, seq, POOL_WIDTH)
    return mixed * scale

def second_inputs(seed: int = 0) -> dict:
    key = jax.random.key(seed)
    ks = jax.random.split(key, 24)
    f32 = jnp.float32
    nrm = lambda k, shape, std: (jax.random.normal(k, shape, f32) * std)
    x = jax.random.normal(ks[0], (BATCH, SEQ, D_MODEL), f32)
    norm_g = 1.0 + nrm(ks[1], (DEPTH_2, D_MODEL), 0.05)
    w_in = nrm(ks[2], (DEPTH_2, D_MODEL, N_IN), D_MODEL ** -0.5)
    b_in = nrm(ks[3], (DEPTH_2, N_IN), 0.02)
    ssm_log_dt = jax.random.uniform(ks[4], (DEPTH_2, SSM_GROUPS), f32,
                                    math.log(DT_MIN), math.log(DT_MAX))
    n_idx = jnp.arange(SSM_STATE, dtype=f32)
    ssm_lam_re = -0.5 + nrm(ks[5], (DEPTH_2, SSM_GROUPS, SSM_STATE), 0.01)
    ssm_lam_im = math.pi * n_idx[None, None, :] + nrm(ks[6], (DEPTH_2, SSM_GROUPS, SSM_STATE), 0.01)
    b_std = (2.0 * SSM_GROUP_SIZE) ** -0.5
    ssm_b_re = nrm(ks[7], (DEPTH_2, SSM_GROUPS, SSM_STATE, SSM_GROUP_SIZE), b_std)
    ssm_b_im = nrm(ks[8], (DEPTH_2, SSM_GROUPS, SSM_STATE, SSM_GROUP_SIZE), b_std)
    c_std = SSM_STATE ** -0.5
    ssm_c_re = nrm(ks[9], (DEPTH_2, SSM_GROUPS, SSM_GROUP_SIZE, SSM_STATE), c_std)
    ssm_c_im = nrm(ks[10], (DEPTH_2, SSM_GROUPS, SSM_GROUP_SIZE, SSM_STATE), c_std)
    ssm_d = nrm(ks[11], (DEPTH_2, SSM_WIDTH), 1.0)
    ssm_w_glu = nrm(ks[12], (DEPTH_2, SSM_WIDTH, SSM_WIDTH), SSM_WIDTH ** -0.5)
    ssm_b_glu = nrm(ks[13], (DEPTH_2, SSM_WIDTH), 0.02)
    pool_w = nrm(ks[14], (DEPTH_2, POOL_GROUPS, POOL_GROUP, POOL_GROUP), POOL_GROUP ** -0.5)
    pool_scale = 1.0 + nrm(ks[15], (DEPTH_2, POOL_WIDTH), 0.1)
    w_branch_a = nrm(ks[16], (DEPTH_2, SSM_WIDTH, D_MODEL), SSM_WIDTH ** -0.5)
    w_branch_b = nrm(ks[17], (DEPTH_2, POOL_WIDTH, D_MODEL), POOL_WIDTH ** -0.5)
    w_out = nrm(ks[18], (DEPTH_2, D_MODEL, D_MODEL), D_MODEL ** -0.5)
    final_norm_g = 1.0 + nrm(ks[19], (D_MODEL,), 0.05)
    return {"x": x, "norm_g": norm_g, "w_in": w_in, "b_in": b_in,
            "ssm_log_dt": ssm_log_dt, "ssm_lam_re": ssm_lam_re, "ssm_lam_im": ssm_lam_im,
            "ssm_b_re": ssm_b_re, "ssm_b_im": ssm_b_im, "ssm_c_re": ssm_c_re, "ssm_c_im": ssm_c_im,
            "ssm_d": ssm_d, "ssm_w_glu": ssm_w_glu, "ssm_b_glu": ssm_b_glu,
            "pool_w": pool_w, "pool_scale": pool_scale,
            "w_branch_a": w_branch_a, "w_branch_b": w_branch_b, "w_out": w_out,
            "final_norm_g": final_norm_g}

def second_block(x, norm_g, w_in, b_in, ssm_log_dt, ssm_lam_re, ssm_lam_im, ssm_b_re, ssm_b_im,
              ssm_c_re, ssm_c_im, ssm_d, ssm_w_glu, ssm_b_glu, pool_w, pool_scale,
              w_branch_a, w_branch_b, w_out, final_norm_g):
    for l in range(DEPTH_2):
        h = _rmsnorm(x, norm_g[l])
        proj = h @ w_in[l] + b_in[l]
        ua, za, ub, zb, ga, gb = jnp.split(proj, SPLITS, axis=-1)
        ya = _s5_branch(ua, ssm_log_dt[l], ssm_lam_re[l], ssm_lam_im[l], ssm_b_re[l], ssm_b_im[l],
                        ssm_c_re[l], ssm_c_im[l], ssm_d[l], ssm_w_glu[l], ssm_b_glu[l])
        ya = ya * jax.nn.silu(za)
        yb = _pool_branch(ub, pool_w[l], pool_scale[l]) * jax.nn.silu(zb)
        merged = (jax.nn.sigmoid(ga) * (ya @ w_branch_a[l])
                  + jax.nn.sigmoid(gb) * (yb @ w_branch_b[l]))
        x = x + merged @ w_out[l]
    return _rmsnorm(x, final_norm_g)


def setup_inputs(seed=0):
    out = dict(first_inputs(seed))
    for name, value in second_inputs(seed + 1).items():
        if name != "x":
            out[name + "_2"] = value
    return out


def reference(
    x, c, ctx, c_ctx, mod_w, mod_b, norm_mix_g, norm_ffn_g, mla_w_dq, mla_g_q, mla_w_uq,
    mla_w_dkv, mla_g_kv, mla_w_uk, mla_w_uv, mla_w_o, hy_w_in, hy_b_in, hy_conv_w, hy_conv_b,
    hy_f_w1, hy_f_b1, hy_f_freq1, hy_f_w2, hy_f_b2, hy_f_freq2, hy_f_w3, hy_decay, hy_d_bias,
    hy_w_out, hy_b_out, ffn_w_up, ffn_conv_w, ffn_conv_b, ffn_w_down, final_g, norm_g_2, w_in_2,
    b_in_2, ssm_log_dt_2, ssm_lam_re_2, ssm_lam_im_2, ssm_b_re_2, ssm_b_im_2, ssm_c_re_2,
    ssm_c_im_2, ssm_d_2, ssm_w_glu_2, ssm_b_glu_2, pool_w_2, pool_scale_2, w_branch_a_2,
    w_branch_b_2, w_out_2, final_norm_g_2,
):
    x = first_block(
        x, c, ctx, c_ctx, mod_w, mod_b, norm_mix_g, norm_ffn_g, mla_w_dq, mla_g_q, mla_w_uq,
        mla_w_dkv, mla_g_kv, mla_w_uk, mla_w_uv, mla_w_o, hy_w_in, hy_b_in, hy_conv_w,
        hy_conv_b, hy_f_w1, hy_f_b1, hy_f_freq1, hy_f_w2, hy_f_b2, hy_f_freq2, hy_f_w3,
        hy_decay, hy_d_bias, hy_w_out, hy_b_out, ffn_w_up, ffn_conv_w, ffn_conv_b, ffn_w_down,
        final_g,
    )
    return second_block(
        x, norm_g_2, w_in_2, b_in_2, ssm_log_dt_2, ssm_lam_re_2, ssm_lam_im_2, ssm_b_re_2,
        ssm_b_im_2, ssm_c_re_2, ssm_c_im_2, ssm_d_2, ssm_w_glu_2, ssm_b_glu_2, pool_w_2,
        pool_scale_2, w_branch_a_2, w_branch_b_2, w_out_2, final_norm_g_2,
    )


_drawn_inputs = setup_inputs


def setup_inputs(seed=0):
    import zlib

    import numpy as np

    out = dict(_drawn_inputs(seed))
    spreads = {}
    factors = {'mla_g_q': 8.0,
     'hy_b_out': 8.0,
     'ffn_conv_b': 2.734,
     'b_in_2': 7.982,
     'ssm_log_dt_2': 45.384,
     'ssm_lam_re_2': 64.0,
     'ssm_lam_im_2': 38.432,
     'ssm_b_re_2': 54.736,
     'ssm_b_im_2': 58.968,
     'ssm_c_re_2': 56.36,
     'ssm_c_im_2': 55.88,
     'ssm_b_glu_2': 54.767}
    for name, (base, spread) in spreads.items():
        noise = np.random.default_rng([zlib.crc32(name.encode()), seed]).standard_normal(out[name].shape)
        drawn = base * np.exp(spread * noise) if base else spread * noise
        out[name] = jnp.asarray(drawn.astype(out[name].dtype))
    for name, factor in factors.items():
        out[name] = (out[name] * factor).astype(out[name].dtype)
    return out
```

```python
import math
from contextlib import ExitStack, contextmanager

import numpy as np
import concourse.bass as bass
from concourse import mybir

F32 = mybir.dt.float32
F32R = mybir.dt.float32r
ALU = mybir.AluOpType
ACT = mybir.ActivationFunctionType
AX = mybir.AxisListType
ds = bass.ds

P = 128
D = 1024
L = 512
LC = 256
LK = L + LC
KD = D // P
HEADS = 16
NOPE, ROPE, VH = 64, 32, 64
QL, KVL = 512, 256
DFF = 2816
KF = DFF // P
NUP = 2 * KF
SW = 512
GROUPS, GC, ST = 32, 16, 64
NM = GROUPS * ST // P
EPS = 1e-6
GRID_W = 64
HY_BANDS = 16
HID_F = 64
ROUND = 1.5 * 2.0 ** 23
TWO_PI = 2.0 * math.pi
PI_A = 6.28125
PI_B = 1.93500518798828125e-3
PI_C = TWO_PI - PI_A - PI_B
LN2_A = 0.693359375
LN2_B = math.log(2.0) - LN2_A
SLOT = 11 * P

STAGES = [("dq", 4, 8), ("kv", 3, 8), ("uv", 2, 8), ("heads", 8, 10), ("wo", 8, 8), ("up0", 44, 8),
          ("down0", 16, 11), ("hyin", 24, 8), ("dft", 8, 8), ("hyout", 8, 8), ("up1", 44, 8),
          ("down1", 16, 11), ("in2a", 8, 8), ("in2b", 24, 8), ("poolw", 1, 4), ("glu", 4, 4),
          ("branch", 8, 8), ("out2", 8, 8)]
FIRST_TILE, CHUNKS = {}, {}
_t = 0
for _name, _count, _chunks in STAGES:
    FIRST_TILE[_name], CHUNKS[_name] = _t, _chunks
    _t += _count

PARAMS = [("modb", 96), ("gmix", 16), ("gffn", 16), ("gq", 4), ("gkv", 2), ("hbin", 24), ("hcw", 72),
          ("hcb", 24), ("hdb", 8), ("hbo", 8), ("fcw", 2 * 3 * NUP), ("fcb", 2 * NUP), ("gfin", 8),
          ("g2", 8), ("bin2", 32), ("sd", 4), ("bglu", 4), ("pscale", 4), ("gfin2", 8),
          ("logdt", NM), ("lre", NM), ("lim", NM), ("tcol", 4), ("invc", 64)]
COL = {}
_c = 0
for _name, _n in PARAMS:
    COL[_name] = _c
    _c += _n
NPAR = _c


class Tally:

    def __init__(self, sem):
        self.sem, self.n, self.step = sem, 0, 0

    def up(self):
        self.n += 1
        return self.n + self.step


@contextmanager
def repeat(eng, count, *per):
    marks = [(t, k, t.n) for t, k in per]
    with eng.Fori(0, count) as i:
        for t, k, _ in marks:
            t.step = i * k
        yield i
    for t, k, n in marks:
        assert t.n - n == k, (t.n - n, k)
        t.step = 0
        t.n = n + k * count


def build(nc, a):
    with ExitStack() as ctx:
        base = nc.sbuf_base
        base = (base + 63) // 64 * 64
        where = [base]

        def place(name, shape, dt, at=None):
            size = 4 * int(np.prod(shape[1:]))
            off = where[0] if at is None else at
            if at is None:
                where[0] = (off + size + 31) // 32 * 32
            assert off + size <= nc.sbuf_usable_end, (name, off + size - nc.sbuf_usable_end)
            return nc.alloc_sbuf_tensor_at(name, shape, dt, offset=off)

        def sem(name):
            return ctx.enter_context(nc.semaphore(name))

        X = place("X", [P, KD, L], F32)
        HH = place("HH", [P, KD, L], F32R)
        HL = place("HL", [P, KD, L], F32R)
        RAW = [place(f"RAW{i}", [P, SLOT], F32) for i in range(2)]
        WH = [place(f"WH{i}", [P, SLOT], F32R) for i in range(2)]
        WL = [place(f"WL{i}", [P, SLOT], F32R) for i in range(2)]
        PAR = place("PAR", [P, NPAR], F32)
        MOD = place("MOD", [P, 96], F32)
        MODC = place("MODC", [P, 16], F32)
        SC = place("SC", [P, 128], F32)
        NMX = SC[:, 64:72]
        MACC = SC[:, 72:88]
        AB = place("AB", [P, 4, KD], F32)
        ONES = place("ONES", [P, P], F32)
        IDENT = place("IDENT", [P, P], F32)
        H2T = place("H2T", [P, L], F32)
        big = where[0]

        class Region:

            def __init__(self, at=None):
                self.at = big if at is None else at

            def put(self, name, shape, dt=F32):
                t = place(name, shape, dt, at=self.at)
                self.at = (self.at + 4 * int(np.prod(shape[1:])) + 31) // 32 * 32
                return t

        r = Region()
        V = r.put("V", [P, 6, HEADS * VH])
        p_at = r.at
        PR = [r.put(f"PR{i}", [P, 4, LK]) for i in range(2)]
        pt_at = r.at
        PT = r.put("PT", [P, 6, L])
        KP = [r.put(f"KP{i}", [P, LK]) for i in range(2)]
        Q = [r.put(f"Q{i}", [P, L]) for i in range(2)]
        QTAB = r.put("QTAB", [P, L])
        CKH = r.put("CKH", [P, 2, LK], F32R)
        CKL = r.put("CKL", [P, 2, LK], F32R)
        CQH = r.put("CQH", [P, 4, L], F32R)
        CQL = r.put("CQL", [P, 4, L], F32R)
        MR = [r.put(f"MR{i}", [P, D]) for i in range(2)]
        CB = r.put("CB", [P, D])
        VC = r.put("VC", [P, 6, P])
        O32 = r.put("O32", [P, L])
        RC = r.put("RC", [P, L])
        r = Region(p_at)
        CTX = r.put("CTX", [P, KD, LC])
        hc_at = r.at
        HCH = r.put("HCH", [P, KD, LC], F32R)
        HCL = r.put("HCL", [P, KD, LC], F32R)
        KCOS = r.put("KCOS", [P // 2, L])
        KSIN = r.put("KSIN", [P, L])
        cc_at = r.at
        CCB = r.put("CCB", [P, D])
        CK32 = Region(cc_at).put("CK32", [P, 2, LK])
        XSQ = Region(hc_at).put("XSQ", [P, KD, L])
        r = Region()
        TA = [r.put(f"TA{i}", [P, L]) for i in range(2)]
        TB = [r.put(f"TB{i}", [P, L]) for i in range(2)]
        C32 = r.put("C32", [P, 4, L])
        SSQA = r.put("SSQA", [P, LK])
        RTA = r.put("RTA", [P, LK])
        K1 = r.put("K1", [P, L])
        r = Region(pt_at + 4 * 6 * L)
        ZT = r.put("ZT", [2 * HY_BANDS + 1, L])
        FW1 = r.put("FW1", [2 * HY_BANDS + 1, HID_F])
        FW2 = r.put("FW2", [HID_F, HID_F])
        FPAR = r.put("FPAR", [HID_F, 4])
        FA = r.put("FA", [HID_F, L])
        FK = r.put("FK", [HID_F, L])

        r = Region()
        HIDH = r.put("HIDH", [P, KF, L], F32R)
        HIDL = r.put("HIDL", [P, KF, L], F32R)
        ZA = r.put("ZA", [P, L])
        ZG = r.put("ZG", [P, L])
        HID = r.put("HID", [P, L])
        t_at = r.at
        SSQ = r.put("SSQ", [P, L])
        RT = r.put("RT", [P, L])
        TN = [r.put(f"TN{i}", [P, L]) for i in range(2)]
        TM = [r.put(f"TM{i}", [P, L]) for i in range(2)]
        SQ = [r.put(f"SQ{i}", [P, L]) for i in range(2)]
        top = r.at

        r = Region()
        VP = r.put("VP", [P, KD, L])
        X1 = r.put("X1", [P, KD, L])
        pq_at = r.at
        UTH = r.put("UTH", [P, 4, 512], F32R)
        UTL = r.put("UTL", [P, 4, 512], F32R)
        PH = r.put("PH", [P, 4, 512], F32R)
        PL = r.put("PL", [P, 4, 512], F32R)
        QH = r.put("QH", [P, 4, 512], F32R)
        QLO = r.put("QLO", [P, 4, 512], F32R)
        z_at = r.at
        Z = r.put("Z", [P, 8, 512])
        DT = [r.put(f"DT{i}", [P, 512]) for i in range(4)]
        WN, TF, TG, TP = DT
        r = Region(pq_at)
        PB = [r.put(f"PB{i}", [P, L]) for i in range(2)]
        ZX = r.put("ZX", [P, L])
        ZV = r.put("ZV", [P, L])
        hl_at = base + 4 * KD * L * 2
        hh_at = base + 4 * KD * L
        r = Region(hl_at)
        G = r.put("G", [P, 8, L])
        r = Region(top)
        FW3 = r.put("FW3", [P, D])
        ADEC = r.put("ADEC", [P, D])
        H2C = r.put("H2C", [P, P])

        r = Region()
        UA = r.put("UA", [P, 4, L])
        z2_at = r.at
        ZAB = r.put("ZAB", [P, 8, L])
        SA = [r.put(f"SA{i}", [P, L]) for i in range(9)]
        GAB = r.put("GAB", [P, 16, L])
        PAD = 16
        ub_at = r.at
        UB = r.put("UB", [P, 4, PAD + L])
        BT = r.put("BT", [P, 2, 4, P])
        CBD = r.put("CBD", [P, NM, 2, 2 * GC])
        CH = r.put("CH", [P, L])
        BTC = r.put("BTC", [P, 2, P])
        assert r.at <= t_at
        r = Region(top)
        PLL = r.put("PLL", [P, 4, L], F32R)
        SL = r.put("SL", [P, 4, NM + 1])
        CC = r.put("CC", [P, 4, 2, 2 * GC])
        HBG = SC[:, 120:124]
        UAC = H2T
        PLH = Region(ub_at).put("PLH", [P, 4, L], F32R)
        COS = SA[0:2]
        SIN, PHA, PHB, T1, T2, T3, SRE = SA[2:9]
        SIM, TVEC = SSQ, RT
        PRD = [TN[0], TN[1], TM[0], TM[1]]
        AH = SQ[0]
        SH = SQ[1]
        TY, TS = SA[5:7], SA[7:9]
        r = Region(z2_at)
        SBC = r.put("SBC", [P, 4, NM, GC])
        S5 = r.put("S5", [P, 20, NM])
        BBD = r.put("BBD", [P, 2, NM, 2 * GC])
        PBUF = [r.put(f"PBUF{i}", [P, PAD + L]) for i in range(2)]
        r = Region()
        MH = r.put("MH", [P, KD, L], F32R)
        ML = r.put("ML", [P, KD, L], F32R)

        PS = ctx.enter_context(nc.psum_tensor("PS", [P, 8, 512], F32))

        def bank(n, w=512):
            return PS[:, n, 0:w]

        def par(name, k=0, n=1):
            return PAR[:, COL[name] + k:COL[name] + k + n]

        def par_at(name, k):
            return PAR[:, ds(k + COL[name], 1)]

        tile_loaded = [sem(f"tile_loaded{i}") for i in range(2)]
        tile_hi = sem("tile_hi")
        tile_split = sem("tile_split")
        tile_done = sem("tile_done")

        names = """par_in x_in ctx_in c_in cc_in mod_in0 mod_in1 tab_in filt_in consts silu_c mod_used modx
            ab ssq stat sqrt rt nt na nh nl xsq fmm fa fsin cq_ev cq_sq cq_add radd kv_x ckv_ev ckv_sq krot v_ev
            proj qready kready vc oev s_ready smax sexp s_tr pt_act pt_dve pv ohi pair_done
            resid rsq hin g_in hev hz vp tapmm tap_read window pq pqh pql tv uth utl dft_h hcopy zd inv iev yhi ylo h2c za zg zc silu hid hidh hidl s5_in tvec_in s5a s5d bbd bt_mm bt_ev cbd p2ev pool plh pll uac ccp bmm burd ph tr sn prd cmm yev gel yh yl pmm ybf ybh ybl sg yaf yah yal amm mev mrg mh ml fin oready dchain achain pchain out_done""".split()
        S = {n: sem("s_" + n) for n in names}

        FROM_ONE = "pt_act pt_dve s_tr pv hid bmm cmm yev prd ml".split()

        NORMS = ["x0", "ctx", "cq", "ckx", "ckc", "ffn0", "hy", "ffn1", "fin", "n2", "fin2"]
        NTILES = dict(x0=8, ctx=8, cq=4, ckx=2, ckc=2, ffn0=8, hy=8, ffn1=8, fin=0, n2=8, fin2=0)
        NINDEX = {n: k for k, n in enumerate(NORMS)}
        NBASE, _n = {}, 0
        for n in NORMS:
            NBASE[n] = _n
            _n += NTILES[n]
        GAIN = dict(x0=lambda k: (AB[:, 0, k:k + 1], AB[:, 1, k:k + 1]),
                    ctx=lambda k: (AB[:, 2, k:k + 1], AB[:, 3, k:k + 1]),
                    cq=lambda k: (par("gq", k), None), ckx=lambda k: (par("gkv", k), None),
                    ckc=lambda k: (par("gkv", k), None))
        for n in ("ffn0", "hy", "ffn1"):
            GAIN[n] = GAIN["x0"]
        GAIN["n2"] = lambda k: (par("g2", k), None)

        OUTS = dict(dq=4, kv=6, uv=12, wo=8, up0=44, down0=8, hyin=24, hyout=8, up1=44, down1=8,
                    in2a=8, in2b=24, poolw=4, glu=4, out2=8)
        OBASE, _n = {}, 0
        for n, k in OUTS.items():
            OBASE[n] = _n
            _n += k

        RBASE = dict(wo=0, down0=8, hyout=16, down1=24, fin=32, out2=40)

        def mod(layer, part, k=0, n=KD):
            at = 48 * layer + KD * part + k
            return MOD[:, at:at + n]

        def wide(b, w):
            return PS[:, b:b + 2, :].rearrange("p a n -> p (a n)")[:, 0:w]

        HALVES = (0, 1)

        def sp_hyena(sp, ring):
            sp.dma_start(FW3[:, :], a["fw3"]).then_inc(S["hin"], 16)
            sp.dma_start(ADEC[:, :], a["decay"].partition_broadcast(P)).then_inc(S["hin"], 16)
            with sp.Fori(0, 4) as i:
                for j in range(6):
                    ring("hyin", a["whin"], j, i, 6)
            for j in range(2):
                ring_at(sp, "dft", a["dft"][j:j + 1], j)
            sp.wait_ge(tile_done, FIRST_TILE["hyin"] + 24)
            sp.dma_start(G[:, :, :], a["idft"]).then_inc(S["g_in"], 16)
            for j in range(2, 8):
                ring_at(sp, "dft", a["dft"][j % 4:j % 4 + 1], j)
            with sp.Fori(0, 4) as i:
                for j in range(2):
                    ring("hyout", a["whout"], j, i, 2)

        def ring_at(sp, stage, src, j):
            t = FIRST_TILE[stage] + j
            sp.wait_ge(tile_split, t - 1)
            sp.dma_start(RAW[t % 2][:, 0:CHUNKS[stage] * P], src.rearrange("a p n -> p (a n)")
                         ).then_inc(tile_loaded[t % 2], 16)

        def pool_hyena(pool, split):
            with pool.Fori(0, 4) as i:
                for j in range(6):
                    split("hyin", j, i, 6)
            for st in ("dft", "hyout"):
                with pool.Fori(0, 4) as i:
                    for j in range(2):
                        split(st, j, i, 2)

        def pe_hyena(pe, linear, stat, mm3, chunk):
            def taps(c, n):
                pe.wait_ge(S["h2c"], n + 1)
                if not (isinstance(n, int) and n == 0):
                    pe.wait_ge(S["tap_read"], n)
                for half in range(2):
                    r = slice(HID_F * half, HID_F * half + HID_F)
                    m = pe.matmul(bank(4 + half), H2C[r, :], FW3[r, 512 * c:512 * c + 512],
                                  start=True, stop=True)
                m.then_inc(S["tapmm"], 1)

            def turn_values(c, tt):
                n = 4 * c + tt
                if n >= 2:
                    pe.wait_ge(S["utl"], n - 1)
                for ct in range(4):
                    m = pe.transpose(PS[:, 6 + tt % 2, ct * P:(ct + 1) * P],
                                     VP[:, 4 * c + ct, tt * P:(tt + 1) * P], IDENT[:, :])
                m.then_inc(S["tv"], 1)

            def spectra(c, f):
                n = 4 * c + f
                t = FIRST_TILE["dft"] + n
                b = 4 * (f % 2)
                pe.wait_ge(tile_split, t + 1)
                if n >= 2:
                    pe.wait_ge(S["zd"], n - 1)
                for part, (xh, xl) in ((2, (PH, PL)), (3, (QH, QLO)), (0, (UTH, UTL)), (1, (UTH, UTL))):
                    for k in range(4):
                        m = mm3(bank(b + part), *chunk(t % 2, 4 * (part % 2) + k), xh[:, k, :], xl[:, k, :],
                                k == 0, k == 3)
                    if part == 3:
                        m.then_inc(S["dft_h"], 1)
                m.then_inc(tile_done, 1)

            def back(c, ct):
                n = 4 * c + ct
                if n >= 2:
                    pe.wait_ge(S["iev"], n - 1)
                for k in range(8):
                    m = pe.matmul(bank(ct % 2), Z[:, k, ct * P:(ct + 1) * P], G[:, k, :],
                                  start=k == 0, stop=k == 7)
                m.then_inc(S["inv"], 1)

            stat("hy", SSQ)
            for j in range(6):
                linear("hyin", j, HH, HL, (S["hev"], 0), nbase=NBASE["hy"] if j == 0 else None)
                if j == 2:
                    pe.wait_ge(S["hin"], 32)
                    taps(0, 0)
            with pe.Fori(0, 3) as i:
                for j in range(6):
                    linear("hyin", 6 + j, HH, HL, (S["hev"], 0), i, 6)
                    if j == 2:
                        taps(0, i + 1)
            pe.wait_ge(S["vp"], 8)
            for tt in range(4):
                turn_values(0, tt)
            pe.wait_ge(S["utl"], 4)
            pe.wait_ge(S["pql"], 4)
            for f in range(4):
                spectra(0, f)
            pe.wait_ge(S["zd"], 4)
            pe.wait_ge(S["g_in"], 16)
            for k in range(4):
                taps(1, 4 + k)
                turn_values(1, k)
                back(0, k)
            pe.wait_ge(S["utl"], 8)
            pe.wait_ge(S["pql"], 8)
            pe.wait_ge(S["iev"], 4)
            for f in range(4):
                spectra(1, f)
            pe.wait_ge(S["zd"], 8)
            for k in range(4):
                back(1, k)
            pe.wait_ge(S["iev"], 8)
            pe.wait_ge(S["ylo"], 8)
            for j in range(2):
                linear("hyout", j, HH, HL, (S["resid"], 16))
            with pe.Fori(0, 3) as i:
                for j in range(2):
                    linear("hyout", 2 + j, HH, HL, (S["resid"], 16), i, 2)

        def act_hyena(act, norm, squares):
            def window(n, c, tt, i=0):
                act.wait_ge(S["tap_read"], n)
                act.activation(WN[:, :], ADEC[:, 512 * c:512 * c + 512], ACT.Exp,
                               scale=par_at("tcol", tt)).then_inc(S["window"], 1)
                act.wait_ge(S["pq"], n + 1)
                act.copy(PH[:, ds(tt, 1), :].rearrange("p a n -> p (a n)"), TP[:, :]).then_inc(S["pqh"], 1)
                act.copy(QH[:, ds(tt, 1), :].rearrange("p a n -> p (a n)"), TF[:, :]).then_inc(S["pqh"], 1)

            def taken(j, i=0):
                jj, kind = j // 3, j % 3
                act.wait_ge(tile_done, i * 6 + (FIRST_TILE["hyin"] + j + 1))
                if j >= 2:
                    act.wait_ge(S["hz"], i * 6 + (j - 1))
                act.activation(PB[j % 2][:, :], bank((OBASE["hyin"] + j) % 2), ACT.Identity,
                               bias=par_at("hbin", i * 2 + ((8, 16, 0)[kind] + jj)), scale=1.0
                               ).then_inc(S["hev"], 1)

            def values_hi(c, tt):
                act.wait_ge(S["tv"], 4 * c + tt + 1)
                act.copy(UTH[:, tt, :], bank(6 + tt % 2)).then_inc(S["uth"], 1)

            act.wait_ge(S["hin"], 32)
            act.activation(ADEC[:, :], ADEC[:, :], ACT.Abs).then_inc(S["achain"], 1)
            act.wait_ge(S["ab"], 3)
            norm("hy", HH, L, D, RT, TN, TM)
            act.wait_ge(S["nl"], NBASE["hy"] + 8)
            act.wait_ge(S["achain"], 2)
            for j in range(6):
                taken(j)
                if j == 2:
                    window(0, 0, 0)
            with act.Fori(0, 3) as i:
                for j in range(6):
                    taken(6 + j, i)
                    if j == 2:
                        window(i + 1, 0, i + 1)
            act.wait_ge(S["hz"], 24)
            act.wait_ge(S["vp"], 8)
            for tt in range(4):
                values_hi(0, tt)

            def spectrum_copies(c):
                for f in range(4):
                    n = 4 * c + f
                    act.wait_ge(S["dft_h"], n + 1)
                    act.wait_ge(*((S["zd"], n) if n != 0 else (S["pql"], 4)))
                    if n == 4:
                        act.wait_ge(S["pql"], 8)
                    for part in range(2):
                        act.copy(DT[part][:, :], bank(4 * (f % 2) + 2 + part)).then_inc(S["hcopy"], 1)

            def y_hi(n):
                act.wait_ge(S["iev"], n + 1)
                act.copy(HH[:, n, :], X1[:, n, :]).then_inc(S["yhi"], 1)

            spectrum_copies(0)
            act.wait_ge(S["zd"], 4)
            for k in range(4):
                window(4 + k, 1, k)
                values_hi(1, k)
                y_hi(k)
            spectrum_copies(1)
            for k in range(4, 8):
                y_hi(k)
            for j in range(2):
                squares("hyout", j)
            with act.Fori(0, 3) as i:
                for j in range(2):
                    squares("hyout", 2 + j, i, 2)

        def dve_hyena(dve, norm, link, own, columns, sums_ready, add_squares):
            def filter_time(n, tt):
                if not (isinstance(n, int) and n == 0):
                    dve.wait_ge(S["tapmm"], n)
                dve.tensor_copy(H2C[:, :], H2T[:, ds(tt * P, P)]).then_inc(S["h2c"], 1)

            def taps(n, tt, first):
                dve.wait_ge(S["window"], n + 1)
                dve.wait_ge(S["tapmm"], n + 1)
                link(dve.tensor_tensor(TF[:, :], bank(4), WN[:, :], ALU.mult))
                dve.tensor_tensor(TG[:, :], bank(5), WN[:, :], ALU.mult).then_inc(S["tap_read"], 1)
                dve.wait_ge(S["tap_read"], n + 1)
                if first:
                    link(dve.memset(TG[0:1, :], 0.0))
                link(dve.tensor_tensor(TP[:, :], TF[:, :], TG[:, :], ALU.add))
                dve.tensor_tensor(TF[:, :], TF[:, :], TG[:, :], ALU.subtract).then_inc(S["pq"], 1)
                at = (slice(None), ds(tt, 1), slice(None))
                for k, (src, h, lo) in enumerate(((TP, PH, PL), (TF, QH, QLO))):
                    dve.wait_ge(S["pqh"], n * 2 + (k + 1))
                    dve.tensor_tensor(lo[at].rearrange("p a n -> p (a n)"), src[:, :],
                                      h[at].rearrange("p a n -> p (a n)").bitcast(F32), ALU.subtract
                                      ).then_inc(*((S["pql"], 1) if k else (S["dchain"], 1)))
                    if k == 0:
                        own.up()

            def short_conv(j, i=0):
                jj, kind = j // 3, j % 3
                col = i * 2 + ((8, 16, 0)[kind] + jj)
                x1 = X1[:, ds(i * 2 + jj, 1), :].rearrange("p a n -> p (a n)")
                z = (ZX[:, :], ZV[:, :], x1)[kind]
                pb = PB[j % 2]
                dve.wait_ge(S["hev"], i * 6 + (j + 1))
                link(dve.tensor_scalar(z, pb[:, :], par_at("hcw", col + 24), par_at("hcb", col), ALU.mult, ALU.add))
                link(dve.scalar_tensor_tensor(z[:, 1:L], pb[:, 0:L - 1], par_at("hcw", col), z[:, 1:L],
                                              ALU.mult, ALU.add))
                dve.scalar_tensor_tensor(z[:, 0:L - 1], pb[:, 1:L], par_at("hcw", col + 48), z[:, 0:L - 1],
                                         ALU.mult, ALU.add).then_inc(S["hz"], 1)
                if kind == 1:
                    dve.wait_ge(S["hz"], i * 6 + (j + 1))
                    dve.tensor_tensor(VP[:, ds(i * 2 + jj, 1), :].rearrange("p a n -> p (a n)"), ZV[:, :],
                                      ZX[:, :], ALU.mult).then_inc(S["vp"], 1)

            def values_lo(c, tt):
                dve.wait_ge(S["uth"], 4 * c + tt + 1)
                dve.tensor_tensor(UTL[:, tt, :], bank(6 + tt % 2), UTH[:, tt, :].bitcast(F32), ALU.subtract
                                  ).then_inc(S["utl"], 1)

            def product(c, f):
                n = 4 * c + f
                b = 4 * (f % 2)
                dve.wait_ge(S["hcopy"], 2 * n + 2)
                dve.wait_ge(tile_done, FIRST_TILE["dft"] + n + 1)
                link(dve.tensor_tensor(DT[2][:, :], bank(b), DT[0][:, :], ALU.mult))
                link(dve.tensor_tensor(DT[3][:, :], bank(b + 1), DT[1][:, :], ALU.mult))
                link(dve.tensor_tensor(Z[:, f, :], DT[2][:, :], DT[3][:, :], ALU.subtract))
                link(dve.tensor_tensor(DT[2][:, :], bank(b), DT[1][:, :], ALU.mult))
                link(dve.tensor_tensor(DT[3][:, :], bank(b + 1), DT[0][:, :], ALU.mult))
                dve.tensor_tensor(Z[:, 4 + f, :], DT[2][:, :], DT[3][:, :], ALU.add).then_inc(S["zd"], 1)

            def gated(n):
                dve.wait_ge(S["inv"], n + 1)
                link(dve.scalar_tensor_tensor(VP[:, n, :], VP[:, n, :], par("hdb", n), bank(n % 2),
                                              ALU.mult, ALU.add))
                dve.tensor_tensor(X1[:, n, :], VP[:, n, :], X1[:, n, :], ALU.mult).then_inc(S["iev"], 1)

            def out(j, i=0, per=0):
                xt = X[:, ds(i * per + j, 1), :].rearrange("p a n -> p (a n)")
                dve.wait_ge(tile_done, i * per + (FIRST_TILE["hyout"] + j + 1))
                link(dve.tensor_scalar(TN[j % 2][:, :], bank((OBASE["hyout"] + j) % 2),
                                       par_at("hbo", i * per + j), MOD[:, ds(i * per + (48 + 16 + j), 1)],
                                       ALU.add, ALU.mult))
                dve.tensor_tensor(xt, xt, TN[j % 2][:, :], ALU.add).then_inc(S["resid"], 1)
                add_squares(16 + j, j, i, per)

            dve.wait_ge(S["fsin"], 3)
            filter_time(0, 0)
            norm("hy", X, HH, HL, L, RT, TN, TM)
            for j in range(6):
                short_conv(j)
                if j == 2:
                    taps(0, 0, True)
            with repeat(dve, 3, (own, 15)) as i:
                filter_time(i + 1, i + 1)
                for j in range(6):
                    short_conv(6 + j, i)
                    if j == 2:
                        taps(i + 1, i + 1, False)
            filter_time(4, 0)
            for tt in range(4):
                values_lo(0, tt)
            for f in range(4):
                product(0, f)
            for k in range(4):
                taps(4 + k, k, k == 0)
                if k < 3:
                    filter_time(5 + k, k + 1)
                values_lo(1, k)
                gated(k)
            for f in range(4):
                product(1, f)
            for k in range(4, 8):
                gated(k)
            dve.wait_ge(S["inv"], 8)
            for n in range(8):
                dve.wait_ge(S["yhi"], n + 1)
                dve.tensor_tensor(HL[:, n, :], X1[:, n, :], HH[:, n, :].bitcast(F32), ALU.subtract
                                  ).then_inc(S["ylo"], 1)
            link(dve.memset(SSQ[:, :], 0.0))
            for j in range(2):
                out(j)
            with repeat(dve, 3, (own, 2)) as i:
                for j in range(2):
                    out(2 + j, i, 2)
            dve.wait_ge(S["radd"], 24)
            columns(1, False)
            sums_ready()


        def sp_second(sp, ring):
            ring("in2a", a["win2a"], 0)
            ring("in2a", a["win2a"], 1)
            sp.wait_ge(tile_done, FIRST_TILE["in2a"])
            sp.dma_start(SBC[:, :, :, :], a["s5bc"]).then_inc(S["s5_in"], 16)
            sp.wait_ge(S["nl"], NBASE["n2"] + 8)
            sp.dma_start(TVEC[:, :], a["tvec"]).then_inc(S["tvec_in"], 16)
            for j in range(2, 8):
                ring("in2a", a["win2a"], j)
            with sp.Fori(0, 4) as i:
                for j in range(6):
                    ring("in2b", a["win2b"], j, i, 6)
            ring("poolw", a["wpool"], 0)
            for j in range(4):
                ring("glu", a["wglu"], j)
            for st, w in (("branch", "wbr"), ("out2", "wout2")):
                with sp.Fori(0, 4) as i:
                    for j in range(2):
                        ring(st, a[w], j, i, 2)

        def pool_second(pool, split):
            for j in range(8):
                split("in2a", j)
            with pool.Fori(0, 4) as i:
                for j in range(6):
                    split("in2b", j, i, 6)
            split("poolw", 0)
            for j in range(4):
                split("glu", j)
            for st in ("branch", "out2"):
                with pool.Fori(0, 4) as i:
                    for j in range(2):
                        split(st, j, i, 2)

        def pe_second(pe, linear, stat, mm3, chunk):
            stat("fin", SSQ)
            stat("n2", SSQ)
            for j in range(8):
                linear("in2a", j, HH, HL, (S["p2ev"], 0), nbase=NBASE["n2"] if j == 0 else None)
                if j == 3:
                    pe.wait_ge(S["bbd"], 1)
                    for part in range(2):
                        for q in range(4):
                            m = pe.transpose(PS[:, 2 + part, q * P:(q + 1) * P],
                                             BBD[:, part, 4 * q:4 * q + 4, :].rearrange("p m c -> p (m c)"),
                                             IDENT[:, :])
                    m.then_inc(S["bt_mm"], 1)
            pe.wait_ge(S["bt_ev"], 2)
            with pe.Fori(0, 4) as i:
                def drive(mm):
                    pe.wait_ge(S["burd"], i * 4 + (mm + 1))
                    r = slice(32 * mm, 32 * mm + 32)
                    for part in range(2):
                        m = pe.matmul(bank(2 + 2 * (mm % 2) + part), BTC[r, part, :], UAC[r, :],
                                      start=True, stop=True)
                    m.then_inc(S["bmm"], 1)

                def read_out(mm):
                    for k, part in enumerate((0, 0, 1, 1)):
                        pe.wait_ge(S["prd"], i * 16 + (4 * mm + k + 1) + 1)
                        m = pe.matmul(PS[32 * mm:32 * mm + 32, 6, :], CC[:, mm, part, :], PRD[k][:, :],
                                      start=k == 0, stop=k == 3)
                    m.then_inc(S["cmm"], 1)

                def gate(j):
                    linear("in2b", j, HH, HL, (S["p2ev"], 8), i, 6)

                pe.wait_ge(S["uac"], i * 2 + 2)
                drive(0)
                drive(1)
                gate(0)
                gate(1)
                pe.wait_ge(S["ccp"], i + 1)
                pe.wait_ge(S["yev"], i + 1)
                read_out(0)
                drive(2)
                gate(2)
                read_out(1)
                drive(3)
                gate(3)
                gate(4)
                read_out(2)
                gate(5)
                read_out(3)
            t = FIRST_TILE["poolw"]
            pe.wait_ge(tile_split, t + 1)
            pe.wait_ge(S["pll"], 4)
            for g in range(4):
                pe.wait_ge(*((S["p2ev"], 31 + g) if g < 2 else (S["ybf"], g - 1)))
                m = mm3(bank((OBASE["poolw"] + g) % 2), *chunk(t % 2, g), PLH[:, g, :], PLL[:, g, :], True, True)
                m.then_inc(*((S["pmm"], 1) if g < 3 else (tile_done, 1)))
            pe.wait_ge(S["yl"], 4)
            for j in range(4):
                if j < 2:
                    pe.wait_ge(S["ybf"], 3 + j)
                linear("glu", j, HH[:, 4:8, :], HL[:, 4:8, :], (S["sg"], 0), kn=4)

            def branches(j, i=0, per=0):
                t = FIRST_TILE["branch"] + j
                pe.wait_ge(tile_split, i * per + (t + 1))
                if per:
                    pe.wait_ge(S["mev"], i * per + (j - 1))
                for c, (h, lo) in enumerate(((HH, HL), (PLH, PLL))):
                    for k in range(4):
                        m = mm3(bank(2 * (j % 2) + c), *chunk(t % 2, 4 * c + k), h[:, k, :], lo[:, k, :],
                                k == 0, k == 3)
                    m.then_inc(*((tile_done, 1) if c else (S["amm"], 1)))

            pe.wait_ge(S["ybl"], 4)
            pe.wait_ge(S["yal"], 4)
            for j in range(2):
                branches(j)
            with pe.Fori(0, 3) as i:
                for j in range(2):
                    branches(2 + j, i, 2)
            pe.wait_ge(S["ml"], 8 + 1)
            for j in range(2):
                linear("out2", j, MH, ML, (S["resid"], RBASE["out2"]))
            with pe.Fori(0, 3) as i:
                for j in range(2):
                    linear("out2", 2 + j, MH, ML, (S["resid"], RBASE["out2"]), i, 2)
            stat("fin2", SSQ)

        def s5(k):
            return S5[:, k, :] if k >= 0 else SL[:, k + 4, 0:NM]

        (MAG5, FT5, FH5, FL5, Z5, AN5, K5, R5, SN5, HS5, E5, NR5, NI5, DEN5, CR5, CI5, TMP5, DT5
         ) = range(-4, 14)
        HB = SC[:, 104:120]

        def act_second(act, norm, squares):
            act.wait_ge(S["stat"], NINDEX["fin"] + 1)
            act.activation(RT[:, :], bank(7), ACT.Sqrt, bias=SC[:, 0:1], scale=1.0 / D).then_inc(S["sqrt"], 1)
            with act.Fori(0, 4) as i:
                for j in range(2):
                    squares("fin", j, i, 2)
            norm("n2", HH, L, D, RT, TN, TM)
            act.wait_ge(S["s5d"], 1)
            act.activation(s5(SN5), s5(AN5), ACT.Sin).then_inc(S["s5a"], 1)
            act.activation(s5(HS5), s5(AN5), ACT.Sin, scale=0.5).then_inc(S["s5a"], 1)

            def pooled_hi(g):
                act.wait_ge(S["pool"], g + 1)
                act.copy(PLH[:, g, :], SA[g % 2][:, :]).then_inc(S["plh"], 1)

            for j in range(8):
                act.wait_ge(tile_done, FIRST_TILE["in2a"] + j + 1)
                dst = UA[:, j, :] if j < 4 else UB[:, j - 4, PAD:PAD + L]
                act.activation(dst, bank((OBASE["in2a"] + j) % 2), ACT.Identity,
                               bias=par("bin2", j if j < 4 else 4 + j), scale=1.0).then_inc(S["p2ev"], 1)
                if j == 3:
                    act.wait_ge(S["bt_mm"], 1)
                    for part in range(2):
                        act.copy(BT[:, part, :, :].rearrange("p q n -> p (q n)"), bank(2 + part)
                                 ).then_inc(S["bt_ev"], 1)
                if j >= 5:
                    pooled_hi(j - 5)
            pooled_hi(3)

            def waves(mm, i=0):
                def n(k):
                    return i * 16 + (4 * mm + k)
                act.wait_ge(S["ph"], i * 4 + (mm + 1))
                act.activation(AH[:, :], PHA[:, :], ACT.Abs).then_inc(S["tr"], 1)
                act.wait_ge(S["sn"], i * 4 + mm)
                act.activation(SH[:, :], PHA[:, :], ACT.Sin, scale=math.pi).then_inc(S["tr"], 1)
                act.wait_ge(S["tr"], n(1))
                act.activation(CH[:, :], AH[:, :], ACT.Sin, bias=SC[:, 6:7], scale=-math.pi).then_inc(S["tr"], 1)
                act.activation(COS[mm % 2][:, :], AH[:, :], ACT.Sin, bias=SC[:, 6:7], scale=-TWO_PI
                               ).then_inc(S["tr"], 1)

            act.wait_ge(S["bt_ev"], 2)
            act.wait_ge(S["pll"], 4)
            act.wait_ge(S["cbd"], 1)
            waves(0)
            with act.Fori(0, 4) as i:
                def gate(j):
                    act.wait_ge(tile_done, i * 6 + (FIRST_TILE["in2b"] + j + 1))
                    src = bank((OBASE["in2b"] + j) % 2)
                    if j < 2:
                        act.activation(ZAB[:, ds(i + 4 * j, 1), :].rearrange("p a n -> p (a n)"), src, ACT.Silu,
                                       bias=par_at("bin2", i + (4 + 8 * j)), scale=1.0).then_inc(S["p2ev"], 1)
                    else:
                        k = 8 * (j // 4) + j % 2
                        act.activation(GAB[:, ds(i * 2 + k, 1), :].rearrange("p a n -> p (a n)"), src, ACT.Tanh,
                                       bias=SC[:, ds(i * 2 + (104 + k), 1)], scale=0.5).then_inc(S["p2ev"], 1)

                act.wait_ge(S["bmm"], i * 4 + 1)
                act.copy(UAC[:, :], UA[:, ds(i, 1), :].rearrange("p a n -> p (a n)")).then_inc(S["uac"], 1)
                act.copy(BTC[:, :, :].rearrange("p a n -> p a n"), BT[:, :, ds(i, 1), :].rearrange(
                    "p a q n -> p a (q n)")).then_inc(S["uac"], 1)
                act.wait_ge(S["cmm"], i * 4 + 1)
                act.copy(CC[:, :, :, :].rearrange("p m a c -> p (m a c)"),
                         CBD[:, ds(i * 4, 4), :, :].rearrange("p m a c -> p (m a c)")).then_inc(S["ccp"], 1)
                waves(1, i)
                gate(0)
                gate(1)
                waves(2, i)
                gate(2)
                waves(3, i)
                gate(3)
                gate(4)
                waves(4, i)
                gate(5)
            act.wait_ge(S["yev"], 4 + 1)
            for k in range(4):
                act.activation(UA[:, k, :], UA[:, k, :], ACT.Gelu_apprx_tanh).then_inc(S["gel"], 1)
            for k in range(4):
                act.wait_ge(S["gel"], k + 1)
                act.copy(HH[:, 4 + k, :], UA[:, k, :]).then_inc(S["yh"], 1)
            for g in range(4):
                act.wait_ge(S["ybf"], g + 1)
                act.copy(PLH[:, g, :], TY[g % 2][:, :]).then_inc(S["ybh"], 1)
            for j in range(4):
                act.wait_ge(tile_done, FIRST_TILE["glu"] + j + 1)
                if j >= 2:
                    act.wait_ge(S["yal"], j - 1)
                act.activation(TS[j % 2][:, :], bank((OBASE["glu"] + j) % 2), ACT.Tanh, bias=HBG[:, j:j + 1],
                               scale=0.5).then_inc(S["sg"], 1)
                if j:
                    act.wait_ge(S["yaf"], j)
                    act.copy(HH[:, j - 1, :], TS[(j - 1) % 2][:, :]).then_inc(S["yah"], 1)
            act.wait_ge(S["yaf"], 4)
            act.copy(HH[:, 3, :], TS[1][:, :]).then_inc(S["yah"], 1)
            with act.Fori(0, 4) as i:
                for j in range(2):
                    act.wait_ge(S["mrg"], i * 2 + (j + 1))
                    act.copy(MH[:, ds(i * 2 + j, 1), :].rearrange("p a n -> p (a n)"), TY[j][:, :]
                             ).then_inc(S["mh"], 1)
            with act.Fori(0, 4) as i:
                for j in range(2):
                    squares("out2", j, i, 2)
            act.wait_ge(S["stat"], NINDEX["fin2"] + 1)
            act.activation(RT[:, :], bank(7), ACT.Sqrt, bias=SC[:, 0:1], scale=1.0 / D).then_inc(S["sqrt"], 1)

        def dve_second(dve, norm, link, own, reduce_angle, add_squares, sums_ready):
            def tt(out, x, y, op):
                link(dve.tensor_tensor(out, x, y, op))

            def tile_of(t, k):
                return t[:, ds(k, 1), :].rearrange("p a n -> p (a n)")

            dve.wait_ge(S["sqrt"], NINDEX["fin"] + 1)
            link(dve.reciprocal(RT[:, :], RT[:, :]))
            link(dve.memset(SSQ[:, :], 0.0))
            with dve.Fori(0, 4) as i:
                for j in range(2):
                    x = tile_of(X, i * 2 + j)
                    dve.scalar_tensor_tensor(x, x, par_at("gfin", i * 2 + j), RT[:, :], ALU.mult, ALU.mult
                                             ).then_inc(S["resid"], 1)
                for j in range(2):
                    add_squares(32 + j, j, i, 2)
            dve.wait_ge(S["radd"], 40)
            sums_ready()
            norm("n2", X, HH, HL, L, RT, TN, TM)

            link(dve.memset(SL[:, :, NM:NM + 1], 0.0))
            link(dve.memset(SC[:, 6:7], math.pi / 2))
            link(dve.tensor_scalar(HB, par("bin2", 16, 16), 0.5, None, ALU.mult))
            link(dve.tensor_scalar(HBG, par("bglu", 0, 4), 0.5, None, ALU.mult))

            def exp(x, out, less_one=None):
                k, r, q, two_k = s5(K5), s5(R5), s5(TMP5), s5(CR5)
                link(dve.tensor_scalar(r, x, 88.72, -88.03, ALU.min, ALU.max))
                link(dve.tensor_scalar(k, r, 1.0 / math.log(2.0), ROUND, ALU.mult, ALU.add))
                link(dve.tensor_scalar(k, k, ROUND, None, ALU.subtract))
                for part in (LN2_A, LN2_B):
                    link(dve.scalar_tensor_tensor(r, k, -part, r, ALU.mult, ALU.add))
                link(dve.tensor_scalar(q, r, 1.0 / math.factorial(8), None, ALU.mult))
                for n in range(7, 0, -1):
                    link(dve.scalar_tensor_tensor(q, q, 1.0 / math.factorial(n), r, ALU.add, ALU.mult))
                link(dve.tensor_scalar(two_k.bitcast(mybir.dt.int32), k, 127.0, 2.0 ** 23, ALU.add, ALU.mult))
                tt(q, q, two_k, ALU.mult)
                tt(out, q, two_k, ALU.add)
                if less_one is not None:
                    link(dve.scalar_tensor_tensor(less_one, two_k, -1.0, q, ALU.add, ALU.add))

            exp(par("logdt", 0, NM), s5(DT5))
            tt(s5(Z5), par("lre", 0, NM), s5(DT5), ALU.mult)
            tt(s5(AN5), par("lim", 0, NM), s5(DT5), ALU.mult)
            reduce_angle(s5(AN5), s5(K5))
            dve.tensor_scalar(s5(AN5), s5(AN5), math.pi, -math.pi, ALU.min, ALU.max).then_inc(S["s5d"], 1)
            dve.wait_ge(S["s5d"], 1)
            grid = ROUND / 2.0 ** 14
            link(dve.tensor_scalar(s5(FT5), s5(AN5), 1.0 / TWO_PI, None, ALU.mult))
            link(dve.tensor_scalar(s5(FH5), s5(FT5), grid, grid, ALU.add, ALU.subtract))
            link(dve.scalar_tensor_tensor(s5(FL5), s5(FH5), -PI_A, s5(AN5), ALU.mult, ALU.add))
            link(dve.scalar_tensor_tensor(s5(FL5), s5(FH5), -PI_B, s5(FL5), ALU.mult, ALU.add))
            link(dve.scalar_tensor_tensor(s5(FL5), s5(FH5), -PI_C, s5(FL5), ALU.mult, ALU.add))
            link(dve.tensor_scalar(s5(FL5), s5(FL5), 1.0 / TWO_PI, None, ALU.mult))
            exp(s5(Z5), s5(MAG5), s5(E5))
            dve.wait_ge(S["s5a"], 2)
            tt(s5(HS5), s5(HS5), s5(HS5), ALU.mult)
            link(dve.tensor_scalar(s5(HS5), s5(HS5), 2.0, None, ALU.mult))
            link(dve.scalar_tensor_tensor(s5(NR5), s5(E5), 1.0, s5(HS5), ALU.add, ALU.mult))
            tt(s5(NR5), s5(E5), s5(NR5), ALU.subtract)
            tt(s5(NI5), s5(MAG5), s5(SN5), ALU.mult)
            tt(s5(DEN5), par("lre", 0, NM), par("lre", 0, NM), ALU.mult)
            tt(s5(TMP5), par("lim", 0, NM), par("lim", 0, NM), ALU.mult)
            tt(s5(DEN5), s5(DEN5), s5(TMP5), ALU.add)
            link(dve.reciprocal(s5(DEN5), s5(DEN5)))
            for out, p, q, op in ((CR5, NR5, NI5, ALU.add), (CI5, NI5, NR5, ALU.subtract)):
                tt(s5(out), s5(p), par("lre", 0, NM), ALU.mult)
                tt(s5(TMP5), s5(q), par("lim", 0, NM), ALU.mult)
                tt(s5(out), s5(out), s5(TMP5), op)
                tt(s5(out), s5(out), s5(DEN5), ALU.mult)
            link(dve.memset(BBD[:, :, :, :], 0.0))
            link(dve.memset(CBD[:, :, :, :], 0.0))
            dve.wait_ge(S["s5_in"], 16)
            pr = [T[:, 0:NM * GC].rearrange("p (m c) -> p m c", c=GC) for T in (T1, T2)]
            wide_c = [s5(k).unsqueeze(2).to_broadcast([P, NM, GC]) for k in (CR5, CI5)]
            for part, (b0, b1, op) in enumerate(((0, 1, ALU.subtract), (1, 0, ALU.add))):
                tt(pr[0], SBC[:, b0, :, :], wide_c[0], ALU.mult)
                tt(pr[1], SBC[:, b1, :, :], wide_c[1], ALU.mult)
                for g in range(2):
                    r = slice(ST * g, ST * g + ST)
                    ins = dve.tensor_tensor(BBD[r, part, :, GC * g:GC * g + GC], pr[0][r, :, :], pr[1][r, :, :], op)
                    if part and g:
                        ins.then_inc(S["bbd"], 1)
                    else:
                        link(ins)
            for part, sign in ((0, 1.0), (1, -1.0)):
                for g in range(2):
                    r = slice(ST * g, ST * g + ST)
                    ins = dve.tensor_scalar(CBD[r, :, part, GC * g:GC * g + GC], SBC[r, 2 + part, :, :], sign,
                                            None, ALU.mult)
                    if part and g:
                        ins.then_inc(S["cbd"], 1)
                    else:
                        link(ins)
            link(dve.memset(UB[:, :, 0:PAD], 0.0))
            for k in range(2):
                link(dve.memset(PBUF[k][:, 0:PAD], 0.0))

            def pooled_lo(g):
                dve.wait_ge(S["plh"], g + 1)
                dve.tensor_tensor(PLL[:, g, :], SA[g % 2][:, :], PLH[:, g, :].bitcast(F32), ALU.subtract
                                  ).then_inc(S["pll"], 1)

            for g in range(4):
                win = 2 << g
                dve.wait_ge(S["p2ev"], 4 + g + 1)
                u = UB[:, g, PAD:PAD + L]
                src = UB[:, g, :]
                for k in range(g + 1):
                    dst = PBUF[k % 2]
                    tt(dst[:, PAD:PAD + L], src[:, PAD:PAD + L], src[:, PAD - (1 << k):PAD + L - (1 << k)], ALU.add)
                    src = dst
                out = SA[g % 2]
                if g >= 2:
                    dve.wait_ge(S["pll"], g - 1)
                link(dve.scalar_tensor_tensor(out[:, :], src[:, PAD:PAD + L], 1.0 / win, u, ALU.mult, ALU.subtract))
                tt(out[:, 0:win], src[:, PAD:PAD + win], par("invc", 16 * g, win), ALU.mult)
                dve.tensor_tensor(out[:, 0:win], out[:, 0:win], u[:, 0:win], ALU.subtract).then_inc(S["pool"], 1)
                if g:
                    pooled_lo(g - 1)
            pooled_lo(3)

            dve.wait_ge(S["tvec_in"], 16)

            def phase(mm, i=0):
                def col(k):
                    return SL[:, k + 4, ds(i * 4 + mm, 1)]
                link(dve.tensor_scalar(PHB[:, :], TVEC[:, :], col(FT5), ROUND, ALU.mult, ALU.add))
                link(dve.tensor_scalar(PHA[:, :], TVEC[:, :], col(FH5), None, ALU.mult))
                link(dve.scalar_tensor_tensor(PHA[:, :], PHB[:, :], ROUND, PHA[:, :], ALU.subtract, ALU.subtract))
                dve.scalar_tensor_tensor(PHA[:, :], TVEC[:, :], col(FL5), PHA[:, :], ALU.mult, ALU.subtract
                                         ).then_inc(S["ph"], 1)

            def group(mm, i):
                cos = COS[mm % 2]
                b = 2 + 2 * (mm % 2)
                dve.wait_ge(S["tr"], i * 16 + (4 * mm + 4))
                dve.wait_ge(S["prd"], i * 16 + 4 * mm + 1)
                dve.scalar_tensor_tensor(SIN[:, :], SH[:, :], 2.0, CH[:, :], ALU.mult, ALU.mult
                                         ).then_inc(S["sn"], 1)
                phase(mm + 1, i)
                dve.wait_ge(S["sn"], i * 4 + (mm + 1))
                dve.wait_ge(S["bmm"], i * 4 + (mm + 1) + 1)
                link(dve.tensor_tensor(T1[:, :], bank(b), cos[:, :], ALU.mult))
                link(dve.tensor_tensor(T2[:, :], bank(b + 1), SIN[:, :], ALU.mult))
                tt(T1[:, :], T1[:, :], T2[:, :], ALU.add)
                link(dve.tensor_tensor(T3[:, :], bank(b + 1), cos[:, :], ALU.mult))
                dve.tensor_tensor(T2[:, :], bank(b), SIN[:, :], ALU.mult).then_inc(S["burd"], 1)
                mag = SL[:, MAG5 + 4, ds(i * 4 + mm, 1)].to_broadcast([P, L])
                link(dve.tensor_tensor_scan(SRE[:, :], mag, T1[:, :], 0.0, ALU.mult, ALU.add))
                dve.wait_ge(S["burd"], i * 4 + (mm + 3))
                tt(T3[:, :], T3[:, :], T2[:, :], ALU.subtract)
                link(dve.tensor_tensor_scan(SIM[:, :], mag, T3[:, :], 0.0, ALU.mult, ALU.add))
                dve.wait_ge(S["cmm"], i * 4 + mm + 1)
                dve.tensor_tensor(PRD[0][:, :], cos[:, :], SRE[:, :], ALU.mult).then_inc(S["prd"], 1)
                dve.scalar_tensor_tensor(PRD[1][:, :], SIN[:, :], -1.0, SIM[:, :], ALU.mult, ALU.mult
                                         ).then_inc(S["prd"], 1)
                dve.tensor_tensor(PRD[2][:, :], SIN[:, :], SRE[:, :], ALU.mult).then_inc(S["prd"], 1)
                dve.tensor_tensor(PRD[3][:, :], cos[:, :], SIM[:, :], ALU.mult).then_inc(S["prd"], 1)

            for k in range(2):
                dve.tensor_copy(SC[:, 8 + k:9 + k], ONES[:, 0:1]).then_inc(S["burd"], 1)
            phase(0)
            with repeat(dve, 4, (own, 40)) as i:
                for mm in range(4):
                    group(mm, i)
                dve.wait_ge(S["cmm"], i * 4 + 4 + 1)
                dve.scalar_tensor_tensor(tile_of(UA, i), tile_of(UA, i), par_at("sd", i), bank(6), ALU.mult,
                                         ALU.add).then_inc(S["yev"], 1)

            def lo(out, src, hi, sem):
                dve.tensor_tensor(out, src, hi.bitcast(F32), ALU.subtract).then_inc(sem, 1)

            def gated_pool(g):
                dve.wait_ge(*((S["pmm"], g + 1) if g < 3 else (tile_done, FIRST_TILE["poolw"] + 1)))
                dve.scalar_tensor_tensor(TY[g % 2][:, :], bank((OBASE["poolw"] + g) % 2), par("pscale", g),
                                         ZAB[:, 4 + g, :], ALU.mult, ALU.mult).then_inc(S["ybf"], 1)

            def gated_pool_lo(g):
                dve.wait_ge(S["ybh"], g + 1)
                lo(PLL[:, g, :], TY[g % 2][:, :], PLH[:, g, :], S["ybl"])

            dve.wait_ge(S["p2ev"], 32)
            gated_pool(0)
            gated_pool(1)
            for k in range(4):
                dve.wait_ge(S["yh"], k + 1)
                lo(HL[:, 4 + k, :], UA[:, k, :], HH[:, 4 + k, :], S["yl"])
            gated_pool_lo(0)
            dve.wait_ge(S["ybl"], 1)
            gated_pool(2)
            gated_pool_lo(1)
            dve.wait_ge(S["ybl"], 2)
            gated_pool(3)
            gated_pool_lo(2)
            gated_pool_lo(3)
            for j in range(4):
                dve.wait_ge(S["sg"], j + 1)
                link(dve.scalar_tensor_tensor(TS[j % 2][:, :], TS[j % 2][:, :], 1.0, UA[:, j, :], ALU.add, ALU.mult))
                dve.scalar_tensor_tensor(TS[j % 2][:, :], TS[j % 2][:, :], 0.5, ZAB[:, j, :], ALU.mult, ALU.mult
                                         ).then_inc(S["yaf"], 1)
                dve.wait_ge(S["yah"], j + 1)
                lo(HL[:, j, :], TS[j % 2][:, :], HH[:, j, :], S["yal"])
            with repeat(dve, 4, (own, 2)) as i:
                for j in range(2):
                    n = i * 2 + j
                    dve.wait_ge(S["amm"], i * 2 + (j + 1))
                    dve.wait_ge(S["ml"], n + 1)
                    link(dve.scalar_tensor_tensor(TY[j][:, :], tile_of(GAB, n), 1.0, bank(2 * j), ALU.add, ALU.mult))
                    dve.wait_ge(tile_done, n + (FIRST_TILE["branch"] + 1))
                    dve.scalar_tensor_tensor(TS[j][:, :], tile_of(GAB, i * 2 + (8 + j)), 1.0, bank(2 * j + 1),
                                             ALU.add, ALU.mult).then_inc(S["mev"], 1)
                    dve.wait_ge(S["mev"], n + 1)
                    dve.tensor_tensor(TY[j][:, :], TY[j][:, :], TS[j][:, :], ALU.add).then_inc(S["mrg"], 1)
                    dve.wait_ge(S["mh"], n + 1)
                    lo(tile_of(ML, n), TY[j][:, :], tile_of(MH, n), S["ml"])
            link(dve.memset(SSQ[:, :], 0.0))
            with dve.Fori(0, 4) as i:
                for j in range(2):
                    n = i * 2 + j
                    dve.wait_ge(tile_done, n + (FIRST_TILE["out2"] + 1))
                    dve.scalar_tensor_tensor(tile_of(X, n), bank((OBASE["out2"] + j) % 2), 0.5, tile_of(X, n),
                                             ALU.mult, ALU.add).then_inc(S["resid"], 1)
                    add_squares(40 + j, j, i, 2)
            dve.wait_ge(S["radd"], 48)
            sums_ready()
            dve.wait_ge(S["sqrt"], NINDEX["fin2"] + 1)
            link(dve.reciprocal(RT[:, :], RT[:, :]))
            for k in range(KD):
                dve.scalar_tensor_tensor(X[:, k, :], X[:, k, :], par("gfin2", k), RT[:, :], ALU.mult, ALU.mult
                                         ).then_inc(S["oready"], 1)

        block = ctx.enter_context(nc.Block())

        @block.sync
        def _(sp):
            def ring(stage, w, j, i=0, per=0, chunks=None):
                t = FIRST_TILE[stage] + j
                n = (chunks or CHUNKS[stage]) * P
                if t >= 2:
                    sp.wait_ge(tile_split, i * per + (t - 1))
                sp.dma_start(RAW[t % 2][:, 0:n],
                             w[ds(i * per + j, 1), :, :].rearrange("a p n -> p (a n)")
                             ).then_inc(tile_loaded[t % 2], 16)

            def mod_load(j, first, i=0, per=0, after=None):
                if after is not None:
                    sp.wait_ge(S["mod_used"], after)
                sp.dma_start(MR[j % 2][:, :], a["modw"][ds(i * per + j, 1), :, :].rearrange("a p n -> p (a n)")
                             ).then_inc(S[f"mod_in{j % 2}"], 16)

            sp.dma_start(CB[:, :], a["c"].partition_broadcast(P)).then_inc(S["c_in"], 16)
            sp.dma_start(CCB[:, :], a["cc"].partition_broadcast(P)).then_inc(S["cc_in"], 16)
            mod_load(0, True)
            mod_load(1, True)
            sp.dma_start(X[:, :, :], a["x"]).then_inc(S["x_in"], 16)
            sp.dma_start(PAR[:, :], a["par"]).then_inc(S["par_in"], 16)
            sp.dma_start(CTX[:, :, :], a["ctx"]).then_inc(S["ctx_in"], 16)
            ring("dq", a["wdq"], 0)
            ring("dq", a["wdq"], 1)
            for j in range(2, 16):
                mod_load(j, True, after=j - 1)
            ring("dq", a["wdq"], 2)
            ring("dq", a["wdq"], 3)
            for j in range(3):
                ring("kv", a["wdkv"], j)
            for j in range(2):
                ring("uv", a["wuv"], j)
            ring("heads", a["whead"], 0)
            with sp.Fori(0, 3) as i:
                for jj in range(2):
                    ring("heads", a["whead"], 1 + jj, i, 2)
                    for m in range(11):
                        j = 16 + 11 * jj + m
                        mod_load(j, False, i, 22, after=i * 22 + (j - 1))
            ring("heads", a["whead"], 7)
            for m in range(14):
                mod_load(82 + m, False, after=82 + m - 1)
            for j in range(2):
                ring("wo", a["wo"], j)
            with sp.Fori(0, 3) as i:
                for j in range(2):
                    ring("wo", a["wo"], 2 + j, i, 2)
            for l in range(2):
                with sp.Fori(0, KF) as i:
                    for j in range(2):
                        ring(f"up{l}", a[f"wup{l}"], j, i, 2)
                with sp.Fori(0, 4) as i:
                    for j in range(4):
                        ring(f"down{l}", a[f"wdn{l}"], j, i, 4)
                if l == 0:
                    sp_hyena(sp, ring)
            sp_second(sp, ring)
            for k in range(KD):
                sp.wait_ge(S["oready"], k + 1)
                sp.dma_start(a["out"][:, k:k + 1, :], X[:, k:k + 1, :]).then_inc(S["out_done"], 16)
            sp.wait_ge(S["out_done"], 16 * KD)

        @block.gpsimd
        def _(pool):
            pool.memset(ONES[:, :], 1.0).then_inc(S["pchain"], 1)
            pool.memset(SC[:, 0:1], EPS).then_inc(S["pchain"], 1)
            pool.memset(IDENT[:, :], 0.0).then_inc(S["pchain"], 1)
            pool.memset(VC[:, :, VH:P], 1.0).then_inc(S["pchain"], 1)
            for k, name in enumerate(FROM_ONE):
                pool.memset(SC[:, 32 + k:33 + k], 0.0).then_inc(S[name], 1)
            pool.wait_ge(S["pchain"], 4)
            pool.affine_select(out=IDENT[:, :], in_=IDENT[:, :], compare_op=ALU.not_equal, fill=1.0,
                               base=0, pattern=[[-1, P]], channel_multiplier=1).then_inc(S["consts"], 1)

            def split(stage, j, i=0, per=0, chunks=None):
                t = FIRST_TILE[stage] + j
                n = (chunks or CHUNKS[stage]) * P
                s = t % 2
                if t >= 2:
                    pool.wait_ge(tile_done, i * per + (t - 1))
                pool.wait_ge(tile_loaded[s], i * (8 * per) + 16 * (t // 2 + 1))
                pool.tensor_tensor(SC[0:1, 100:101], ONES[0:1, 0:1], ONES[0:1, 0:1], ALU.add)
                pool.tensor_scalar(WH[s][:, 0:n], RAW[s][:, 0:n], 1.0, 0.0, ALU.mult, ALU.add
                                   ).then_inc(tile_hi, 1)
                pool.wait_ge(tile_hi, i * per + (t + 1))
                pool.tensor_tensor(WL[s][:, 0:n], RAW[s][:, 0:n], WH[s][:, 0:n].bitcast(F32),
                                   ALU.subtract).then_inc(tile_split, 1)

            for st, n in (("dq", 4), ("kv", 3), ("uv", 2)):
                for j in range(n):
                    split(st, j)
            with pool.Fori(0, 4) as i:
                for j in range(2):
                    split("heads", j, i, 2)
            with pool.Fori(0, 4) as i:
                for j in range(2):
                    split("wo", j, i, 2)
            for l in range(2):
                with pool.Fori(0, KF) as i:
                    for j in range(2):
                        split(f"up{l}", j, i, 2)
                with pool.Fori(0, 8) as i:
                    for j in range(2):
                        split(f"down{l}", j, i, 2)
                if l == 0:
                    pool_hyena(pool, split)
            pool_second(pool, split)

        @block.tensor
        def _(pe):
            def stat(name, ssq, w=L):
                n = NINDEX[name]
                pe.wait_ge(S["ssq"], n + 1)
                if n:
                    pe.wait_ge(S["sqrt"], n)
                pe.matmul(bank(7, w), ONES[:, :], ssq[:, 0:w], start=True, stop=True
                          ).then_inc(S["stat"], 1)

            def mm3(out, wh, wl, xh, xl, first, last):
                pe.matmul(out, wh, xh, start=first, stop=False)
                pe.matmul(out, wh, xl, start=False, stop=False)
                return pe.matmul(out, wl, xh, start=False, stop=last)

            def chunk(s, k):
                return WH[s][:, k * P:(k + 1) * P], WL[s][:, k * P:(k + 1) * P]

            def linear(stage, j, xh, xl, evac, i=0, per=0, kn=KD, tiles=1, nbase=None):
                bk = (OBASE[stage] + j) % 2
                if per or j >= 2:
                    pe.wait_ge(evac[0], i * per + (evac[1] + j - 1))
                for h in range(tiles):
                    t = FIRST_TILE[stage] + j * tiles + h
                    pe.wait_ge(tile_split, i * (per * tiles) + (t + 1))
                    for k in range(kn):
                        kk = h * kn + k
                        if nbase is not None:
                            pe.wait_ge(S["nl"], nbase + k + 1)
                        m = mm3(bank(bk), *chunk(t % 2, k), xh[:, kk, :], xl[:, kk, :],
                                kk == 0, kk == tiles * kn - 1)
                    m.then_inc(tile_done, 1)

            pe.wait_ge(S["filt_in"], 64)
            pe.matmul(PS[0:HID_F, 2, :], FW1[:, :], ZT[:, :], start=True, stop=True).then_inc(S["fmm"], 1)
            pe.wait_ge(S["consts"], 1)
            stat("x0", SSQA)
            pe.wait_ge(S["fsin"], 1)
            pe.matmul(PS[0:HID_F, 3, :], FW2[:, :], FA[:, :], start=True, stop=True).then_inc(S["fmm"], 1)
            stat("ctx", SSQA, LC)
            for j in range(4):
                linear("dq", j, HH, HL, (S["cq_sq"], 0), nbase=NBASE["x0"] if j == 0 else None)
            for j in range(3):
                t = FIRST_TILE["kv"] + j
                b = OBASE["kv"] + 2 * j
                pe.wait_ge(tile_split, t + 1)
                pe.wait_ge(*((S["ckv_ev"], 2 * j - 1) if j else (S["cq_sq"], 3)))
                for k in range(KD):
                    m = mm3(bank(b % 2), *chunk(t % 2, k), HH[:, k, :], HL[:, k, :], k == 0, k == KD - 1)
                m.then_inc(S["kv_x"], 1)
                b += 1
                pe.wait_ge(*((S["ckv_ev"], 2 * j) if j else (S["cq_sq"], 4)))
                for k in range(KD):
                    if j == 0:
                        pe.wait_ge(S["nl"], NBASE["ctx"] + k + 1)
                    m = mm3(bank(b % 2, LC), *chunk(t % 2, k), HCH[:, k, :], HCL[:, k, :], k == 0, k == KD - 1)
                m.then_inc(tile_done, 1)
                if j == 0:
                    stat("cq", SSQA)
            stat("ckx", SSQA)
            stat("ckc", SSQA[:, L:LK], LC)
            pe.wait_ge(S["nl"], NBASE["ckc"] + 2)
            for j in range(2):
                t = FIRST_TILE["uv"] + j
                pe.wait_ge(tile_split, t + 1)
                for m6 in range(6):
                    n = 6 * j + m6
                    b = OBASE["uv"] + n
                    pe.wait_ge(*((S["krot"], 2 + 4 * n) if n < 2 else (S["v_ev"], n - 1)))
                    for k in range(2):
                        wh = WH[t % 2][:, 512 * k:512 * k + 512]
                        wl = WL[t % 2][:, 512 * k:512 * k + 512]
                        kh = CKH[:, k, m6 * P:(m6 + 1) * P]
                        kl = CKL[:, k, m6 * P:(m6 + 1) * P]
                        pe.matmul(bank(b % 2), kh, wh, start=k == 0, stop=False)
                        pe.matmul(bank(b % 2), kh, wl, start=False, stop=False)
                        m = pe.matmul(bank(b % 2), kl, wh, start=False, stop=k == 1)
                    if m6 < 5:
                        m.then_inc(S["proj"], 1)
                    else:
                        m.then_inc(tile_done, 1)

            def project(p, i=0, per=0):
                t = FIRST_TILE["heads"] + p
                s = t % 2
                pe.wait_ge(tile_split, i * per + (t + 1))
                for hb in range(2):
                    if p and hb:
                        pe.wait_ge(S["vc"], i * (2 * per) + (2 * p - 1))
                    for k in range(4):
                        m = mm3(bank(4 + hb), *chunk(s, 4 * hb + k), CQH[:, k, :], CQL[:, k, :], k == 0, k == 3)
                    m.then_inc(S["proj"], 1)
                for c, (lo, hi) in enumerate(((0, L), (L, LK))):
                    pe.wait_ge(S["qready"], i * (2 * per) + (2 * p + 1 + c))
                    for k in range(2):
                        m = mm3(bank(4 + c, hi - lo), *chunk(s, 8 + k), CKH[:, k, lo:hi], CKL[:, k, lo:hi],
                                k == 0, k == 1)
                    m.then_inc(S["proj"] if c == 0 else tile_done, 1)

            def scores(h, i=0, per=0):
                hb = h % 2
                pe.wait_ge(S["qready"], i * per + (h + 1))
                pe.wait_ge(S["kready"], i * (2 * per) + 4 * (h // 2 + 1))
                for qt in range(4):
                    g = 4 * h + qt
                    if g >= 2:
                        pe.wait_ge(S["sexp"], i * (4 * per) + (g - 1))
                    b = 2 * (qt % 2)
                    pe.matmul(bank(b), Q[hb][:, qt * P:(qt + 1) * P], KP[hb][:, 0:L], start=True, stop=True)
                    pe.matmul(bank(b + 1, LC), Q[hb][:, qt * P:(qt + 1) * P], KP[hb][:, L:LK],
                              start=True, stop=True).then_inc(S["s_ready"], 1)

            def attend(h, i=0, per=0):
                hb = h % 2
                ob = 4 + hb
                pe.wait_ge(S["sexp"], i * (4 * per) + 4 * (h + 1))

                def turn(kt):
                    if per or 3 * h + kt // 2 > 0:
                        pe.wait_ge(S["pt_act"] if kt % 2 == 0 else S["pt_dve"], i * (3 * per) + (3 * h + kt // 2) + 1)
                    for qt in range(4):
                        m = pe.transpose(PS[:, 6 + kt % 2, qt * P:(qt + 1) * P],
                                         PR[hb][:, qt, kt * P:(kt + 1) * P], IDENT[:, :])
                    m.then_inc(S["s_tr"], 1)

                def value(kt):
                    pe.wait_ge(S["pt_act"] if kt % 2 == 0 else S["pt_dve"], i * (3 * per) + (3 * h + kt // 2 + 1) + 1)
                    m = pe.matmul(bank(ob), VC[:, kt, :], PT[:, kt, :], start=kt == 0, stop=kt == 5)
                    if kt == 5:
                        m.then_inc(S["pv"], 1)

                turn(0)
                turn(1)
                pe.wait_ge(S["vc"], i * per + (h + 1))
                pe.wait_ge(S["kready"], i * (2 * per) + (4 * min(h // 2 + 2, 8) - 2 + 2 * hb))
                for kt in range(6):
                    value(kt)
                    if kt + 2 < 6:
                        turn(kt + 2)

            pe.wait_ge(S["v_ev"], 12)
            project(0)
            scores(0)

            def pair(p, i=0, per=0):
                scores(2 * p + 1, i, 2 * per)
                project(p + 1, i, per)
                attend(2 * p, i, 2 * per)
                scores(2 * p + 2, i, 2 * per)
                attend(2 * p + 1, i, 2 * per)

            with pe.Fori(0, 3) as i:
                pair(0, i, 2)
                pair(1, i, 2)
            pair(6)
            scores(15)
            attend(14)
            attend(15)

            pe.wait_ge(S["pair_done"], 8)
            for j in range(2):
                linear("wo", j, HH, HL, (S["resid"], 0))
            with pe.Fori(0, 3) as i:
                for j in range(2):
                    linear("wo", 2 + j, HH, HL, (S["resid"], 0), i, 2)
            for l in range(2):
                if l == 1:
                    pe_hyena(pe, linear, stat, mm3, chunk)
                stat(f"ffn{l}", SSQ)
                for j in range(2):
                    linear(f"up{l}", j, HH, HL, (S["zc"], NUP * l), nbase=NBASE[f"ffn{l}"])
                with pe.Fori(0, KF - 1) as i:
                    for j in range(2):
                        linear(f"up{l}", 2 + j, HH, HL, (S["zc"], NUP * l), i, 2)
                pe.wait_ge(S["hidl"], KF * (l + 1))
                with pe.Fori(0, 4) as i:
                    for j in range(2):
                        linear(f"down{l}", j, HIDH, HIDL, (S["resid"], RBASE[f"down{l}"]), i, 2, kn=11, tiles=2)
            pe_second(pe, linear, stat, mm3, chunk)

        @block.scalar
        def _(act):
            act.dma_start(ZT[:, :], a["zt"]).then_inc(S["filt_in"], 16)
            act.dma_start(FW1[:, :], a["fw1"]).then_inc(S["filt_in"], 16)
            act.dma_start(FW2[:, :], a["fw2"]).then_inc(S["filt_in"], 16)
            act.dma_start(FPAR[:, :], a["fpar"]).then_inc(S["filt_in"], 16)
            act.dma_start(QTAB[:, :], a["qtab"]).then_inc(S["tab_in"], 16)
            act.dma_start(KCOS[:, :], a["kcos"]).then_inc(S["tab_in"], 16)
            act.dma_start(KSIN[P // 2:P, :], a["ksin"]).then_inc(S["tab_in"], 16)

            def norm(name, dst, w, dn, rt, tn, tm, shift=0):
                n = NINDEX[name]
                act.wait_ge(S["stat"], n + 1)
                act.wait_ge(S["nt"], NBASE[name])
                act.activation(rt[:, 0:w], bank(7, w), ACT.Sqrt, bias=SC[:, 0:1], scale=1.0 / dn
                               ).then_inc(S["sqrt"], 1)
                for k in range(NTILES[name]):
                    g = NBASE[name] + k
                    scale, bias = GAIN[name](k)
                    act.wait_ge(S["nt"], g + 1)
                    if g >= 2:
                        act.wait_ge(S["nl"], g - 1)
                    if bias is None:
                        act.activation(tm[k % 2][:, 0:w], tn[k % 2][:, 0:w], ACT.Identity, scale=scale
                                       ).then_inc(S["na"], 1)
                    else:
                        act.activation(tm[k % 2][:, 0:w], tn[k % 2][:, 0:w], ACT.Identity, bias=bias,
                                       scale=scale).then_inc(S["na"], 1)
                    act.wait_ge(S["na"], g + 1)
                    act.copy(dst[:, k, shift:shift + w], tm[k % 2][:, 0:w]).then_inc(S["nh"], 1)

            act.wait_ge(S["c_in"], 16)
            act.activation(CB[:, :], CB[:, :], ACT.Silu).then_inc(S["silu_c"], 1)
            act.wait_ge(S["cc_in"], 16)
            act.activation(CCB[:, :], CCB[:, :], ACT.Silu).then_inc(S["silu_c"], 1)
            act.wait_ge(S["x_in"], 16)
            act.activation(XSQ[:, :, :], X[:, :, :], ACT.Square).then_inc(S["xsq"], 1)
            act.wait_ge(S["fa"], 1)
            act.activation(FA[:, :], FA[:, :], ACT.Sin).then_inc(S["fsin"], 1)
            act.wait_ge(S["fa"], 2)
            for half in range(2):
                act.activation(H2T[HID_F * half:HID_F * half + HID_F, :], FA[:, :], ACT.Sin
                               ).then_inc(S["fsin"], 1)
            act.wait_ge(S["ctx_in"], 16)
            act.wait_ge(S["ssq"], 1)
            act.activation(XSQ[:, 0:4, :].rearrange("p a n -> p (a n)"),
                           CTX[:, :, :].rearrange("p a n -> p (a n)"), ACT.Square).then_inc(S["xsq"], 1)
            act.wait_ge(S["ab"], 1)
            norm("x0", HH, L, D, RTA, TA, TB)
            norm("ctx", HCH, LC, D, RTA, TA, TB)
            for j in range(4):
                act.wait_ge(tile_done, FIRST_TILE["dq"] + j + 1)
                act.copy(C32[:, j, :], bank((OBASE["dq"] + j) % 2)).then_inc(S["cq_ev"], 1)
                if j >= 2:
                    act.wait_ge(S["cq_add"], j - 1)
                act.activation(TA[j % 2][:, :], bank((OBASE["dq"] + j) % 2), ACT.Square
                               ).then_inc(S["cq_sq"], 1)
            for j in range(2):
                b = OBASE["kv"] + 2 * j
                act.wait_ge(S["kv_x"], j + 1)
                act.copy(CK32[:, j, 0:L], bank(b % 2)).then_inc(S["ckv_ev"], 1)
                act.wait_ge(tile_done, FIRST_TILE["kv"] + j + 1)
                act.copy(CK32[:, j, L:LK], bank((b + 1) % 2, LC)).then_inc(S["ckv_ev"], 1)
                if j == 0:
                    norm("cq", CQH, L, QL, RTA, TA, TB)
            norm("ckx", CKH, L, KVL, RTA, TA, TB)
            norm("ckc", CKH, LC, KVL, RTA, TA, TB, shift=L)
            for n in range(12):
                if n % 6 < 5:
                    act.wait_ge(S["proj"], 5 * (n // 6) + n % 6 + 1)
                else:
                    act.wait_ge(tile_done, FIRST_TILE["uv"] + n // 6 + 1)
                act.copy(V[:, n % 6, 512 * (n // 6):512 * (n // 6) + 512], bank((OBASE["uv"] + n) % 2)
                         ).then_inc(S["v_ev"], 1)

            def keys(p, i=0, per=0):
                act.wait_ge(S["proj"], i * (3 * per) + (10 + 3 * p + 3))
                for hb in range(2):
                    act.copy(KP[hb][0:NOPE, 0:L], PS[NOPE * hb:NOPE * hb + NOPE, 4, :]
                             ).then_inc(S["kready"], 1)
                act.wait_ge(tile_done, i * per + (FIRST_TILE["heads"] + p + 1))
                for hb in range(2):
                    act.copy(KP[hb][0:NOPE, L:LK], PS[NOPE * hb:NOPE * hb + NOPE, 5, 0:LC]
                             ).then_inc(S["kready"], 1)

            def exps(h, i=0, per=0):
                if per or h >= 2:
                    act.wait_ge(S["s_tr"], i * (6 * per) + 6 * (h - 1) + 1)
                for qt in range(4):
                    act.wait_ge(S["smax"], i * (4 * per) + (4 * h + qt + 1))
                    act.activation(PR[h % 2][:, qt, :], wide(2 * (qt % 2), LK), ACT.Exp,
                                   bias=NMX[:, (4 * h + qt) % 8:(4 * h + qt) % 8 + 1], scale=1.0
                                   ).then_inc(S["sexp"], 1)

            def turned(h, i=0, per=0):
                for kt in (0, 2, 4):
                    act.wait_ge(S["s_tr"], i * (6 * per) + (6 * h + kt + 1) + 1)
                    if kt == 0 and (per or h):
                        act.wait_ge(S["pv"], i * per + h + 1)
                    act.copy(PT[:, kt, :], bank(6)).then_inc(S["pt_act"], 1)

            def pair(p, i=0, per=0):
                exps(2 * p + 1, i, 2 * per)
                keys(p + 1, i, per)
                turned(2 * p, i, 2 * per)
                exps(2 * p + 2, i, 2 * per)
                turned(2 * p + 1, i, 2 * per)
                heads_out(p, i, per)

            def heads_out(p, i=0, per=0):
                act.wait_ge(S["oev"], i * (2 * per) + (2 * p + 2))
                act.copy(HH[:, ds(i * per + p, 1), :].rearrange("p a n -> p (a n)"), O32[:, :]
                         ).then_inc(S["ohi"], 1)

            keys(0)
            exps(0)
            with act.Fori(0, 3) as i:
                pair(0, i, 2)
                pair(1, i, 2)
            pair(6)
            exps(15)
            turned(14)
            turned(15)
            heads_out(7)

            def squares(stage, j, i=0, per=0):
                n = RBASE[stage] + j
                act.wait_ge(S["resid"], i * per + (n + 1))
                if n >= 2:
                    act.wait_ge(S["radd"], i * per + (n - 1))
                act.activation(SQ[j % 2][:, :], X[:, ds(i * per + j, 1), :].rearrange("p a n -> p (a n)"),
                               ACT.Square).then_inc(S["rsq"], 1)

            def ffn_up(l, i):
                n = KF * l
                t = FIRST_TILE[f"up{l}"]
                for half, buf in ((0, ZA), (1, ZG)):
                    act.wait_ge(tile_done, i * 2 + (t + half + 1))
                    if half == 0:
                        act.wait_ge(S["hid"], i + n + 1)
                    c = KF * half + l * NUP
                    act.activation(buf[:, :], bank((OBASE[f"up{l}"] + half) % 2), ACT.Identity,
                                   scale=par_at("fcw", i + (l * 3 * NUP + NUP + KF * half)),
                                   bias=par_at("fcb", i + c)).then_inc(S["za"], 1)
                act.wait_ge(S["zc"], i * 2 + (2 * n + 2))
                act.activation(ZG[:, :], ZG[:, :], ACT.Silu).then_inc(S["silu"], 1)
                act.wait_ge(S["hid"], i + (n + 1) + 1)
                act.copy(HIDH[:, ds(i, 1), :].rearrange("p a n -> p (a n)"), HID[:, :]
                         ).then_inc(S["hidh"], 1)

            for j in range(2):
                squares("wo", j)
            with act.Fori(0, 3) as i:
                for j in range(2):
                    squares("wo", 2 + j, i, 2)
            for l in range(2):
                if l == 1:
                    act_hyena(act, norm, squares)
                act.wait_ge(S["ab"], 2 if l == 0 else 4)
                norm(f"ffn{l}", HH, L, D, RT, TN, TM)
                act.activation(SC[:, 1:2], SC[:, 0:1], ACT.Silu).then_inc(S["achain"], 1)
                with act.Fori(0, KF) as i:
                    ffn_up(l, i)
                with act.Fori(0, 4) as i:
                    for j in range(2):
                        squares(f"down{l}", j, i, 2)
            act_second(act, norm, squares)

        @block.vector
        def _(dve):
            own = Tally(S["dchain"])

            def link(ins):
                v = own.up()
                ins.then_inc(S["dchain"], 1)
                dve.wait_ge(S["dchain"], v)

            def norm(name, src, dst_h, dst_l, w, rt, tn, tm, shift=0):
                n = NINDEX[name]
                dve.wait_ge(S["sqrt"], n + 1)
                link(dve.reciprocal(rt[:, 0:w], rt[:, 0:w]))

                def low(k):
                    g = NBASE[name] + k
                    dve.wait_ge(S["nh"], g + 1)
                    dve.tensor_tensor(dst_l[:, k, shift:shift + w], tm[k % 2][:, 0:w],
                                      dst_h[:, k, shift:shift + w].bitcast(F32), ALU.subtract
                                      ).then_inc(S["nl"], 1)

                for k in range(NTILES[name]):
                    g = NBASE[name] + k
                    if g >= 2:
                        dve.wait_ge(S["na"], g - 1)
                    dve.tensor_tensor(tn[k % 2][:, 0:w], src[:, k, shift:shift + w], rt[:, 0:w], ALU.mult
                                      ).then_inc(S["nt"], 1)
                    if k:
                        low(k - 1)
                low(NTILES[name] - 1)

            def reduce_angle(x, k, w=L):
                link(dve.tensor_scalar(k, x, 1.0 / TWO_PI, None, ALU.mult))
                link(dve.tensor_scalar(k, k, ROUND, ROUND, ALU.add, ALU.subtract))
                for part in (PI_A, PI_B, PI_C):
                    link(dve.scalar_tensor_tensor(x, k, -part, x, ALU.mult, ALU.add))

            for layer in range(2):
                dve.wait_ge(S["fmm"], layer + 1)
                link(dve.tensor_scalar(FA[:, :], PS[0:HID_F, 2 + layer, :], FPAR[:, 2 * layer:2 * layer + 1],
                                       FPAR[:, 2 * layer + 1:2 * layer + 2], ALU.add, ALU.mult))
                reduce_angle(FA[:, :], FK[:, :])
                dve.tensor_scalar(FA[:, :], FA[:, :], math.pi, -math.pi, ALU.min, ALU.max
                                  ).then_inc(S["fa"], 1)
                if layer == 0:
                    dve.wait_ge(S["xsq"], 1)
                    dve.tensor_reduce(SSQA[:, 0:L], XSQ[:, :, :].rearrange("p k t -> p t k"), AX.X, ALU.add
                                      ).then_inc(S["ssq"], 1)
            dve.wait_ge(S["silu_c"], 2)
            for j in range(16):
                dve.wait_ge(S[f"mod_in{j % 2}"], 16 * (j // 2 + 1))
                link(dve.tensor_tensor_reduce(C32[:, 0:2, :].rearrange("p a n -> p (a n)"), MR[j % 2][:, :],
                                              CB[:, :], 1.0, 0.0, ALU.mult, ALU.add, MOD[:, j:j + 1]))
                dve.tensor_tensor_reduce(MR[j % 2][:, :], MR[j % 2][:, :], CCB[:, :], 1.0, 0.0,
                                         ALU.mult, ALU.add, MODC[:, j:j + 1]).then_inc(S["mod_used"], 1)
            dve.wait_ge(S["xsq"], 2)
            dve.wait_ge(S["stat"], 1)
            dve.tensor_reduce(SSQA[:, 0:LC], XSQ[:, 0:4, :].rearrange("p a n -> p (a n)").rearrange(
                "p (k t) -> p t k", t=LC), AX.X, ALU.add).then_inc(S["ssq"], 1)
            dve.wait_ge(S["par_in"], 16)
            dve.wait_ge(S["mod_used"], 16)
            link(dve.tensor_tensor(MOD[:, 0:16], MOD[:, 0:16], par("modb", 0, 16), ALU.add))
            link(dve.tensor_tensor(MODC[:, :], MODC[:, :], par("modb", 0, 16), ALU.add))
            for row, m in ((0, MOD), (2, MODC)):
                link(dve.scalar_tensor_tensor(AB[:, row, :], m[:, 8:16], 1.0, par("gmix", 0, 8), ALU.add, ALU.mult))
                link(dve.tensor_copy(AB[:, row + 1, :], m[:, 0:8]))
            dve.tensor_copy(SC[:, 2:3], ONES[:, 0:1]).then_inc(S["ab"], 1)
            norm("x0", X, HH, HL, L, RTA, TA, TB)
            norm("ctx", CTX, HCH, HCL, LC, RTA, TA, TB)
            dve.wait_ge(S["stat"], 2)
            for j in range(4):
                dve.wait_ge(S["cq_sq"], j + 1)
                if j == 0:
                    ins = dve.tensor_copy(SSQA[:, 0:L], TA[0][:, :])
                else:
                    dve.wait_ge(S["cq_add"], j)
                    ins = dve.tensor_tensor(SSQA[:, 0:L], SSQA[:, 0:L], TA[j % 2][:, :], ALU.add)
                ins.then_inc(S["cq_add"] if j < 3 else S["ssq"], 1)
            norm("cq", C32, CQH, CQL, L, RTA, TA, TB)
            dve.wait_ge(S["ckv_ev"], 4)
            link(dve.tensor_tensor(SSQA[:, :], CK32[:, 0, :], CK32[:, 0, :], ALU.mult))
            link(dve.tensor_tensor(RTA[:, :], CK32[:, 1, :], CK32[:, 1, :], ALU.mult))
            link(dve.tensor_tensor(SSQA[:, :], SSQA[:, :], RTA[:, :], ALU.add))
            dve.tensor_copy(SC[:, 3:4], ONES[:, 0:1]).then_inc(S["ssq"], 1)
            hi = slice(P // 2, P)
            dve.wait_ge(S["tab_in"], 48)
            dve.wait_ge(S["fsin"], 3)
            dve.wait_ge(S["kv_x"], 3)
            b = OBASE["kv"] + 4
            dve.tensor_tensor(K1[hi, :], PS[0:P // 2, b % 2, :], KCOS[:, :], ALU.mult).then_inc(S["krot"], 1)
            dve.tensor_tensor(C32[hi, 0, :], PS[hi, b % 2, :], KSIN[hi, :], ALU.mult).then_inc(S["krot"], 1)
            dve.wait_ge(S["krot"], 2)
            for hb in range(2):
                dve.tensor_tensor(KP[hb][hi, 0:L], K1[hi, :], C32[hi, 0, :], ALU.add).then_inc(S["krot"], 1)
            dve.wait_ge(tile_done, FIRST_TILE["kv"] + 3)
            for hb in range(2):
                dve.tensor_copy(KP[hb][hi, L:LK], PS[0:P // 2, (b + 1) % 2, 0:LC]).then_inc(S["krot"], 1)
            norm("ckx", CK32, CKH, CKL, L, RTA, TA, TB)
            dve.tensor_copy(SC[:, 4:5], ONES[:, 0:1]).then_inc(S["ssq"], 1)
            norm("ckc", CK32, CKH, CKL, LC, RTA, TA, TB, shift=L)

            def mod_rows(j, i=0, per=0, column=0):
                dve.wait_ge(S[f"mod_in{j % 2}"], i * (8 * per) + 16 * ((16 + j) // 2 + 1))
                dve.tensor_tensor_reduce(MR[j % 2][:, :], MR[j % 2][:, :], CB[:, :], 1.0, 0.0,
                                         ALU.mult, ALU.add, MACC[:, column:column + 1]
                                         ).then_inc(S["mod_used"], 1)

            def mod_store(j, n, i=0, per=0):
                dve.wait_ge(S["mod_used"], i * per + (16 + j + n))
                dve.tensor_copy(MOD[:, ds(i * per + (16 + j), n)], MACC[:, 0:n]).then_inc(S["modx"], 1)

            def queries(p, i=0, per=0):
                for hb in range(2):
                    dve.wait_ge(S["proj"], i * (3 * per) + (10 + 3 * p + 1 + hb))
                    dve.tensor_tensor(Q[hb][:, :], bank(4 + hb), QTAB[:, :], ALU.mult).then_inc(S["qready"], 1)

            def maxes(h, i=0, per=0, between=lambda qt: None):
                for qt in range(4):
                    dve.wait_ge(S["s_ready"], i * (4 * per) + (4 * h + qt + 1))
                    c = (4 * h + qt) % 8
                    dve.tensor_reduce(NMX[:, c:c + 1], wide(2 * (qt % 2), LK), AX.X, ALU.max, negate=True
                                      ).then_inc(S["smax"], 1)
                    between(qt)

            def value_copy(h, i=0, per=0):
                if per or h:
                    dve.wait_ge(S["pv"], i * per + h + 1)
                dve.tensor_copy(VC[:, :, 0:VH], V[:, :, ds(i * (VH * per) + VH * h, VH)]).then_inc(S["vc"], 1)

            def finish_head(h, i=0, per=0):
                for kt in (1, 3, 5):
                    dve.wait_ge(S["s_tr"], i * (6 * per) + (6 * h + kt + 1) + 1)
                    dve.tensor_copy(PT[:, kt, :], bank(7)).then_inc(S["pt_dve"], 1)
                hb = h % 2
                dve.wait_ge(S["pv"], i * per + (h + 1) + 1)
                link(dve.reciprocal(RC[0:VH, :], PS[VH:P, 4 + hb, :]))
                dve.tensor_tensor(O32[VH * hb:VH * hb + VH, :], PS[0:VH, 4 + hb, :], RC[0:VH, :], ALU.mult
                                  ).then_inc(S["oev"], 1)

            def pair_low(p, i=0, per=0):
                dve.wait_ge(S["ohi"], i * per + (p + 1))
                dve.tensor_tensor(HL[:, ds(i * per + p, 1), :].rearrange("p a n -> p (a n)"), O32[:, :],
                                  HH[:, ds(i * per + p, 1), :].rearrange("p a n -> p (a n)").bitcast(F32),
                                  ALU.subtract).then_inc(S["pair_done"], 1)

            def pair(p, i=0, per=0):
                m = 11 * p
                two = 11 * per
                value_copy(2 * p, i, 2 * per)
                maxes(2 * p + 1, i, 2 * per, lambda qt: mod_rows(m + qt, i, two, qt))
                queries(p + 1, i, per)
                mod_rows(m + 4, i, two, 4)
                finish_head(2 * p, i, 2 * per)
                value_copy(2 * p + 1, i, 2 * per)
                maxes(2 * p + 2, i, 2 * per, lambda qt: mod_rows(m + 5 + qt, i, two, 5 + qt))
                finish_head(2 * p + 1, i, 2 * per)
                pair_low(p, i, per)
                mod_rows(m + 9, i, two, 9)
                mod_rows(m + 10, i, two, 10)
                mod_store(m, 11, i, two)
                dve.wait_ge(S["modx"], i * per + (p + 1))

            queries(0)
            maxes(0)
            with repeat(dve, 3, (own, 4)) as i:
                pair(0, i, 2)
                pair(1, i, 2)
            pair(6)
            value_copy(14)
            maxes(15)
            finish_head(14)
            value_copy(15)
            finish_head(15)
            pair_low(7)
            for n in range(3):
                mod_rows(77 + n, column=n)
            mod_store(77, 3)
            dve.wait_ge(S["modx"], 8)
            link(dve.tensor_tensor(MOD[:, 16:96], MOD[:, 16:96], par("modb", 16, 80), ALU.add))

            def residual(stage, j, layer, i=0, per=0, tiles=1, gate=2):
                n = RBASE[stage] + j
                t = FIRST_TILE[stage] + j * tiles + tiles - 1
                xt = X[:, ds(i * per + j, 1), :].rearrange("p a n -> p (a n)")
                dve.wait_ge(tile_done, i * (per * tiles) + (t + 1))
                dve.scalar_tensor_tensor(xt, bank((OBASE[stage] + j) % 2),
                                         MOD[:, ds(i * per + (48 * layer + KD * gate + j), 1)], xt,
                                         ALU.mult, ALU.add).then_inc(S["resid"], 1)
                add_squares(n, j, i, per)

            def add_squares(n, j, i, per):
                dve.wait_ge(S["rsq"], i * per + (n + 1))
                if n or per:
                    dve.wait_ge(S["radd"], i * per + n)
                dve.tensor_tensor(SSQ[:, :], SSQ[:, :], SQ[j % 2][:, :], ALU.add).then_inc(S["radd"], 1)

            def conv_side(buf, bk, w0, w2, z, zwait, i):
                dve.wait_ge(S["za"], zwait)
                link(dve.scalar_tensor_tensor(buf[:, 1:L], bank(bk)[:, 0:L - 1], w0, buf[:, 1:L],
                                              ALU.mult, ALU.add))
                dve.scalar_tensor_tensor(buf[:, 0:L - 1], bank(bk)[:, 1:L], w2, buf[:, 0:L - 1],
                                         ALU.mult, ALU.add).then_inc(S["zc"], 1)

            def ffn_up(l, i):
                n = KF * l
                for half, buf in ((0, ZA), (1, ZG)):
                    c = l * 3 * NUP + KF * half
                    conv_side(buf, (OBASE[f"up{l}"] + half) % 2, par_at("fcw", i + c),
                              par_at("fcw", i + (c + 2 * NUP)), None, i * 2 + (2 * n + half + 1), i)
                dve.wait_ge(S["silu"], i + (n + 1))
                dve.wait_ge(S["zc"], i * 2 + (2 * n + 2))
                dve.tensor_tensor(HID[:, :], ZG[:, :], ZA[:, :], ALU.mult).then_inc(S["hid"], 1)
                dve.wait_ge(S["hidh"], i + (n + 1))
                dve.tensor_tensor(HIDL[:, ds(i, 1), :].rearrange("p a n -> p (a n)"), HID[:, :],
                                  HIDH[:, ds(i, 1), :].rearrange("p a n -> p (a n)").bitcast(F32),
                                  ALU.subtract).then_inc(S["hidl"], 1)

            def columns(layer, mix):
                k = 0 if mix else 3
                g = par("gmix" if mix else "gffn", KD * layer, KD)
                link(dve.scalar_tensor_tensor(AB[:, 0, :], mod(layer, k + 1), 1.0, g, ALU.add, ALU.mult))
                dve.tensor_copy(AB[:, 1, :], mod(layer, k)).then_inc(S["ab"], 1)

            def sums_ready():
                dve.tensor_copy(SC[:, 3:4], ONES[:, 0:1]).then_inc(S["ssq"], 1)

            link(dve.memset(SSQ[:, :], 0.0))
            columns(0, False)
            for j in range(2):
                residual("wo", j, 0)
            with dve.Fori(0, 3) as i:
                for j in range(2):
                    residual("wo", 2 + j, 0, i, 2)
            dve.wait_ge(S["radd"], 8)
            sums_ready()
            for l in range(2):
                if l == 1:
                    dve_hyena(dve, norm, link, own, columns, sums_ready, add_squares)
                norm(f"ffn{l}", X, HH, HL, L, RT, TN, TM)
                link(dve.memset(SSQ[:, :], 0.0))
                with repeat(dve, KF, (own, 2)) as i:
                    ffn_up(l, i)
                with dve.Fori(0, 4) as i:
                    for j in range(2):
                        residual(f"down{l}", j, l, i, 2, tiles=2, gate=5)
                dve.wait_ge(S["radd"], RBASE[f"down{l}"] + 8)
                if l == 0:
                    columns(1, True)
                sums_ready()
            dve_second(dve, norm, link, own, reduce_angle, add_squares, sums_ready)


def constants():
    f4 = np.float32
    t = np.linspace(0.0, 1.0, L, dtype=f4)
    w = (f4(TWO_PI) * np.arange(L, dtype=f4) / f4(L)).astype(f4)
    f = np.linspace(1e-4, HY_BANDS - 1, HY_BANDS, dtype=f4)
    wf = (w[:, None] * f).astype(f4).astype(np.float64)
    zt = np.concatenate([t[:, None], np.cos(wf), -np.sin(wf)], axis=1).T.astype(f4)
    half = ROPE // 2
    inv = (10000.0 ** (-np.arange(0, half, 2, dtype=np.float64) / half)).astype(f4)
    row = np.repeat(np.arange(L // GRID_W, dtype=f4), GRID_W)
    col = np.tile(np.arange(GRID_W, dtype=f4), L // GRID_W)
    ar, ac = row[:, None] * inv, col[:, None] * inv
    ang = np.concatenate([ar, ar, ac, ac], axis=1).astype(np.float64).T
    q = ROPE // 4
    sign = np.repeat([-1.0, 1.0, -1.0, 1.0], q)[:, None]
    cos, sin = np.cos(ang), np.sin(ang) * sign
    qtab = np.concatenate([np.ones((NOPE, L)), cos, sin]) / math.sqrt(NOPE + ROPE)
    kcos = np.concatenate([cos, cos])
    ksin = np.concatenate([sin, sin])
    tt, ff = np.arange(L), np.arange(L)
    turn = (tt[:, None] * (2 * ff[None, :] + 1)) % (4 * L)
    th = np.pi * turn / (2 * L)
    c, s = np.cos(th), np.sin(th)
    fwd = np.stack([c, s]).reshape(2, 4, P, 4, P).transpose(3, 2, 0, 1, 4)
    inv_t = np.stack([c.T, s.T]).reshape(2, 4, P, L).transpose(2, 0, 1, 3) / L
    tvec = np.broadcast_to(np.arange(L, dtype=f4), (P, L))
    asf = lambda x: np.ascontiguousarray(x, dtype=f4)
    pos = np.arange(16)
    invc = np.stack([1.0 / np.minimum(pos + 1, win) for win in (2, 4, 8, 16)])
    return dict(zt=asf(zt), qtab=asf(qtab), kcos=asf(kcos), ksin=asf(ksin), dft=asf(fwd.reshape(4, P, 8 * P)),
                idft=asf(inv_t.reshape(P, 8, L)), tvec=asf(tvec)), asf(-t.reshape(4, P).T), asf(
                    np.broadcast_to(invc.reshape(1, 64), (P, 64)))


def tiles(w):
    k, n = w.shape
    return w.reshape(k // P, P, n // P, P).transpose(2, 1, 0, 3).reshape(n // P, P, k)


def cols(v):
    return v.reshape(-1, P).T


def lay_out(x):
    g = {}
    g["x"] = x["x"][0].T.reshape(KD, P, L).transpose(1, 0, 2)
    g["ctx"] = x["ctx"][0].T.reshape(KD, P, LC).transpose(1, 0, 2)
    g["c"] = x["c"].reshape(D)
    g["cc"] = x["c_ctx"].reshape(D)
    g["modw"] = x["mod_w"].transpose(0, 2, 1).reshape(96, P, D)
    g["wdq"] = tiles(x["mla_w_dq"][0])
    dkv = x["mla_w_dkv"][0]
    q = ROPE // 4
    perm = np.concatenate([np.arange(q, 2 * q), np.arange(q), np.arange(3 * q, 4 * q), np.arange(2 * q, 3 * q)])
    kr = dkv[:, KVL:]
    g["wdkv"] = tiles(np.concatenate([dkv[:, :KVL], kr, kr, kr[:, perm], kr[:, perm]], axis=1))
    g["wuv"] = x["mla_w_uv"][0].reshape(2, P, 2, 512).transpose(2, 1, 0, 3).reshape(2, P, 1024)
    uq = x["mla_w_uq"][0].reshape(QL, HEADS, NOPE + ROPE)
    uq = np.concatenate([uq, uq[:, :, NOPE:][:, :, perm]], axis=2).reshape(QL, HEADS * P)
    uq = tiles(uq).reshape(HEADS // 2, 2, P, 4 * P).transpose(0, 2, 1, 3).reshape(HEADS // 2, P, 8 * P)
    g["whead"] = np.concatenate([uq, tiles(x["mla_w_uk"][0])], axis=2)
    g["wo"] = tiles(x["mla_w_o"][0])
    for l in range(2):
        up = tiles(x["ffn_w_up"][l])
        g[f"wup{l}"] = up.reshape(2, KF, P, D).transpose(1, 0, 2, 3).reshape(NUP, P, D)
        dn = tiles(x["ffn_w_down"][l])
        g[f"wdn{l}"] = dn.reshape(8, P, 2, 11 * P).transpose(0, 2, 1, 3).reshape(16, P, 11 * P)
    hy = tiles(x["hy_w_in"][0]).reshape(3, KD, P, D)
    g["whin"] = hy[[1, 2, 0]].transpose(1, 0, 2, 3).reshape(24, P, D)
    g["whout"] = tiles(x["hy_w_out"][0])
    g["fw1"], g["fw2"] = x["hy_f_w1"][0], x["hy_f_w2"][0]
    g["fw3"] = x["hy_f_w3"][0].reshape(HID_F, 2, D).transpose(1, 0, 2).reshape(P, D)
    g["fpar"] = np.stack([x["hy_f_b1"][0], x["hy_f_freq1"][0], x["hy_f_b2"][0], x["hy_f_freq2"][0]], axis=1)
    g["decay"] = x["hy_decay"].reshape(D)
    w2 = tiles(x["w_in_2"][0])
    g["win2a"] = np.concatenate([w2[0:4], w2[8:12]])
    za, zb, ga, gb = w2[4:8], w2[12:16], w2[16:24].reshape(4, 2, P, D), w2[24:32].reshape(4, 2, P, D)
    g["win2b"] = np.concatenate([za[:, None], zb[:, None], ga, gb], axis=1).reshape(24, P, D)
    g["wglu"] = tiles(x["ssm_w_glu_2"][0])
    g["wpool"] = x["pool_w_2"][0].transpose(1, 0, 2).reshape(1, P, 4 * P)
    g["wbr"] = np.concatenate([tiles(x["w_branch_a_2"][0]), tiles(x["w_branch_b_2"][0])], axis=2)
    g["wout2"] = tiles(x["w_out_2"][0])
    b = [x[n].reshape(NM, P, GC) for n in ("ssm_b_re_2", "ssm_b_im_2")]
    c = [x[n].reshape(NM, 2, GC, ST).transpose(0, 1, 3, 2).reshape(NM, P, GC) for n in ("ssm_c_re_2", "ssm_c_im_2")]
    g["s5bc"] = np.stack(b + c).transpose(2, 0, 1, 3)
    consts, tcol, invc = constants()
    g.update(consts)
    packed = dict(
        modb=cols(x["mod_b"]), gmix=cols(x["norm_mix_g"]), gffn=cols(x["norm_ffn_g"]), gq=cols(x["mla_g_q"]),
        gkv=cols(x["mla_g_kv"]), hbin=cols(x["hy_b_in"]), hcw=cols(x["hy_conv_w"]), hcb=cols(x["hy_conv_b"]),
        hdb=cols(x["hy_d_bias"]), hbo=cols(x["hy_b_out"]), fcw=cols(x["ffn_conv_w"]), fcb=cols(x["ffn_conv_b"]),
        gfin=cols(x["final_g"]), g2=cols(x["norm_g_2"]), bin2=cols(x["b_in_2"]), sd=cols(x["ssm_d_2"]),
        bglu=cols(x["ssm_b_glu_2"]), pscale=cols(x["pool_scale_2"]), gfin2=cols(x["final_norm_g_2"]),
        logdt=cols(np.repeat(x["ssm_log_dt_2"].reshape(GROUPS, 1), ST, axis=1)), lre=cols(x["ssm_lam_re_2"]),
        lim=cols(x["ssm_lam_im_2"]), tcol=tcol, invc=invc)
    g["par"] = np.concatenate([packed[n] for n, _ in PARAMS], axis=1)
    return {n: np.ascontiguousarray(v) for n, v in g.items()}


def kernel(**inputs):
    import concourse.bacc as bacc
    from concourse.bass_utils import run_bass_kernel_spmd

    nc = bacc.Bacc("TRN2", target_bir_lowering=False, num_devices=1)
    arrays = lay_out({n: np.asarray(v) for n, v in inputs.items()})
    aps = {n: nc.dram_tensor(f"in_{n}", v.shape, F32, kind="ExternalInput").ap() for n, v in arrays.items()}
    aps["out"] = nc.dram_tensor("out_y", (P, KD, L), F32, kind="ExternalOutput").ap()
    build(nc, aps)
    r = run_bass_kernel_spmd(nc, [{f"in_{n}": v for n, v in arrays.items()}], core_ids=[0])
    y = r.results[0]["out_y"]
    return y.transpose(1, 0, 2).reshape(D, L).T[None]
```

```python
import math
from contextlib import ExitStack, contextmanager

import numpy as np
import concourse.bass as bass
from concourse import mybir

F32 = mybir.dt.float32
F32R = mybir.dt.float32r
ALU = mybir.AluOpType
ACT = mybir.ActivationFunctionType
AX = mybir.AxisListType
ds = bass.ds

P = 128
D = 1024
L = 512
LC = 256
LK = L + LC
KD = D // P
HEADS = 16
NOPE, ROPE, VH = 64, 32, 64
QL, KVL = 512, 256
DFF = 2816
KF = DFF // P
NUP = 2 * KF
GROUPS, GC, ST = 32, 16, 64
NM = GROUPS * ST // P
EPS = 1e-6
GRID_W = 64
HY_BANDS = 16
HID_F = 64
ROUND = 1.5 * 2.0 ** 23
TWO_PI = 2.0 * math.pi
PI_A = 6.28125
PI_B = 1.93500518798828125e-3
PI_C = TWO_PI - PI_A - PI_B
LN2_A = 0.693359375
LN2_B = math.log(2.0) - LN2_A
SLOT = 11 * P

STAGES = [("dq", 4, 8), ("kv", 3, 8), ("uv", 2, 8), ("heads", 8, 10), ("wo", 8, 8), ("up0", 44, 8),
          ("down0", 16, 11), ("hyin", 24, 8), ("dft", 8, 8), ("hyout", 8, 8), ("up1", 44, 8),
          ("down1", 16, 11), ("in2a", 8, 8), ("in2b", 24, 8), ("poolw", 1, 4), ("glu", 4, 4),
          ("branch", 8, 8), ("out2", 8, 8)]
FIRST_TILE, CHUNKS = {}, {}
_t = 0
for _name, _count, _chunks in STAGES:
    FIRST_TILE[_name], CHUNKS[_name] = _t, _chunks
    _t += _count

PARAMS = [("modb", 96), ("gmix", 16), ("gffn", 16), ("gq", 4), ("gkv", 2), ("hbin", 24), ("hcw", 72),
          ("hcb", 24), ("hdb", 8), ("hbo", 8), ("fcw", 2 * 3 * NUP), ("fcb", 2 * NUP), ("gfin", 8),
          ("g2", 8), ("bin2", 32), ("sd", 4), ("bglu", 4), ("pscale", 4), ("gfin2", 8),
          ("logdt", NM), ("lre", NM), ("lim", NM), ("tcol", 4), ("invc", 64)]
COL = {}
_c = 0
for _name, _n in PARAMS:
    COL[_name] = _c
    _c += _n
NPAR = _c


class Tally:

    def __init__(self, sem):
        self.sem, self.n, self.step = sem, 0, 0

    def up(self):
        self.n += 1
        return self.n + self.step


@contextmanager
def repeat(eng, count, *per):
    marks = [(t, k, t.n) for t, k in per]
    with eng.Fori(0, count) as i:
        for t, k, _ in marks:
            t.step = i * k
        yield i
    for t, k, n in marks:
        assert t.n - n == k, (t.n - n, k)
        t.step = 0
        t.n = n + k * count


def build(nc, a):
    with ExitStack() as ctx:
        base = nc.sbuf_base
        base = (base + 63) // 64 * 64
        where = [base]

        def place(name, shape, dt, at=None):
            size = 4 * int(np.prod(shape[1:]))
            off = where[0] if at is None else at
            if at is None:
                where[0] = (off + size + 31) // 32 * 32
            assert off + size <= nc.sbuf_usable_end, (name, off + size - nc.sbuf_usable_end)
            return nc.alloc_sbuf_tensor_at(name, shape, dt, offset=off)

        def sem(name):
            return ctx.enter_context(nc.semaphore(name))

        X = place("X", [P, KD, L], F32)
        HH = place("HH", [P, KD, L], F32R)
        HL = place("HL", [P, KD, L], F32R)
        RAW = [place(f"RAW{i}", [P, SLOT], F32) for i in range(2)]
        WH = [place(f"WH{i}", [P, SLOT], F32R) for i in range(2)]
        WL = [place(f"WL{i}", [P, SLOT], F32R) for i in range(2)]
        PAR = place("PAR", [P, NPAR], F32)
        MOD = place("MOD", [P, 96], F32)
        MODC = place("MODC", [P, 16], F32)
        SC = place("SC", [P, 128], F32)
        NMX = SC[:, 64:72]
        MACC = SC[:, 72:88]
        SUMS = SC[:, 88:96]
        RSUM = SC[:, 16:24]
        AB = place("AB", [P, 4, KD], F32)
        ONES = place("ONES", [P, P], F32)
        IDENT = place("IDENT", [P, P], F32)
        H2T = place("H2T", [P, L], F32)
        big = where[0]

        class Region:

            def __init__(self, at=None):
                self.at = big if at is None else at

            def put(self, name, shape, dt=F32):
                t = place(name, shape, dt, at=self.at)
                self.at = (self.at + 4 * int(np.prod(shape[1:])) + 31) // 32 * 32
                return t

        r = Region()
        V = r.put("V", [P, 6, HEADS * VH])
        p_at = r.at
        PR = [r.put(f"PR{i}", [P, 4, LK]) for i in range(2)]
        pt_at = r.at
        PT = r.put("PT", [P, 6, L])
        KP = [r.put(f"KP{i}", [P, LK]) for i in range(2)]
        Q = [r.put(f"Q{i}", [P, L]) for i in range(2)]
        QTAB = r.put("QTAB", [P, L])
        CKH = r.put("CKH", [P, 2, LK], F32R)
        CKL = r.put("CKL", [P, 2, LK], F32R)
        CQH = r.put("CQH", [P, 4, L], F32R)
        CQL = r.put("CQL", [P, 4, L], F32R)
        MF = [Region(r.at - 4 * 8 * L + 4 * D * i).put(f"MF{i}", [P, D]) for i in range(4)]
        MX = [Region(r.at - 4 * 8 * L - 4 * 4 * LK + 4 * D * i).put(f"MX{i}", [P, D]) for i in range(3)]
        MR = [r.put(f"MR{i}", [P, D]) for i in range(2)]
        CB = r.put("CB", [P, D])
        VC = r.put("VC", [P, 6, P])
        DG = [r.put(f"DG{i}", [P, 4, P]) for i in range(2)]
        r = Region(p_at)
        CTX = r.put("CTX", [P, KD, LC])
        hc_at = r.at
        HCH = r.put("HCH", [P, KD, LC], F32R)
        HCL = r.put("HCL", [P, KD, LC], F32R)
        KCOS = r.put("KCOS", [P // 2, L])
        KSIN = r.put("KSIN", [P, L])
        cc_at = r.at
        CCB = r.put("CCB", [P, D])
        CK32 = Region(cc_at).put("CK32", [P, 2, LK])
        XSQ = Region(hc_at).put("XSQ", [P, KD, L])
        r = Region()
        TA = [r.put(f"TA{i}", [P, L]) for i in range(2)]
        TB = [r.put(f"TB{i}", [P, L]) for i in range(2)]
        C32 = r.put("C32", [P, 4, L])
        SSQA = r.put("SSQA", [P, LK])
        RTA = r.put("RTA", [P, LK])
        K1 = r.put("K1", [P, L])
        r = Region(pt_at + 4 * 6 * L)
        ZT = r.put("ZT", [2 * HY_BANDS + 1, L])
        FW1 = r.put("FW1", [2 * HY_BANDS + 1, HID_F])
        FW2 = r.put("FW2", [HID_F, HID_F])
        FPAR = r.put("FPAR", [HID_F, 4])
        FA = r.put("FA", [HID_F, L])
        FK = r.put("FK", [HID_F, L])

        r = Region()
        HIDH = r.put("HIDH", [P, KF, L], F32R)
        HIDL = r.put("HIDL", [P, KF, L], F32R)
        ZA = r.put("ZA", [P, L])
        ZG = r.put("ZG", [P, L])
        HID = r.put("HID", [P, L])
        t_at = r.at
        SSQ = r.put("SSQ", [P, L])
        RT = r.put("RT", [P, L])
        TN = [r.put(f"TN{i}", [P, L]) for i in range(2)]
        TM = [r.put(f"TM{i}", [P, L]) for i in range(2)]
        SQ = [r.put(f"SQ{i}", [P, L]) for i in range(2)]
        top = r.at

        r = Region()
        VP = r.put("VP", [P, KD, L])
        X1 = r.put("X1", [P, KD, L])
        pq_at = r.at
        UTH = r.put("UTH", [P, 4, 512], F32R)
        UTL = r.put("UTL", [P, 4, 512], F32R)
        PH = r.put("PH", [P, 4, 512], F32R)
        PL = r.put("PL", [P, 4, 512], F32R)
        QH = r.put("QH", [P, 4, 512], F32R)
        QLO = r.put("QLO", [P, 4, 512], F32R)
        Z = r.put("Z", [P, 8, 512])
        DT = [r.put(f"DT{i}", [P, 512]) for i in range(4)]
        WN, TF, TG, TP = DT
        r = Region(pq_at)
        PB = [r.put(f"PB{i}", [P, L]) for i in range(2)]
        ZX = r.put("ZX", [P, L])
        ZV = r.put("ZV", [P, L])
        hl_at = base + 4 * KD * L * 2
        r = Region(hl_at)
        G = r.put("G", [P, 8, L])
        r = Region(top)
        FW3 = r.put("FW3", [P, D])
        ADEC = r.put("ADEC", [P, D])
        H2C = r.put("H2C", [P, P])

        r = Region()
        UA = r.put("UA", [P, 4, L])
        z2_at = r.at
        ZAB = r.put("ZAB", [P, 8, L])
        SA = [r.put(f"SA{i}", [P, L]) for i in range(9)]
        GAB = r.put("GAB", [P, 16, L])
        PAD = 16
        ub_at = r.at
        UB = r.put("UB", [P, 4, PAD + L])
        BT = r.put("BT", [P, 2, 4, P])
        CBD = r.put("CBD", [P, NM, 2, 2 * GC])
        CH = r.put("CH", [P, L])
        BTC = r.put("BTC", [P, 2, P])
        assert r.at <= t_at
        r = Region(top)
        PLL = r.put("PLL", [P, 4, L], F32R)
        SL = r.put("SL", [P, 4, NM + 2])
        CC = r.put("CC", [P, 4, 2, 2 * GC])
        HBG = SC[:, 120:124]
        UAC = H2T
        PLH = Region(ub_at).put("PLH", [P, 4, L], F32R)
        COS = SA[0:2]
        SIN, PHA, PHB, T1, T2, T3, SRE = SA[2:9]
        SIM, TVEC = SSQ, RT
        PRD = [TN[0], TN[1], TM[0], TM[1]]
        AH = SQ[0]
        SH = SQ[1]
        TY, TS = SA[5:7], SA[7:9]
        r = Region(z2_at)
        SBC = r.put("SBC", [P, 4, NM, GC])
        S5 = r.put("S5", [P, 20, NM])
        BBD = r.put("BBD", [P, 2, NM, 2 * GC])
        PBUF = [r.put(f"PBUF{i}", [P, PAD + L]) for i in range(2)]
        r = Region()
        MH = r.put("MH", [P, KD, L], F32R)
        ML = r.put("ML", [P, KD, L], F32R)

        PS = ctx.enter_context(nc.psum_tensor("PS", [P, 8, 512], F32))

        def bank(n, w=512):
            return PS[:, n, 0:w]

        def par(name, k=0, n=1):
            return PAR[:, COL[name] + k:COL[name] + k + n]

        def par_at(name, k):
            return PAR[:, ds(k + COL[name], 1)]

        tile_loaded = [sem(f"tile_loaded{i}") for i in range(2)]
        tile_hi = sem("tile_hi")
        tile_split = sem("tile_split")
        tile_done = sem("tile_done")

        names = """par_in x_in ctx_in c_in cc_in first_in0 first_in1 first_in2 first_in3 mod_in0 mod_in1 tab_in
            filt_in consts silu_c mod_used ctx_mul ctx_sum modx ab ssq stat sqrt nt nh nl xsq fmm fa fsin cq_ev
            cq_sq cq_add radd kv_x ckv_ev krot v_ev proj qready kready vc s_ready smax sexp s_tr pt diag pv ohi
            olo resid rsq hin g_in hev hz vp tapmm tap_read window pq pqh pql tv uth utl dft_h hcopy zd inv iev
            yhi ylo h2c za zc silu hid hidh hidl s5_in tvec_in s5a s5d bbd bt_mm bt_ev cbd p2ev pool plh pll uac
            ccp bmm burd gv ph tr sn prd srd cmm yev gel yh yl pmm ybf ybh ybl sg yaf yah yal amm mev mrg mh ml
            fin oready dchain achain pchain out_done""".split()
        S = {n: sem("s_" + n) for n in names}

        BY_POOL = (0, 2, 4, 6, 8, 10, 12, 13)

        FROM_ONE = "pt s_tr pv hid bmm cmm yev prd ml".split()

        NORMS = ["x0", "ctx", "cq", "ckx", "ckc", "ffn0", "hy", "ffn1", "fin", "n2", "fin2"]
        NTILES = dict(x0=8, ctx=8, cq=4, ckx=2, ckc=2, ffn0=8, hy=8, ffn1=8, fin=0, n2=8, fin2=0)
        NINDEX = {n: k for k, n in enumerate(NORMS)}
        NBASE, _n = {}, 0
        for n in NORMS:
            NBASE[n] = _n
            _n += NTILES[n]
        GAIN = dict(x0=lambda k: (AB[:, 0, k:k + 1], AB[:, 1, k:k + 1]),
                    ctx=lambda k: (AB[:, 2, k:k + 1], AB[:, 3, k:k + 1]),
                    cq=lambda k: (par("gq", k), None), ckx=lambda k: (par("gkv", k), None),
                    ckc=lambda k: (par("gkv", k), None))
        for n in ("ffn0", "hy", "ffn1"):
            GAIN[n] = GAIN["x0"]
        GAIN["n2"] = lambda k: (par("g2", k), None)

        OUTS = dict(dq=4, kv=6, uv=12, wo=8, up0=44, down0=8, hyin=24, hyout=8, up1=44, down1=8,
                    in2a=8, in2b=24, poolw=4, glu=4, out2=8)
        OBASE, _n = {}, 0
        for n, k in OUTS.items():
            OBASE[n] = _n
            _n += k

        RBASE = dict(wo=0, down0=8, hyout=16, down1=24, fin=32, out2=40)

        def mod(layer, part, k=0, n=KD):
            at = 48 * layer + KD * part + k
            return MOD[:, at:at + n]

        def wide(b, w):
            return PS[:, b:b + 2, :].rearrange("p a n -> p (a n)")[:, 0:w]


        def sp_hyena(sp, ring):
            sp.dma_start(FW3[:, :], a["fw3"]).then_inc(S["hin"], 16)
            sp.dma_start(ADEC[:, :], a["decay"].partition_broadcast(P)).then_inc(S["hin"], 16)
            with sp.Fori(0, 4) as i:
                for j in range(6):
                    ring("hyin", a["whin"], j, i, 6)
            for j in range(2):
                ring_at(sp, "dft", a["dft"][j:j + 1], j)
            sp.wait_ge(tile_done, FIRST_TILE["hyin"] + 24)
            sp.dma_start(G[:, :, :], a["idft"]).then_inc(S["g_in"], 16)
            for j in range(2, 8):
                ring_at(sp, "dft", a["dft"][j % 4:j % 4 + 1], j)
            with sp.Fori(0, 4) as i:
                for j in range(2):
                    ring("hyout", a["whout"], j, i, 2)

        def ring_at(sp, stage, src, j):
            t = FIRST_TILE[stage] + j
            sp.wait_ge(tile_split, t - 1)
            sp.dma_start(RAW[t % 2][:, 0:CHUNKS[stage] * P], src.rearrange("a p n -> p (a n)")
                         ).then_inc(tile_loaded[t % 2], 16)

        def pool_hyena(pool, split):
            with pool.Fori(0, 4) as i:
                for j in range(6):
                    split("hyin", j, i, 6)
            for st in ("dft", "hyout"):
                with pool.Fori(0, 4) as i:
                    for j in range(2):
                        split(st, j, i, 2)

        def pe_hyena(pe, linear, first_two, stat, mm3, chunk):
            def taps(c, n):
                pe.wait_ge(S["h2c"], n + 1)
                if not (isinstance(n, int) and n == 0):
                    pe.wait_ge(S["tap_read"], n)
                for half in range(2):
                    r = slice(HID_F * half, HID_F * half + HID_F)
                    m = pe.matmul(bank(4 + half), H2C[r, :], FW3[r, 512 * c:512 * c + 512],
                                  start=True, stop=True)
                m.then_inc(S["tapmm"], 1)

            def turn_values(c, tt):
                n = 4 * c + tt
                if n >= 2:
                    pe.wait_ge(S["utl"], n - 1)
                for ct in range(4):
                    m = pe.transpose(PS[:, 6 + tt % 2, ct * P:(ct + 1) * P],
                                     VP[:, 4 * c + ct, tt * P:(tt + 1) * P], IDENT[:, :])
                m.then_inc(S["tv"], 1)

            def spectra(c, f):
                n = 4 * c + f
                t = FIRST_TILE["dft"] + n
                b = 4 * ((f + 1) % 2)
                pe.wait_ge(tile_split, t + 1)
                if n >= 2:
                    pe.wait_ge(S["zd"], n - 1)
                for part, (xh, xl) in ((2, (PH, PL)), (3, (QH, QLO)), (0, (UTH, UTL)), (1, (UTH, UTL))):
                    for k in range(4):
                        m = mm3(bank(b + part), *chunk(t % 2, 4 * (part % 2) + k), xh[:, k, :], xl[:, k, :],
                                k == 0, k == 3)
                    if part == 3:
                        m.then_inc(S["dft_h"], 1)
                m.then_inc(tile_done, 1)

            def back(c, ct):
                n = 4 * c + ct
                if n >= 2:
                    pe.wait_ge(S["iev"], n - 1)
                for k in range(8):
                    m = pe.matmul(bank(ct % 2), Z[:, k, ct * P:(ct + 1) * P], G[:, k, :],
                                  start=k == 0, stop=k == 7)
                m.then_inc(S["inv"], 1)

            stat("hy", SSQ)
            first_two("hyin", "hy")
            for j in range(2, 6):
                linear("hyin", j, HH, HL, (S["hev"], 0))
                if j == 2:
                    pe.wait_ge(S["hin"], 32)
                    taps(0, 0)
            with pe.Fori(0, 3) as i:
                for j in range(6):
                    linear("hyin", 6 + j, HH, HL, (S["hev"], 0), i, 6)
                    if j == 2:
                        taps(0, i + 1)
            pe.wait_ge(S["vp"], 8)
            for tt in range(4):
                turn_values(0, tt)
            pe.wait_ge(S["utl"], 4)
            pe.wait_ge(S["pql"], 4)
            for f in range(4):
                spectra(0, f)
            pe.wait_ge(S["zd"], 3)
            for k in range(4):
                taps(1, 4 + k)
                turn_values(1, k)
                if k == 0:
                    pe.wait_ge(S["zd"], 4)
                    pe.wait_ge(S["g_in"], 16)
                back(0, k)
            pe.wait_ge(S["utl"], 8)
            pe.wait_ge(S["pql"], 8)
            for f in range(4):
                if f == 1:
                    pe.wait_ge(S["iev"], 4)
                spectra(1, f)
            pe.wait_ge(S["zd"], 8)
            for k in range(4):
                back(1, k)
            pe.wait_ge(S["iev"], 8)
            pe.wait_ge(S["ylo"], 8)
            for j in range(2):
                linear("hyout", j, HH, HL, (S["resid"], 16))
            with pe.Fori(0, 3) as i:
                for j in range(2):
                    linear("hyout", 2 + j, HH, HL, (S["resid"], 16), i, 2)

        def act_hyena(act, norm, squares, load_table):
            def window(n, c, tt, i=0):
                act.wait_ge(S["tap_read"], n)
                act.activation(WN[:, :], ADEC[:, 512 * c:512 * c + 512], ACT.Exp,
                               scale=par_at("tcol", tt)).then_inc(S["window"], 1)
                act.wait_ge(S["pq"], n + 1)
                act.copy(PH[:, ds(tt, 1), :].rearrange("p a n -> p (a n)"), TP[:, :]).then_inc(S["pqh"], 1)
                act.copy(QH[:, ds(tt, 1), :].rearrange("p a n -> p (a n)"), TF[:, :]).then_inc(S["pqh"], 1)

            def taken(j, i=0):
                jj, kind = j // 3, j % 3
                act.wait_ge(tile_done, i * 6 + (FIRST_TILE["hyin"] + j + 1))
                if j >= 2:
                    act.wait_ge(S["hz"], i * 6 + (j - 1))
                act.activation(PB[j % 2][:, :], bank((OBASE["hyin"] + j) % 2), ACT.Identity,
                               bias=par_at("hbin", i * 2 + ((8, 16, 0)[kind] + jj)), scale=1.0
                               ).then_inc(S["hev"], 1)

            def values_hi(c, tt):
                act.wait_ge(S["tv"], 4 * c + tt + 1)
                act.copy(UTH[:, tt, :], bank(6 + tt % 2)).then_inc(S["uth"], 1)

            act.wait_ge(S["ab"], 3)
            norm("hy", HH, L, D, RT, TN, TM)
            act.wait_ge(S["nl"], NBASE["hy"] + 8)
            act.wait_ge(S["hin"], 32)
            act.activation(ADEC[:, :], ADEC[:, :], ACT.Abs).then_inc(S["achain"], 1)
            act.wait_ge(S["achain"], 1)
            for j in range(6):
                taken(j)
                if j == 2:
                    window(0, 0, 0)
            with act.Fori(0, 3) as i:
                for j in range(6):
                    taken(6 + j, i)
                    if j == 2:
                        window(i + 1, 0, i + 1)
            act.wait_ge(S["hz"], 24)
            act.wait_ge(S["vp"], 8)
            for tt in range(4):
                values_hi(0, tt)

            def spectrum_copies(c):
                for f in range(4):
                    n = 4 * c + f
                    act.wait_ge(S["dft_h"], n + 1)
                    act.wait_ge(*((S["zd"], n) if n != 0 else (S["pql"], 4)))
                    if n == 4:
                        act.wait_ge(S["pql"], 8)
                    for part in range(2):
                        act.copy(DT[part][:, :], bank(4 * ((f + 1) % 2) + 2 + part)).then_inc(S["hcopy"], 1)

            def y_hi(n):
                act.wait_ge(S["iev"], n + 1)
                act.copy(HH[:, n, :], X1[:, n, :]).then_inc(S["yhi"], 1)

            spectrum_copies(0)
            act.wait_ge(S["zd"], 4)
            for k in range(4):
                window(4 + k, 1, k)
                values_hi(1, k)
                y_hi(k)
            spectrum_copies(1)
            for k in range(4, 8):
                y_hi(k)
            load_table(ACT.Sqrt)
            for j in range(2):
                squares("hyout", j)
            with act.Fori(0, 3) as i:
                for j in range(2):
                    squares("hyout", 2 + j, i, 2)

        def dve_hyena(dve, norm, link, own, columns, sums_ready, add_squares):
            def filter_time(n, tt):
                if not (isinstance(n, int) and n == 0):
                    dve.wait_ge(S["tapmm"], n)
                dve.tensor_copy(H2C[:, :], H2T[:, ds(tt * P, P)]).then_inc(S["h2c"], 1)

            def taps(n, tt, first):
                dve.wait_ge(S["window"], n + 1)
                dve.wait_ge(S["tapmm"], n + 1)
                link(dve.tensor_tensor(TF[:, :], bank(4), WN[:, :], ALU.mult))
                dve.tensor_tensor(TG[:, :], bank(5), WN[:, :], ALU.mult).then_inc(S["tap_read"], 1)
                dve.wait_ge(S["tap_read"], n + 1)
                if first:
                    link(dve.memset(TG[0:1, :], 0.0))
                link(dve.tensor_tensor(TP[:, :], TF[:, :], TG[:, :], ALU.add))
                dve.tensor_tensor(TF[:, :], TF[:, :], TG[:, :], ALU.subtract).then_inc(S["pq"], 1)
                at = (slice(None), ds(tt, 1), slice(None))
                for k, (src, h, lo) in enumerate(((TP, PH, PL), (TF, QH, QLO))):
                    dve.wait_ge(S["pqh"], n * 2 + (k + 1))
                    dve.tensor_tensor(lo[at].rearrange("p a n -> p (a n)"), src[:, :],
                                      h[at].rearrange("p a n -> p (a n)").bitcast(F32), ALU.subtract
                                      ).then_inc(*((S["pql"], 1) if k else (S["dchain"], 1)))
                    if k == 0:
                        own.up()

            def short_conv(j, i=0):
                jj, kind = j // 3, j % 3
                col = i * 2 + ((8, 16, 0)[kind] + jj)
                x1 = X1[:, ds(i * 2 + jj, 1), :].rearrange("p a n -> p (a n)")
                z = (ZX[:, :], ZV[:, :], x1)[kind]
                pb = PB[j % 2]
                dve.wait_ge(S["hev"], i * 6 + (j + 1))
                link(dve.tensor_scalar(z, pb[:, :], par_at("hcw", col + 24), par_at("hcb", col), ALU.mult, ALU.add))
                link(dve.scalar_tensor_tensor(z[:, 1:L], pb[:, 0:L - 1], par_at("hcw", col), z[:, 1:L],
                                              ALU.mult, ALU.add))
                dve.scalar_tensor_tensor(z[:, 0:L - 1], pb[:, 1:L], par_at("hcw", col + 48), z[:, 0:L - 1],
                                         ALU.mult, ALU.add).then_inc(S["hz"], 1)
                if kind == 1:
                    dve.wait_ge(S["hz"], i * 6 + (j + 1))
                    dve.tensor_tensor(VP[:, ds(i * 2 + jj, 1), :].rearrange("p a n -> p (a n)"), ZV[:, :],
                                      ZX[:, :], ALU.mult).then_inc(S["vp"], 1)

            def values_lo(c, tt):
                dve.wait_ge(S["uth"], 4 * c + tt + 1)
                dve.tensor_tensor(UTL[:, tt, :], bank(6 + tt % 2), UTH[:, tt, :].bitcast(F32), ALU.subtract
                                  ).then_inc(S["utl"], 1)

            def product(c, f):
                n = 4 * c + f
                b = 4 * ((f + 1) % 2)
                dve.wait_ge(S["hcopy"], 2 * n + 2)
                dve.wait_ge(tile_done, FIRST_TILE["dft"] + n + 1)
                link(dve.tensor_tensor(DT[2][:, :], bank(b), DT[0][:, :], ALU.mult))
                link(dve.tensor_tensor(DT[3][:, :], bank(b + 1), DT[1][:, :], ALU.mult))
                link(dve.tensor_tensor(Z[:, f, :], DT[2][:, :], DT[3][:, :], ALU.subtract))
                link(dve.tensor_tensor(DT[2][:, :], bank(b), DT[1][:, :], ALU.mult))
                link(dve.tensor_tensor(DT[3][:, :], bank(b + 1), DT[0][:, :], ALU.mult))
                dve.tensor_tensor(Z[:, 4 + f, :], DT[2][:, :], DT[3][:, :], ALU.add).then_inc(S["zd"], 1)

            def gated(n):
                dve.wait_ge(S["inv"], n + 1)
                link(dve.scalar_tensor_tensor(VP[:, n, :], VP[:, n, :], par("hdb", n), bank(n % 2),
                                              ALU.mult, ALU.add))
                dve.tensor_tensor(X1[:, n, :], VP[:, n, :], X1[:, n, :], ALU.mult).then_inc(S["iev"], 1)

            def out(j, i=0, per=0):
                xt = X[:, ds(i * per + j, 1), :].rearrange("p a n -> p (a n)")
                dve.wait_ge(tile_done, i * per + (FIRST_TILE["hyout"] + j + 1))
                link(dve.tensor_scalar(TN[j % 2][:, :], bank((OBASE["hyout"] + j) % 2),
                                       par_at("hbo", i * per + j), MOD[:, ds(i * per + (48 + 16 + j), 1)],
                                       ALU.add, ALU.mult))
                dve.tensor_tensor(xt, xt, TN[j % 2][:, :], ALU.add).then_inc(S["resid"], 1)
                add_squares(16 + j, j, i, per)

            dve.wait_ge(S["fsin"], 3)
            filter_time(0, 0)
            norm("hy", X, HH, HL, L, RT, TN, TM)
            for j in range(6):
                short_conv(j)
                if j == 2:
                    taps(0, 0, True)
            with repeat(dve, 3, (own, 15)) as i:
                filter_time(i + 1, i + 1)
                for j in range(6):
                    short_conv(6 + j, i)
                    if j == 2:
                        taps(i + 1, i + 1, False)
            filter_time(4, 0)
            for tt in range(4):
                values_lo(0, tt)
            for f in range(4):
                product(0, f)
            for k in range(4):
                taps(4 + k, k, k == 0)
                if k < 3:
                    filter_time(5 + k, k + 1)
                values_lo(1, k)
                gated(k)
            for f in range(4):
                product(1, f)
            for k in range(4, 8):
                gated(k)
            dve.wait_ge(S["inv"], 8)
            for n in range(8):
                dve.wait_ge(S["yhi"], n + 1)
                dve.tensor_tensor(HL[:, n, :], X1[:, n, :], HH[:, n, :].bitcast(F32), ALU.subtract
                                  ).then_inc(S["ylo"], 1)
            link(dve.memset(SSQ[:, :], 0.0))
            for j in range(2):
                out(j)
            with repeat(dve, 3, (own, 2)) as i:
                for j in range(2):
                    out(2 + j, i, 2)
            dve.wait_ge(S["radd"], 24)
            sums_ready()
            columns(1, False)


        def sp_second(sp, ring):
            ring("in2a", a["win2a"], 0)
            ring("in2a", a["win2a"], 1)
            sp.wait_ge(tile_done, FIRST_TILE["in2a"])
            sp.dma_start(SBC[:, :, :, :], a["s5bc"]).then_inc(S["s5_in"], 16)
            sp.wait_ge(S["nl"], NBASE["n2"] + 8)
            sp.dma_start(TVEC[:, :], a["tvec"]).then_inc(S["tvec_in"], 16)
            for j in range(2, 8):
                ring("in2a", a["win2a"], j)
            with sp.Fori(0, 4) as i:
                for j in range(6):
                    ring("in2b", a["win2b"], j, i, 6)
            ring("poolw", a["wpool"], 0)
            for j in range(4):
                ring("glu", a["wglu"], j)
            for st, w in (("branch", "wbr"), ("out2", "wout2")):
                with sp.Fori(0, 4) as i:
                    for j in range(2):
                        ring(st, a[w], j, i, 2)

        def pool_second(pool, split):
            for j in range(8):
                split("in2a", j)
            with pool.Fori(0, 4) as i:
                def states(mm):
                    for part in range(2):
                        pool.wait_ge(S["prd"], i * 16 + (4 * mm + 2 * part + 2) + 1)
                        pool.tensor_tensor(PRD[2 * part][:, :], PRD[2 * part][:, :], PRD[2 * part + 1][:, :],
                                           ALU.add).then_inc(S["srd"], 1)

                split("in2b", 0, i, 6)
                split("in2b", 1, i, 6)
                split("in2b", 2, i, 6)
                states(0)
                split("in2b", 3, i, 6)
                states(1)
                split("in2b", 4, i, 6)
                split("in2b", 5, i, 6)
                states(2)
                states(3)
            split("poolw", 0)
            for j in range(4):
                split("glu", j)
            for st in ("branch", "out2"):
                with pool.Fori(0, 4) as i:
                    for j in range(2):
                        split(st, j, i, 2)

        def pe_second(pe, linear, first_two, stat, mm3, chunk):
            stat("fin", SSQ)
            pe.wait_ge(S["sqrt"], NINDEX["fin"] + 1)
            for k in range(KD):
                pe.wait_ge(S["rsq"], RBASE["fin"] + k + 1)
                pe.matmul(bank(7), ONES[:, :], SQ[k % 2][:, :], start=k == 0, stop=k == KD - 1
                          ).then_inc(S["radd"] if k < KD - 1 else S["stat"], 1)
            first_two("in2a", "n2")
            for j in range(2, 8):
                linear("in2a", j, HH, HL, (S["p2ev"], 0))
                if j == 5:
                    pe.wait_ge(S["bbd"], 1)
                    for part in range(2):
                        for q in range(4):
                            m = pe.transpose(PS[:, 2 + part, q * P:(q + 1) * P],
                                             BBD[:, part, 4 * q:4 * q + 4, :].rearrange("p m c -> p (m c)"),
                                             IDENT[:, :])
                    m.then_inc(S["bt_mm"], 1)
            pe.wait_ge(S["bt_ev"], 2)
            def scan_turn(i, last):
                def drive(mm, i=i):
                    pe.wait_ge(S["burd"], i * 4 + (mm + 1))
                    r = slice(32 * mm, 32 * mm + 32)
                    for part in range(2):
                        m = pe.matmul(bank(2 + 2 * (mm % 2) + part), BTC[r, part, :], UAC[r, :],
                                      start=True, stop=True)
                    m.then_inc(S["bmm"], 1)

                def read_out(mm):
                    for part in range(2):
                        pe.wait_ge(S["srd"], i * 8 + (2 * mm + part + 1))
                        m = pe.matmul(PS[32 * mm:32 * mm + 32, 6, :], CC[:, mm, part, :], PRD[2 * part][:, :],
                                      start=part == 0, stop=part == 1)
                    m.then_inc(S["cmm"], 1)

                def gate(j):
                    linear("in2b", j, HH, HL, (S["p2ev"], 8), i, 6)

                if isinstance(i, int) and i < 0:
                    pe.wait_ge(S["uac"], 2)
                    drive(0, 0)
                    drive(1, 0)
                    return
                gate(0)
                gate(1)
                pe.wait_ge(S["ccp"], i + 1)
                pe.wait_ge(S["yev"], i + 1)
                read_out(0)
                drive(2)
                gate(2)
                read_out(1)
                drive(3)
                gate(3)
                gate(4)
                read_out(2)
                gate(5)
                if not last:
                    pe.wait_ge(S["uac"], i * 2 + 4)
                    drive(0, i + 1)
                read_out(3)
                if not last:
                    drive(1, i + 1)

            scan_turn(-1, False)
            with pe.Fori(0, 3) as i:
                scan_turn(i, False)
            scan_turn(3, True)
            t = FIRST_TILE["poolw"]
            pe.wait_ge(tile_split, t + 1)
            pe.wait_ge(S["pll"], 4)
            for g in range(4):
                pe.wait_ge(*((S["p2ev"], 31 + g) if g < 2 else (S["ybf"], g - 1)))
                m = mm3(bank((OBASE["poolw"] + g) % 2), *chunk(t % 2, g), PLH[:, g, :], PLL[:, g, :], True, True)
                m.then_inc(*((S["pmm"], 1) if g < 3 else (tile_done, 1)))
            pe.wait_ge(S["yl"], 4)
            for j in range(4):
                if j < 2:
                    pe.wait_ge(S["ybf"], 3 + j)
                linear("glu", j, HH[:, 4:8, :], HL[:, 4:8, :], (S["sg"], 0), kn=4)

            def branches(j, i=0, per=0):
                t = FIRST_TILE["branch"] + j
                pe.wait_ge(tile_split, i * per + (t + 1))
                if per:
                    pe.wait_ge(S["mev"], i * per + (j - 1))
                for c, (h, lo) in enumerate(((HH, HL), (PLH, PLL))):
                    for k in range(4):
                        m = mm3(bank(2 * (j % 2) + c), *chunk(t % 2, 4 * c + k), h[:, k, :], lo[:, k, :],
                                k == 0, k == 3)
                    m.then_inc(*((tile_done, 1) if c else (S["amm"], 1)))

            pe.wait_ge(S["ybl"], 4)
            pe.wait_ge(S["yal"], 4)
            for j in range(2):
                branches(j)
            with pe.Fori(0, 3) as i:
                for j in range(2):
                    branches(2 + j, i, 2)
            pe.wait_ge(S["ml"], 8 + 1)
            for j in range(2):
                linear("out2", j, MH, ML, (S["resid"], RBASE["out2"]))
            with pe.Fori(0, 3) as i:
                for j in range(2):
                    linear("out2", 2 + j, MH, ML, (S["resid"], RBASE["out2"]), i, 2)
            stat("fin2", SSQ)

        def s5(k):
            return S5[:, k, :] if k >= 0 else SL[:, k + 4, 0:NM]

        (MAG5, FT5, FH5, FL5, Z5, AN5, K5, R5, SN5, HS5, E5, NR5, NI5, DEN5, CR5, CI5, TMP5, DT5
         ) = range(-4, 14)
        HB = SC[:, 104:120]

        def act_second(act, norm, squares, load_table):
            act.wait_ge(S["stat"], NINDEX["fin"] + 1)
            act.activation(RT[:, :], bank(7), ACT.Sqrt, bias=SC[:, 0:1], scale=1.0 / D).then_inc(S["sqrt"], 1)
            with act.Fori(0, 4) as i:
                for j in range(2):
                    squares("fin", j, i, 2)
            norm("n2", HH, L, D, RT, TN, TM)
            act.wait_ge(S["s5d"], 1)
            act.activation(s5(SN5), s5(AN5), ACT.Sin).then_inc(S["s5a"], 1)
            act.activation(s5(HS5), s5(AN5), ACT.Sin, scale=0.5).then_inc(S["s5a"], 1)

            def waves(mm, i=0):
                def n(k):
                    return i * 16 + (4 * mm + k)
                act.wait_ge(S["ph"], i * 4 + (mm + 1))
                act.activation(AH[:, :], PHA[:, :], ACT.Abs).then_inc(S["tr"], 1)
                act.wait_ge(S["sn"], i * 4 + mm)
                act.activation(SH[:, :], PHA[:, :], ACT.Sin, scale=math.pi).then_inc(S["tr"], 1)
                act.wait_ge(S["tr"], n(1))
                act.activation(CH[:, :], AH[:, :], ACT.Sin, bias=SC[:, 6:7], scale=-math.pi).then_inc(S["tr"], 1)
                act.activation(COS[mm % 2][:, :], AH[:, :], ACT.Sin, bias=SC[:, 6:7], scale=-TWO_PI
                               ).then_inc(S["tr"], 1)

            def turns(mm, i=0):
                if mm:
                    act.wait_ge(S["tr"], i * 16 + 4 * mm)
                for out, k, kw in ((PHB, FT5, dict(bias=SC[:, 7:8])), (PHA, FH5, {})):
                    act.activation(out[:, :], TVEC[:, :], ACT.Identity, scale=SL[:, k + 4, ds(i * 4 + mm, 1)], **kw
                                   ).then_inc(S["gv"], 1)

            def pooled_hi(g):
                act.wait_ge(S["pool"], g + 1)
                act.copy(PLH[:, g, :], TY[g % 2][:, :]).then_inc(S["plh"], 1)

            for j in range(8):
                if j >= 4:
                    pooled_hi(j - 4)
                if j == 6:
                    act.wait_ge(S["tvec_in"], 16)
                    act.wait_ge(S["bbd"], 1)
                    turns(0)
                if j == 7:
                    waves(0)
                    turns(1)
                act.wait_ge(tile_done, FIRST_TILE["in2a"] + j + 1)
                dst = UB[:, j, PAD:PAD + L] if j < 4 else UA[:, j - 4, :]
                act.activation(dst, bank((OBASE["in2a"] + j) % 2), ACT.Identity,
                               bias=par("bin2", 8 + j if j < 4 else j - 4), scale=1.0).then_inc(S["p2ev"], 1)
                if j == 5:
                    act.wait_ge(S["bt_mm"], 1)
                    for part in range(2):
                        act.copy(BT[:, part, :, :].rearrange("p q n -> p (q n)"), bank(2 + part)
                                 ).then_inc(S["bt_ev"], 1)

            act.wait_ge(S["bt_ev"], 2)
            act.wait_ge(S["pll"], 4)
            act.wait_ge(S["cbd"], 1)
            def copies(i):
                act.wait_ge(S["bmm"], i * 4 + 1)
                act.copy(UAC[:, :], UA[:, ds(i, 1), :].rearrange("p a n -> p (a n)")).then_inc(S["uac"], 1)
                act.copy(BTC[:, :, :], BT[:, :, ds(i, 1), :].rearrange("p a q n -> p a (q n)")
                         ).then_inc(S["uac"], 1)

            def scan_turn(i, last):
                def gate(j):
                    act.wait_ge(tile_done, i * 6 + (FIRST_TILE["in2b"] + j + 1))
                    src = bank((OBASE["in2b"] + j) % 2)
                    if j < 2:
                        act.activation(ZAB[:, ds(i + 4 * j, 1), :].rearrange("p a n -> p (a n)"), src, ACT.Silu,
                                       bias=par_at("bin2", i + (4 + 8 * j)), scale=1.0).then_inc(S["p2ev"], 1)
                    else:
                        k = 8 * (j // 4) + j % 2
                        act.activation(GAB[:, ds(i * 2 + k, 1), :].rearrange("p a n -> p (a n)"), src, ACT.Tanh,
                                       bias=SC[:, ds(i * 2 + (104 + k), 1)], scale=0.5).then_inc(S["p2ev"], 1)

                act.wait_ge(S["cmm"], i * 4 + 1)
                act.copy(CC[:, :, :, :].rearrange("p m a c -> p (m a c)"),
                         CBD[:, ds(i * 4, 4), :, :].rearrange("p m a c -> p (m a c)")).then_inc(S["ccp"], 1)
                waves(1, i)
                turns(2, i)
                gate(0)
                gate(1)
                waves(2, i)
                turns(3, i)
                gate(2)
                waves(3, i)
                turns(4, i)
                gate(3)
                gate(4)
                if not last:
                    copies(i + 1)
                waves(4, i)
                if not last:
                    turns(5, i)
                gate(5)

            copies(0)
            with act.Fori(0, 3) as i:
                scan_turn(i, False)
            scan_turn(3, True)
            act.wait_ge(S["yev"], 4 + 1)
            for k in range(4):
                act.activation(UA[:, k, :], UA[:, k, :], ACT.Gelu_apprx_tanh).then_inc(S["gel"], 1)
            for k in range(4):
                act.wait_ge(S["gel"], k + 1)
                act.copy(HH[:, 4 + k, :], UA[:, k, :]).then_inc(S["yh"], 1)
            for g in range(4):
                act.wait_ge(S["ybf"], g + 1)
                act.copy(PLH[:, g, :], TY[g % 2][:, :]).then_inc(S["ybh"], 1)
            for j in range(4):
                act.wait_ge(tile_done, FIRST_TILE["glu"] + j + 1)
                if j >= 2:
                    act.wait_ge(S["yal"], j - 1)
                act.activation(TS[j % 2][:, :], bank((OBASE["glu"] + j) % 2), ACT.Tanh, bias=HBG[:, j:j + 1],
                               scale=0.5).then_inc(S["sg"], 1)
                if j:
                    act.wait_ge(S["yaf"], j)
                    act.copy(HH[:, j - 1, :], TS[(j - 1) % 2][:, :]).then_inc(S["yah"], 1)
            act.wait_ge(S["yaf"], 4)
            act.copy(HH[:, 3, :], TS[1][:, :]).then_inc(S["yah"], 1)
            with act.Fori(0, 4) as i:
                for j in range(2):
                    act.wait_ge(S["mrg"], i * 2 + (j + 1))
                    act.copy(MH[:, ds(i * 2 + j, 1), :].rearrange("p a n -> p (a n)"), TY[j][:, :]
                             ).then_inc(S["mh"], 1)
            load_table(ACT.Sqrt)
            with act.Fori(0, 4) as i:
                for j in range(2):
                    squares("out2", j, i, 2)
            act.wait_ge(S["stat"], NINDEX["fin2"] + 1)
            act.activation(RT[:, :], bank(7), ACT.Sqrt, bias=SC[:, 0:1], scale=1.0 / D).then_inc(S["sqrt"], 1)

        def dve_second(dve, norm, link, own, reduce_angle, add_squares, sums_ready):
            def tt(out, x, y, op):
                link(dve.tensor_tensor(out, x, y, op))

            def tile_of(t, k):
                return t[:, ds(k, 1), :].rearrange("p a n -> p (a n)")

            dve.wait_ge(S["sqrt"], NINDEX["fin"] + 1)
            link(dve.reciprocal(RT[:, :], RT[:, :]))
            with dve.Fori(0, 4) as i:
                for j in range(2):
                    x = tile_of(X, i * 2 + j)
                    dve.scalar_tensor_tensor(x, x, par_at("gfin", i * 2 + j), RT[:, :], ALU.mult, ALU.mult
                                             ).then_inc(S["resid"], 1)
            dve.wait_ge(S["resid"], RBASE["fin"] + KD)
            sums_ready()
            dve.wait_ge(S["sqrt"], NINDEX["n2"] + 1)
            dve.tensor_copy(SC[:, 10:11], ONES[:, 0:1]).then_inc(S["radd"], 1)
            norm("n2", X, HH, HL, L, RT, TN, TM)

            link(dve.memset(SL[:, :, NM:NM + 2], 0.0))
            link(dve.memset(SC[:, 6:7], math.pi / 2))
            link(dve.memset(SC[:, 7:8], ROUND))
            link(dve.tensor_scalar(HB, par("bin2", 16, 16), 0.5, None, ALU.mult))
            link(dve.tensor_scalar(HBG, par("bglu", 0, 4), 0.5, None, ALU.mult))

            def exp(x, out, less_one=None):
                k, r, q, two_k = s5(K5), s5(R5), s5(TMP5), s5(CR5)
                link(dve.tensor_scalar(r, x, 88.72, -88.03, ALU.min, ALU.max))
                link(dve.tensor_scalar(k, r, 1.0 / math.log(2.0), ROUND, ALU.mult, ALU.add))
                link(dve.tensor_scalar(k, k, ROUND, None, ALU.subtract))
                for part in (LN2_A, LN2_B):
                    link(dve.scalar_tensor_tensor(r, k, -part, r, ALU.mult, ALU.add))
                link(dve.tensor_scalar(q, r, 1.0 / math.factorial(8), None, ALU.mult))
                for n in range(7, 0, -1):
                    link(dve.scalar_tensor_tensor(q, q, 1.0 / math.factorial(n), r, ALU.add, ALU.mult))
                link(dve.tensor_scalar(two_k.bitcast(mybir.dt.int32), k, 127.0, 2.0 ** 23, ALU.add, ALU.mult))
                tt(q, q, two_k, ALU.mult)
                tt(out, q, two_k, ALU.add)
                if less_one is not None:
                    link(dve.scalar_tensor_tensor(less_one, two_k, -1.0, q, ALU.add, ALU.add))

            exp(par("logdt", 0, NM), s5(DT5))
            tt(s5(Z5), par("lre", 0, NM), s5(DT5), ALU.mult)
            tt(s5(AN5), par("lim", 0, NM), s5(DT5), ALU.mult)
            reduce_angle(s5(AN5), s5(K5))
            dve.tensor_scalar(s5(AN5), s5(AN5), math.pi, -math.pi, ALU.min, ALU.max).then_inc(S["s5d"], 1)
            dve.wait_ge(S["s5d"], 1)
            grid = ROUND / 2.0 ** 14
            link(dve.tensor_scalar(s5(FT5), s5(AN5), 1.0 / TWO_PI, None, ALU.mult))
            link(dve.tensor_scalar(s5(FH5), s5(FT5), grid, grid, ALU.add, ALU.subtract))
            link(dve.scalar_tensor_tensor(s5(FL5), s5(FH5), -PI_A, s5(AN5), ALU.mult, ALU.add))
            link(dve.scalar_tensor_tensor(s5(FL5), s5(FH5), -PI_B, s5(FL5), ALU.mult, ALU.add))
            link(dve.scalar_tensor_tensor(s5(FL5), s5(FH5), -PI_C, s5(FL5), ALU.mult, ALU.add))
            link(dve.tensor_scalar(s5(FL5), s5(FL5), 1.0 / TWO_PI, None, ALU.mult))
            exp(s5(Z5), s5(MAG5), s5(E5))
            dve.wait_ge(S["s5a"], 2)
            tt(s5(HS5), s5(HS5), s5(HS5), ALU.mult)
            link(dve.tensor_scalar(s5(HS5), s5(HS5), 2.0, None, ALU.mult))
            link(dve.scalar_tensor_tensor(s5(NR5), s5(E5), 1.0, s5(HS5), ALU.add, ALU.mult))
            tt(s5(NR5), s5(E5), s5(NR5), ALU.subtract)
            tt(s5(NI5), s5(MAG5), s5(SN5), ALU.mult)
            tt(s5(DEN5), par("lre", 0, NM), par("lre", 0, NM), ALU.mult)
            tt(s5(TMP5), par("lim", 0, NM), par("lim", 0, NM), ALU.mult)
            tt(s5(DEN5), s5(DEN5), s5(TMP5), ALU.add)
            link(dve.reciprocal(s5(DEN5), s5(DEN5)))
            for out, p, q, op in ((CR5, NR5, NI5, ALU.add), (CI5, NI5, NR5, ALU.subtract)):
                tt(s5(out), s5(p), par("lre", 0, NM), ALU.mult)
                tt(s5(TMP5), s5(q), par("lim", 0, NM), ALU.mult)
                tt(s5(out), s5(out), s5(TMP5), op)
                tt(s5(out), s5(out), s5(DEN5), ALU.mult)
            link(dve.memset(BBD[:, :, :, :], 0.0))
            link(dve.memset(CBD[:, :, :, :], 0.0))
            dve.wait_ge(S["s5_in"], 16)
            pr = [T[:, 0:NM * GC].rearrange("p (m c) -> p m c", c=GC) for T in (T1, T2)]
            wide_c = [s5(k).unsqueeze(2).to_broadcast([P, NM, GC]) for k in (CR5, CI5)]
            for part, (b0, b1, op) in enumerate(((0, 1, ALU.subtract), (1, 0, ALU.add))):
                tt(pr[0], SBC[:, b0, :, :], wide_c[0], ALU.mult)
                tt(pr[1], SBC[:, b1, :, :], wide_c[1], ALU.mult)
                for g in range(2):
                    r = slice(ST * g, ST * g + ST)
                    ins = dve.tensor_tensor(BBD[r, part, :, GC * g:GC * g + GC], pr[0][r, :, :], pr[1][r, :, :], op)
                    if part and g:
                        ins.then_inc(S["bbd"], 1)
                    else:
                        link(ins)
            for part, sign in ((0, 1.0), (1, -1.0)):
                for g in range(2):
                    r = slice(ST * g, ST * g + ST)
                    ins = dve.tensor_scalar(CBD[r, :, part, GC * g:GC * g + GC], SBC[r, 2 + part, :, :], sign,
                                            None, ALU.mult)
                    if part and g:
                        ins.then_inc(S["cbd"], 1)
                    else:
                        link(ins)
            link(dve.memset(UB[:, :, 0:PAD], 0.0))
            for k in range(2):
                link(dve.memset(PBUF[k][:, 0:PAD], 0.0))

            def phase(mm, i=0):
                def col(k):
                    return SL[:, k + 4, ds(i * 4 + mm, 1)]
                dve.wait_ge(S["gv"], i * 8 + (2 * mm + 2))
                link(dve.scalar_tensor_tensor(PHA[:, :], PHB[:, :], ROUND, PHA[:, :], ALU.subtract, ALU.subtract))
                dve.scalar_tensor_tensor(PHA[:, :], TVEC[:, :], col(FL5), PHA[:, :], ALU.mult, ALU.subtract
                                         ).then_inc(S["ph"], 1)

            def pooled_lo(g):
                dve.wait_ge(S["plh"], g + 1)
                dve.tensor_tensor(PLL[:, g, :], TY[g % 2][:, :], PLH[:, g, :].bitcast(F32), ALU.subtract
                                  ).then_inc(S["pll"], 1)

            for g in range(4):
                if g == 3:
                    dve.wait_ge(S["tvec_in"], 16)
                    phase(0)
                win = 2 << g
                dve.wait_ge(S["p2ev"], g + 1)
                u = UB[:, g, PAD:PAD + L]
                src = UB[:, g, :]
                for k in range(g + 1):
                    dst = PBUF[k % 2]
                    tt(dst[:, PAD:PAD + L], src[:, PAD:PAD + L], src[:, PAD - (1 << k):PAD + L - (1 << k)], ALU.add)
                    src = dst
                out = TY[g % 2]
                if g >= 2:
                    dve.wait_ge(S["pll"], g - 1)
                link(dve.scalar_tensor_tensor(out[:, :], src[:, PAD:PAD + L], 1.0 / win, u, ALU.mult, ALU.subtract))
                tt(out[:, 0:win], src[:, PAD:PAD + win], par("invc", 16 * g, win), ALU.mult)
                dve.tensor_tensor(out[:, 0:win], out[:, 0:win], u[:, 0:win], ALU.subtract).then_inc(S["pool"], 1)
                if g:
                    pooled_lo(g - 1)
            pooled_lo(3)

            def group(mm, i):
                cos = COS[mm % 2]
                b = 2 + 2 * (mm % 2)
                dve.wait_ge(S["tr"], i * 16 + (4 * mm + 4))
                dve.wait_ge(S["prd"], i * 16 + 4 * mm + 1)
                dve.scalar_tensor_tensor(SIN[:, :], SH[:, :], 2.0, CH[:, :], ALU.mult, ALU.mult
                                         ).then_inc(S["sn"], 1)
                phase(mm + 1, i)
                dve.wait_ge(S["sn"], i * 4 + (mm + 1))
                dve.wait_ge(S["bmm"], i * 4 + (mm + 1) + 1)
                link(dve.tensor_tensor(T1[:, :], bank(b), cos[:, :], ALU.mult))
                link(dve.tensor_tensor(T2[:, :], bank(b + 1), SIN[:, :], ALU.mult))
                tt(T1[:, :], T1[:, :], T2[:, :], ALU.add)
                link(dve.tensor_tensor(T3[:, :], bank(b + 1), cos[:, :], ALU.mult))
                dve.tensor_tensor(T2[:, :], bank(b), SIN[:, :], ALU.mult).then_inc(S["burd"], 1)
                mag = SL[:, MAG5 + 4, ds(i * 4 + mm, 1)].to_broadcast([P, L])
                link(dve.tensor_tensor_scan(SRE[:, :], mag, T1[:, :], 0.0, ALU.mult, ALU.add))
                dve.wait_ge(S["burd"], i * 4 + (mm + 3))
                tt(T3[:, :], T3[:, :], T2[:, :], ALU.subtract)
                link(dve.tensor_tensor_scan(SIM[:, :], mag, T3[:, :], 0.0, ALU.mult, ALU.add))
                dve.wait_ge(S["cmm"], i * 4 + mm + 1)
                dve.tensor_tensor(PRD[0][:, :], cos[:, :], SRE[:, :], ALU.mult).then_inc(S["prd"], 1)
                dve.scalar_tensor_tensor(PRD[1][:, :], SIN[:, :], -1.0, SIM[:, :], ALU.mult, ALU.mult
                                         ).then_inc(S["prd"], 1)
                dve.tensor_tensor(PRD[2][:, :], SIN[:, :], SRE[:, :], ALU.mult).then_inc(S["prd"], 1)
                dve.tensor_tensor(PRD[3][:, :], cos[:, :], SIM[:, :], ALU.mult).then_inc(S["prd"], 1)

            for k in range(2):
                dve.tensor_copy(SC[:, 8 + k:9 + k], ONES[:, 0:1]).then_inc(S["burd"], 1)
            with repeat(dve, 4, (own, 32)) as i:
                for mm in range(4):
                    group(mm, i)
                dve.wait_ge(S["cmm"], i * 4 + 4 + 1)
                dve.scalar_tensor_tensor(tile_of(UA, i), tile_of(UA, i), par_at("sd", i), bank(6), ALU.mult,
                                         ALU.add).then_inc(S["yev"], 1)

            def lo(out, src, hi, sem):
                dve.tensor_tensor(out, src, hi.bitcast(F32), ALU.subtract).then_inc(sem, 1)

            def gated_pool(g):
                dve.wait_ge(*((S["pmm"], g + 1) if g < 3 else (tile_done, FIRST_TILE["poolw"] + 1)))
                dve.scalar_tensor_tensor(TY[g % 2][:, :], bank((OBASE["poolw"] + g) % 2), par("pscale", g),
                                         ZAB[:, 4 + g, :], ALU.mult, ALU.mult).then_inc(S["ybf"], 1)

            def gated_pool_lo(g):
                dve.wait_ge(S["ybh"], g + 1)
                lo(PLL[:, g, :], TY[g % 2][:, :], PLH[:, g, :], S["ybl"])

            dve.wait_ge(S["p2ev"], 32)
            gated_pool(0)
            gated_pool(1)
            for k in range(4):
                dve.wait_ge(S["yh"], k + 1)
                lo(HL[:, 4 + k, :], UA[:, k, :], HH[:, 4 + k, :], S["yl"])
            gated_pool_lo(0)
            dve.wait_ge(S["ybl"], 1)
            gated_pool(2)
            gated_pool_lo(1)
            dve.wait_ge(S["ybl"], 2)
            gated_pool(3)
            gated_pool_lo(2)
            gated_pool_lo(3)
            for j in range(4):
                dve.wait_ge(S["sg"], j + 1)
                link(dve.scalar_tensor_tensor(TS[j % 2][:, :], TS[j % 2][:, :], 1.0, UA[:, j, :], ALU.add, ALU.mult))
                dve.scalar_tensor_tensor(TS[j % 2][:, :], TS[j % 2][:, :], 0.5, ZAB[:, j, :], ALU.mult, ALU.mult
                                         ).then_inc(S["yaf"], 1)
                dve.wait_ge(S["yah"], j + 1)
                lo(HL[:, j, :], TS[j % 2][:, :], HH[:, j, :], S["yal"])
            with repeat(dve, 4, (own, 2)) as i:
                for j in range(2):
                    n = i * 2 + j
                    dve.wait_ge(S["amm"], i * 2 + (j + 1))
                    dve.wait_ge(S["ml"], n + 1)
                    link(dve.scalar_tensor_tensor(TY[j][:, :], tile_of(GAB, n), 1.0, bank(2 * j), ALU.add, ALU.mult))
                    dve.wait_ge(tile_done, n + (FIRST_TILE["branch"] + 1))
                    dve.scalar_tensor_tensor(TS[j][:, :], tile_of(GAB, i * 2 + (8 + j)), 1.0, bank(2 * j + 1),
                                             ALU.add, ALU.mult).then_inc(S["mev"], 1)
                    dve.wait_ge(S["mev"], n + 1)
                    dve.tensor_tensor(TY[j][:, :], TY[j][:, :], TS[j][:, :], ALU.add).then_inc(S["mrg"], 1)
                    dve.wait_ge(S["mh"], n + 1)
                    lo(tile_of(ML, n), TY[j][:, :], tile_of(MH, n), S["ml"])
            link(dve.memset(SSQ[:, :], 0.0))
            with dve.Fori(0, 4) as i:
                for j in range(2):
                    n = i * 2 + j
                    dve.wait_ge(tile_done, n + (FIRST_TILE["out2"] + 1))
                    dve.scalar_tensor_tensor(tile_of(X, n), bank((OBASE["out2"] + j) % 2), 0.5, tile_of(X, n),
                                             ALU.mult, ALU.add).then_inc(S["resid"], 1)
                    add_squares(40 + j, j, i, 2)
            dve.wait_ge(S["radd"], 48)
            sums_ready()
            dve.wait_ge(S["sqrt"], NINDEX["fin2"] + 1)
            link(dve.reciprocal(RT[:, :], RT[:, :]))
            for k in range(KD):
                dve.scalar_tensor_tensor(X[:, k, :], X[:, k, :], par("gfin2", k), RT[:, :], ALU.mult, ALU.mult
                                         ).then_inc(S["oready"], 1)

        block = ctx.enter_context(nc.Block())

        @block.sync
        def _(sp):
            def ring(stage, w, j, i=0, per=0):
                t = FIRST_TILE[stage] + j
                n = CHUNKS[stage] * P
                if t >= 2:
                    sp.wait_ge(tile_split, i * per + (t - 1))
                sp.dma_start(RAW[t % 2][:, 0:n],
                             w[ds(i * per + j, 1), :, :].rearrange("a p n -> p (a n)")
                             ).then_inc(tile_loaded[t % 2], 16)

            def mod_load(j, i=0, per=0, after=None):
                if after is not None:
                    sp.wait_ge(S["mod_used"], after)
                sp.dma_start(MR[j % 2][:, :], a["modw"][ds(i * per + j, 1), :, :].rearrange("a p n -> p (a n)")
                             ).then_inc(S[f"mod_in{j % 2}"], 16)

            sp.dma_start(CB[:, :], a["c"].partition_broadcast(P)).then_inc(S["c_in"], 16)
            sp.dma_start(CCB[:, :], a["cc"].partition_broadcast(P)).then_inc(S["cc_in"], 16)
            for j in range(16):
                if j >= 4:
                    sp.wait_ge(S["mod_used"], j - 3)
                    sp.wait_ge(S["ctx_mul"], len([k for k in BY_POOL if k <= j - 4]))
                sp.dma_start(MF[j % 4][:, :], a["modw"][j:j + 1, :, :].rearrange("a p n -> p (a n)")
                             ).then_inc(S[f"first_in{j % 4}"], 16)
                if j == 3:
                    sp.dma_start(X[:, :, :], a["x"]).then_inc(S["x_in"], 16)
                if j == 7:
                    sp.dma_start(CTX[:, :, :], a["ctx"]).then_inc(S["ctx_in"], 16)
            sp.dma_start(PAR[:, :], a["par"]).then_inc(S["par_in"], 16)
            ring("dq", a["wdq"], 0)
            ring("dq", a["wdq"], 1)
            ring("dq", a["wdq"], 2)
            ring("dq", a["wdq"], 3)
            for j in range(3):
                ring("kv", a["wdkv"], j)
            for j in range(2):
                ring("uv", a["wuv"], j)
            ring("heads", a["whead"], 0)
            with sp.Fori(0, 3) as i:
                for jj in range(2):
                    ring("heads", a["whead"], 1 + jj, i, 2)
                    for m in range(11):
                        j = 16 + 11 * jj + m
                        mod_load(j, i, 22, after=i * 22 + (j - 1))
            ring("heads", a["whead"], 7)
            for m in range(14):
                mod_load(82 + m, after=82 + m - 1)
                if m % 4 == 3 and m < 8:
                    ring("wo", a["wo"], m // 4)
            with sp.Fori(0, 3) as i:
                for j in range(2):
                    ring("wo", a["wo"], 2 + j, i, 2)
            for l in range(2):
                with sp.Fori(0, KF) as i:
                    for j in range(2):
                        ring(f"up{l}", a[f"wup{l}"], j, i, 2)
                with sp.Fori(0, 4) as i:
                    for j in range(4):
                        ring(f"down{l}", a[f"wdn{l}"], j, i, 4)
                if l == 0:
                    sp_hyena(sp, ring)
            sp_second(sp, ring)
            for k in range(KD):
                sp.wait_ge(S["oready"], k + 1)
                sp.dma_start(a["out"][:, k:k + 1, :], X[:, k:k + 1, :]).then_inc(S["out_done"], 16)
            sp.wait_ge(S["out_done"], 16 * KD)

        @block.gpsimd
        def _(pool):
            pool.memset(ONES[:, :], 1.0).then_inc(S["pchain"], 1)
            pool.memset(SC[:, 0:1], EPS).then_inc(S["pchain"], 1)
            pool.memset(IDENT[:, :], 0.0).then_inc(S["pchain"], 1)
            for k, name in enumerate(FROM_ONE):
                pool.memset(SC[:, 32 + k:33 + k], 0.0).then_inc(S[name], 1)
            pool.wait_ge(S["pchain"], 3)
            pool.affine_select(out=IDENT[:, :], in_=IDENT[:, :], compare_op=ALU.not_equal, fill=1.0,
                               base=0, pattern=[[-1, P]], channel_multiplier=1).then_inc(S["consts"], 1)

            def split(stage, j, i=0, per=0):
                t = FIRST_TILE[stage] + j
                n = CHUNKS[stage] * P
                s = t % 2
                if t >= 2:
                    pool.wait_ge(tile_done, i * per + (t - 1))
                pool.wait_ge(tile_loaded[s], i * (8 * per) + 16 * (t // 2 + 1))
                pool.tensor_tensor(SC[0:1, 100:101], ONES[0:1, 0:1], ONES[0:1, 0:1], ALU.add)
                pool.tensor_scalar(WH[s][:, 0:n], RAW[s][:, 0:n], 1.0, 0.0, ALU.mult, ALU.add
                                   ).then_inc(tile_hi, 1)
                pool.wait_ge(tile_hi, i * per + (t + 1))
                pool.tensor_tensor(WL[s][:, 0:n], RAW[s][:, 0:n], WH[s][:, 0:n].bitcast(F32),
                                   ALU.subtract).then_inc(tile_split, 1)

            pool.wait_ge(S["silu_c"], 2)
            for n, j in enumerate(BY_POOL):
                pool.wait_ge(S[f"first_in{j % 4}"], 16 * (j // 4 + 1))
                if n >= 3:
                    pool.wait_ge(S["ctx_sum"], n - 2)
                pool.tensor_tensor(MX[n % 3][:, :], MF[j % 4][:, :], CCB[:, :], ALU.mult).then_inc(S["ctx_mul"], 1)

            for st, n in (("dq", 4), ("kv", 3), ("uv", 2)):
                for j in range(n):
                    split(st, j)
            with pool.Fori(0, 4) as i:
                for j in range(2):
                    split("heads", j, i, 2)
            with pool.Fori(0, 4) as i:
                for j in range(2):
                    split("wo", j, i, 2)
            for l in range(2):
                with pool.Fori(0, KF) as i:
                    for j in range(2):
                        split(f"up{l}", j, i, 2)
                with pool.Fori(0, 8) as i:
                    for j in range(2):
                        split(f"down{l}", j, i, 2)
                if l == 0:
                    pool_hyena(pool, split)
            pool_second(pool, split)

        @block.tensor
        def _(pe):
            def stat(name, ssq, w=L):
                n = NINDEX[name]
                pe.wait_ge(S["ssq"], n - 1)
                if n:
                    pe.wait_ge(S["sqrt"], n)
                pe.matmul(bank(7, w), ONES[:, :], ssq[:, 0:w], start=True, stop=True
                          ).then_inc(S["stat"], 1)

            def mm3(out, wh, wl, xh, xl, first, last):
                pe.matmul(out, wh, xh, start=first, stop=False)
                pe.matmul(out, wh, xl, start=False, stop=False)
                return pe.matmul(out, wl, xh, start=False, stop=last)

            def chunk(s, k):
                return WH[s][:, k * P:(k + 1) * P], WL[s][:, k * P:(k + 1) * P]

            def linear(stage, j, xh, xl, evac, i=0, per=0, kn=KD, tiles=1, hidden=None):
                bk = (OBASE[stage] + j) % 2
                if per or j >= 2:
                    pe.wait_ge(evac[0], i * per + (evac[1] + j - 1))
                for h in range(tiles):
                    t = FIRST_TILE[stage] + j * tiles + h
                    pe.wait_ge(tile_split, i * (per * tiles) + (t + 1))
                    for k in range(kn):
                        kk = h * kn + k
                        if hidden is not None:
                            pe.wait_ge(S["hidl"], hidden + kk + 1)
                        m = mm3(bank(bk), *chunk(t % 2, k), xh[:, kk, :], xl[:, kk, :],
                                kk == 0, kk == tiles * kn - 1)
                    m.then_inc(tile_done, 1)

            def first_two(stage, norm):
                t = FIRST_TILE[stage]
                pe.wait_ge(tile_split, t + 2)
                for step in range(KD + KD // 2):
                    for j, k in ((0, step), (1, step - KD // 2)):
                        if not 0 <= k < KD:
                            continue
                        if j == 0:
                            pe.wait_ge(S["nl"], NBASE[norm] + k + 1)
                        m = mm3(bank((OBASE[stage] + j) % 2), *chunk((t + j) % 2, k), HH[:, k, :], HL[:, k, :],
                                k == 0, k == KD - 1)
                        if k == KD - 1:
                            m.then_inc(tile_done, 1)

            pe.wait_ge(S["filt_in"], 64)
            pe.matmul(PS[0:HID_F, 2, :], FW1[:, :], ZT[:, :], start=True, stop=True).then_inc(S["fmm"], 1)
            pe.wait_ge(S["consts"], 1)
            for k in range(KD):
                pe.wait_ge(S["xsq"], k // 4 + 1)
                m = pe.matmul(bank(7), ONES[:, :], XSQ[:, k, :], start=k == 0, stop=k == KD - 1)
            m.then_inc(S["stat"], 1)
            pe.wait_ge(S["fsin"], 1)
            pe.matmul(PS[0:HID_F, 3, :], FW2[:, :], FA[:, :], start=True, stop=True).then_inc(S["fmm"], 1)
            pe.wait_ge(S["xsq"], 3)
            pe.wait_ge(S["sqrt"], 1)
            for k in range(KD):
                m = pe.matmul(bank(7, LC), ONES[:, :], XSQ[:, k // 2, LC * (k % 2):LC * (k % 2) + LC],
                              start=k == 0, stop=k == KD - 1)
            m.then_inc(S["stat"], 1)
            first_two("dq", "x0")
            for j in range(2, 4):
                linear("dq", j, HH, HL, (S["cq_sq"], 0))
            for j in range(3):
                t = FIRST_TILE["kv"] + j
                b = OBASE["kv"] + 2 * j
                pe.wait_ge(tile_split, t + 1)
                pe.wait_ge(*((S["ckv_ev"], 2 * j - 1) if j else (S["cq_sq"], 3)))
                for k in range(KD):
                    m = mm3(bank(b % 2), *chunk(t % 2, k), HH[:, k, :], HL[:, k, :], k == 0, k == KD - 1)
                m.then_inc(S["kv_x"], 1)
                b += 1
                pe.wait_ge(*((S["ckv_ev"], 2 * j) if j else (S["cq_sq"], 4)))
                for k in range(KD):
                    if j == 0:
                        pe.wait_ge(S["nl"], NBASE["ctx"] + k + 1)
                    m = mm3(bank(b % 2, LC), *chunk(t % 2, k), HCH[:, k, :], HCL[:, k, :], k == 0, k == KD - 1)
                m.then_inc(tile_done, 1)
                if j == 0:
                    stat("cq", SSQA)
            stat("ckx", SSQA)
            stat("ckc", SSQA[:, L:LK], LC)
            pe.wait_ge(S["nl"], NBASE["ckx"] + 2)
            for j in range(2):
                t = FIRST_TILE["uv"] + j
                pe.wait_ge(tile_split, t + 1)
                for m6 in range(6):
                    n = 6 * j + m6
                    b = OBASE["uv"] + n
                    if n == 4:
                        pe.wait_ge(S["nl"], NBASE["ckc"] + 2)
                    pe.wait_ge(*((S["krot"], 2 + 4 * n) if n < 2 else (S["v_ev"], n - 1)))
                    for k in range(2):
                        wh = WH[t % 2][:, 512 * k:512 * k + 512]
                        wl = WL[t % 2][:, 512 * k:512 * k + 512]
                        kh = CKH[:, k, m6 * P:(m6 + 1) * P]
                        kl = CKL[:, k, m6 * P:(m6 + 1) * P]
                        pe.matmul(bank(b % 2), kh, wh, start=k == 0, stop=False)
                        pe.matmul(bank(b % 2), kh, wl, start=False, stop=False)
                        m = pe.matmul(bank(b % 2), kl, wh, start=False, stop=k == 1)
                    if m6 < 5:
                        m.then_inc(S["proj"], 1)
                    else:
                        m.then_inc(tile_done, 1)

            def project(p, i=0, per=0):
                t = FIRST_TILE["heads"] + p
                s = t % 2
                pe.wait_ge(tile_split, i * per + (t + 1))
                for hb in range(2):
                    if p and not hb:
                        pe.wait_ge(S["vc"], i * per + p)
                    for k in range(4):
                        m = mm3(bank(4 + hb), *chunk(s, 4 * hb + k), CQH[:, k, :], CQL[:, k, :], k == 0, k == 3)
                    m.then_inc(S["proj"], 1)
                for c, (lo, hi) in enumerate(((0, L), (L, LK))):
                    pe.wait_ge(S["qready"], i * (2 * per) + (2 * p + 1 + c))
                    for k in range(2):
                        m = mm3(bank(4 + c, hi - lo), *chunk(s, 8 + k), CKH[:, k, lo:hi], CKL[:, k, lo:hi],
                                k == 0, k == 1)
                    m.then_inc(S["proj"] if c == 0 else tile_done, 1)

            def scores(h, i=0, per=0):
                hb = h % 2
                pe.wait_ge(S["qready"], i * per + (h + 1))
                pe.wait_ge(S["kready"], i * (2 * per) + 4 * (h // 2 + 1))
                for qt in range(4):
                    g = 4 * h + qt
                    if g >= 2:
                        pe.wait_ge(S["sexp"], i * (4 * per) + (g - 1))
                    b = 2 * (qt % 2)
                    pe.matmul(bank(b), Q[hb][:, qt * P:(qt + 1) * P], KP[hb][:, 0:L], start=True, stop=True)
                    pe.matmul(bank(b + 1, LC), Q[hb][:, qt * P:(qt + 1) * P], KP[hb][:, L:LK],
                              start=True, stop=True).then_inc(S["s_ready"], 1)

            def attend(h, i=0, per=0):
                hb = h % 2
                v = slice(VH * hb, VH * hb + VH)
                pe.wait_ge(S["diag"], i * (4 * per) + 4 * (h + 1))

                def turn(kt):
                    pe.wait_ge(S["pt"], i * (6 * per) + (6 * h + max(kt - 1, 0)) + 1)
                    for qt in range(4):
                        m = pe.matmul(PS[:, 6 + kt % 2, qt * P:(qt + 1) * P],
                                      PR[hb][:, qt, kt * P:(kt + 1) * P], DG[hb][:, qt, :],
                                      start=True, stop=True)
                    m.then_inc(S["s_tr"], 1)

                def value(kt):
                    pe.wait_ge(S["pt"], i * (6 * per) + (6 * h + kt + 1) + 1)
                    m = pe.matmul(PS[v, 4 + hb, :], VC[:, kt, v], PT[:, kt, :], start=kt == 0, stop=kt == 5)
                    if kt == 5:
                        m.then_inc(S["pv"], 1)

                turn(0)
                turn(1)
                pe.wait_ge(S["vc"], i * (per // 2) + (h // 2 + 1))
                pe.wait_ge(S["kready"], i * (2 * per) + (4 * min(h // 2 + 2, 8) - 2 + 2 * hb))
                for kt in range(6):
                    value(kt)
                    if kt + 2 < 6:
                        turn(kt + 2)

            pe.wait_ge(S["v_ev"], 12)
            project(0)
            scores(0)

            def pair(p, i=0, per=0):
                scores(2 * p + 1, i, 2 * per)
                project(p + 1, i, per)
                attend(2 * p, i, 2 * per)
                scores(2 * p + 2, i, 2 * per)
                attend(2 * p + 1, i, 2 * per)

            with pe.Fori(0, 3) as i:
                pair(0, i, 2)
                pair(1, i, 2)
            pair(6)
            scores(15)
            attend(14)
            attend(15)

            pe.wait_ge(S["olo"], HEADS)
            for j in range(2):
                linear("wo", j, HH, HL, (S["resid"], 0))
            with pe.Fori(0, 3) as i:
                for j in range(2):
                    linear("wo", 2 + j, HH, HL, (S["resid"], 0), i, 2)
            for l in range(2):
                if l == 1:
                    pe_hyena(pe, linear, first_two, stat, mm3, chunk)
                stat(f"ffn{l}", SSQ)
                first_two(f"up{l}", f"ffn{l}")
                with pe.Fori(0, KF - 1) as i:
                    for j in range(2):
                        linear(f"up{l}", 2 + j, HH, HL, (S["zc"], NUP * l), i, 2)
                for j in range(2):
                    pe.wait_ge(S["zc"], NUP * (l + 1) - 1 + j)
                    linear(f"down{l}", j, HIDH, HIDL, (S["resid"], RBASE[f"down{l}"]), kn=11, tiles=2,
                           hidden=KF * l if j == 0 else None)
                with pe.Fori(0, 3) as i:
                    for j in range(2):
                        linear(f"down{l}", 2 + j, HIDH, HIDL, (S["resid"], RBASE[f"down{l}"]), i, 2, kn=11, tiles=2)
            pe_second(pe, linear, first_two, stat, mm3, chunk)

        @block.scalar
        def _(act):
            act.dma_start(ZT[:, :], a["zt"]).then_inc(S["filt_in"], 16)
            act.dma_start(FW1[:, :], a["fw1"]).then_inc(S["filt_in"], 16)
            act.dma_start(FW2[:, :], a["fw2"]).then_inc(S["filt_in"], 16)
            act.dma_start(FPAR[:, :], a["fpar"]).then_inc(S["filt_in"], 16)
            act.dma_start(QTAB[:, :], a["qtab"]).then_inc(S["tab_in"], 16)
            act.dma_start(KCOS[:, :], a["kcos"]).then_inc(S["tab_in"], 16)
            act.dma_start(KSIN[P // 2:P, :], a["ksin"]).then_inc(S["tab_in"], 16)

            def root(name, w, dn, rt):
                act.wait_ge(S["stat"], NINDEX[name] + 1)
                if NBASE[name]:
                    act.wait_ge(S["nt"], NBASE[name])
                act.activation(rt[:, 0:w], bank(7, w), ACT.Sqrt, bias=SC[:, 0:1], scale=1.0 / dn
                               ).then_inc(S["sqrt"], 1)

            def norm(name, dst, w, dn, rt, tn, tm, shift=0):
                if name != "x0":
                    root(name, w, dn, rt)
                for k in range(NTILES[name]):
                    g = NBASE[name] + k
                    _, bias = GAIN[name](k)
                    out = dst[:, k, shift:shift + w]
                    src = (tn + tm)[k % 4][:, 0:w]
                    act.wait_ge(S["nt"], g + 1)
                    if bias is None:
                        act.copy(out, src).then_inc(S["nh"], 1)
                    else:
                        act.activation(out, src, ACT.Identity, bias=bias, scale=1.0).then_inc(S["nh"], 1)

            spare = iter(range(44, 60))

            def load_table(func):
                c = next(spare)
                act.activation(SC[:, c:c + 1], SC[:, 0:1], func)

            act.wait_ge(S["c_in"], 16)
            act.activation(CB[:, :], CB[:, :], ACT.Silu).then_inc(S["silu_c"], 1)
            act.wait_ge(S["cc_in"], 16)
            act.activation(CCB[:, :], CCB[:, :], ACT.Silu).then_inc(S["silu_c"], 1)
            act.wait_ge(S["fa"], 1)
            act.activation(FA[:, :], FA[:, :], ACT.Sin).then_inc(S["fsin"], 1)
            act.wait_ge(S["x_in"], 16)
            for k in range(2):
                act.activation(XSQ[:, 4 * k:4 * k + 4, :], X[:, 4 * k:4 * k + 4, :], ACT.Square
                               ).then_inc(S["xsq"], 1)

            def context_sums(lo, hi):
                for n in range(lo, hi):
                    act.wait_ge(S["ctx_mul"], n + 1)
                    act.activation(MX[n % 3][:, :], MX[n % 3][:, :], ACT.Identity,
                                   accum_out=MODC[:, BY_POOL[n]:BY_POOL[n] + 1]).then_inc(S["ctx_sum"], 1)

            context_sums(0, 4)
            act.wait_ge(S["ctx_in"], 16)
            act.wait_ge(S["stat"], 1)
            act.activation(XSQ[:, 0:4, :].rearrange("p a n -> p (a n)"),
                           CTX[:, :, :].rearrange("p a n -> p (a n)"), ACT.Square).then_inc(S["xsq"], 1)
            root("x0", L, D, RTA)
            context_sums(4, len(BY_POOL))
            act.wait_ge(S["ab"], 1)
            norm("x0", HH, L, D, RTA, TA, TB)
            for j in range(4):
                if j == 2:
                    norm("ctx", HCH, LC, D, RTA, TA, TB)
                act.wait_ge(tile_done, FIRST_TILE["dq"] + j + 1)
                act.copy(C32[:, j, :], bank((OBASE["dq"] + j) % 2)).then_inc(S["cq_ev"], 1)
                if j >= 2:
                    act.wait_ge(S["cq_add"], j - 1)
                act.activation(MX[j % 2][:, 0:L], bank((OBASE["dq"] + j) % 2), ACT.Square
                               ).then_inc(S["cq_sq"], 1)
            for j in range(2):
                b = OBASE["kv"] + 2 * j
                act.wait_ge(S["kv_x"], j + 1)
                act.copy(CK32[:, j, 0:L], bank(b % 2)).then_inc(S["ckv_ev"], 1)
                act.wait_ge(tile_done, FIRST_TILE["kv"] + j + 1)
                act.copy(CK32[:, j, L:LK], bank((b + 1) % 2, LC)).then_inc(S["ckv_ev"], 1)
                if j == 0:
                    norm("cq", CQH, L, QL, RTA, TA, TB)
            act.wait_ge(S["fa"], 2)
            for half in range(2):
                act.activation(H2T[HID_F * half:HID_F * half + HID_F, :], FA[:, :], ACT.Sin
                               ).then_inc(S["fsin"], 1)
            norm("ckx", CKH, L, KVL, RTA, TA, TB)
            norm("ckc", CKH, LC, KVL, RTA, TA, TB, shift=L)
            act.wait_ge(S["nl"], NBASE["ckc"] + 2)
            for n in range(12):
                if n % 6 < 5:
                    act.wait_ge(S["proj"], 5 * (n // 6) + n % 6 + 1)
                else:
                    act.wait_ge(tile_done, FIRST_TILE["uv"] + n // 6 + 1)
                act.copy(V[:, n % 6, 512 * (n // 6):512 * (n // 6) + 512], bank((OBASE["uv"] + n) % 2)
                         ).then_inc(S["v_ev"], 1)

            def keys(p, i=0, per=0):
                act.wait_ge(S["proj"], i * (3 * per) + (10 + 3 * p + 3))
                for hb in range(2):
                    act.copy(KP[hb][0:NOPE, 0:L], PS[NOPE * hb:NOPE * hb + NOPE, 4, :]
                             ).then_inc(S["kready"], 1)
                act.wait_ge(tile_done, i * per + (FIRST_TILE["heads"] + p + 1))
                for hb in range(2):
                    act.copy(KP[hb][0:NOPE, L:LK], PS[NOPE * hb:NOPE * hb + NOPE, 5, 0:LC]
                             ).then_inc(S["kready"], 1)

            def exps(h, i=0, per=0, turned_first=None):
                if per or h >= 2:
                    act.wait_ge(S["s_tr"], i * (6 * per) + 6 * (h - 1) + 1)
                for qt in range(4):
                    if qt == 3 and turned_first is not None:
                        turn_copy(turned_first, 0, i, per)
                    act.wait_ge(S["smax"], i * (4 * per) + (4 * h + qt + 1))
                    act.activation(PR[h % 2][:, qt, :], wide(2 * (qt % 2), LK), ACT.Exp,
                                   bias=NMX[:, (4 * h + qt) % 8:(4 * h + qt) % 8 + 1], scale=1.0,
                                   accum_out=SUMS[:, (4 * h + qt) % 8:(4 * h + qt) % 8 + 1]
                                   ).then_inc(S["sexp"], 1)

            def turn_copy(h, kt, i=0, per=0):
                act.wait_ge(S["s_tr"], i * (6 * per) + (6 * h + kt + 1) + 1)
                if kt == 0:
                    act.wait_ge(S["pv"], i * per + h + 1)
                act.copy(PT[:, kt, :], bank(6 + kt % 2)).then_inc(S["pt"], 1)

            def turned(h, i=0, per=0, first=0):
                for kt in range(first, 6):
                    turn_copy(h, kt, i, per)
                v = slice(VH * (h % 2), VH * (h % 2) + VH)
                act.wait_ge(S["pv"], i * per + (h + 1) + 1)
                act.copy(HH[v, ds(i * (per // 2) + h // 2, 1), :].rearrange("p a n -> p (a n)"),
                         PS[v, 4 + h % 2, :]).then_inc(S["ohi"], 1)

            def pair(p, i=0, per=0):
                exps(2 * p + 1, i, 2 * per)
                keys(p + 1, i, per)
                turned(2 * p, i, 2 * per)
                exps(2 * p + 2, i, 2 * per, 2 * p + 1)
                turned(2 * p + 1, i, 2 * per, 1)

            keys(0)
            exps(0)
            with act.Fori(0, 3) as i:
                pair(0, i, 2)
                pair(1, i, 2)
            pair(6)
            exps(15)
            turned(14)
            turned(15)

            def squares(stage, j, i=0, per=0):
                n = RBASE[stage] + j
                act.wait_ge(S["resid"], i * per + (n + 1))
                if n >= 2:
                    act.wait_ge(S["radd"], i * per + (n - 1))
                act.activation(SQ[j % 2][:, :], X[:, ds(i * per + j, 1), :].rearrange("p a n -> p (a n)"),
                               ACT.Square).then_inc(S["rsq"], 1)

            def ffn_up(l, i):
                n = KF * l
                t = FIRST_TILE[f"up{l}"]
                for half, buf in ((0, ZA), (1, ZG)):
                    act.wait_ge(tile_done, i * 2 + (t + half + 1))
                    if half == 0:
                        act.wait_ge(S["hid"], i + n + 1)
                    c = KF * half + l * NUP
                    act.activation(buf[:, :], bank((OBASE[f"up{l}"] + half) % 2), ACT.Identity,
                                   scale=par_at("fcw", i + (l * 3 * NUP + NUP + KF * half)),
                                   bias=par_at("fcb", i + c)).then_inc(S["za"], 1)
                act.wait_ge(S["zc"], i * 2 + (2 * n + 2))
                act.activation(ZG[:, :], ZG[:, :], ACT.Silu).then_inc(S["silu"], 1)
                act.wait_ge(S["hid"], i + (n + 1) + 1)
                act.copy(HIDH[:, ds(i, 1), :].rearrange("p a n -> p (a n)"), HID[:, :]
                         ).then_inc(S["hidh"], 1)

            load_table(ACT.Sqrt)
            for j in range(2):
                squares("wo", j)
            with act.Fori(0, 3) as i:
                for j in range(2):
                    squares("wo", 2 + j, i, 2)
            for l in range(2):
                if l == 1:
                    act_hyena(act, norm, squares, load_table)
                act.wait_ge(S["ab"], 2 if l == 0 else 4)
                norm(f"ffn{l}", HH, L, D, RT, TN, TM)
                load_table(ACT.Silu)
                with act.Fori(0, KF) as i:
                    ffn_up(l, i)
                load_table(ACT.Sqrt)
                with act.Fori(0, 4) as i:
                    for j in range(2):
                        squares(f"down{l}", j, i, 2)
            act_second(act, norm, squares, load_table)

        @block.vector
        def _(dve):
            own = Tally(S["dchain"])

            def link(ins):
                v = own.up()
                ins.then_inc(S["dchain"], 1)
                dve.wait_ge(S["dchain"], v)

            def inverse(name, w, rt):
                dve.wait_ge(S["sqrt"], NINDEX[name] + 1)
                link(dve.reciprocal(rt[:, 0:w], rt[:, 0:w]))

            def norm(name, src, dst_h, dst_l, w, rt, tn, tm, shift=0):
                if name != "x0":
                    inverse(name, w, rt)

                def low(k):
                    g = NBASE[name] + k
                    _, bias = GAIN[name](k)
                    t = (tn + tm)[k % 4][:, 0:w]
                    hi = dst_h[:, k, shift:shift + w].bitcast(F32)
                    dve.wait_ge(S["nh"], g + 1)
                    if bias is None:
                        ins = dve.tensor_tensor(dst_l[:, k, shift:shift + w], t, hi, ALU.subtract)
                    else:
                        ins = dve.scalar_tensor_tensor(dst_l[:, k, shift:shift + w], t, bias, hi, ALU.add,
                                                       ALU.subtract)
                    ins.then_inc(S["nl"], 1)

                for k in range(NTILES[name]):
                    g = NBASE[name] + k
                    if g >= 4:
                        dve.wait_ge(S["nl"], g - 3)
                    dve.scalar_tensor_tensor((tn + tm)[k % 4][:, 0:w], src[:, k, shift:shift + w],
                                             GAIN[name](k)[0], rt[:, 0:w], ALU.mult, ALU.mult
                                             ).then_inc(S["nt"], 1)
                    if k:
                        low(k - 1)
                low(NTILES[name] - 1)

            def reduce_angle(x, k, w=L):
                link(dve.tensor_scalar(k, x, 1.0 / TWO_PI, None, ALU.mult))
                link(dve.tensor_scalar(k, k, ROUND, ROUND, ALU.add, ALU.subtract))
                for part in (PI_A, PI_B, PI_C):
                    link(dve.scalar_tensor_tensor(x, k, -part, x, ALU.mult, ALU.add))

            def filter_layer(layer):
                dve.wait_ge(S["fmm"], layer + 1)
                link(dve.tensor_scalar(FA[:, :], PS[0:HID_F, 2 + layer, :], FPAR[:, 2 * layer:2 * layer + 1],
                                       FPAR[:, 2 * layer + 1:2 * layer + 2], ALU.add, ALU.mult))
                reduce_angle(FA[:, :], FK[:, :])
                dve.tensor_scalar(FA[:, :], FA[:, :], math.pi, -math.pi, ALU.min, ALU.max
                                  ).then_inc(S["fa"], 1)

            filter_layer(0)
            dve.wait_ge(S["silu_c"], 2)
            for j in range(16):
                dve.wait_ge(S[f"first_in{j % 4}"], 16 * (j // 4 + 1))
                if j >= 2:
                    dve.wait_ge(S["mod_used"], j - 1)
                ins = dve.tensor_tensor_reduce(C32[:, 2 * (j % 2):2 * (j % 2) + 2, :].rearrange("p a n -> p (a n)"),
                                               MF[j % 4][:, :], CB[:, :], 1.0, 0.0, ALU.mult, ALU.add,
                                               MOD[:, j:j + 1])
                if j == 12:
                    inverse("x0", L, RTA)
                if j in BY_POOL:
                    ins.then_inc(S["mod_used"], 1)
                    continue
                link(ins)
                dve.tensor_tensor_reduce(MF[j % 4][:, :], MF[j % 4][:, :], CCB[:, :], 1.0, 0.0,
                                         ALU.mult, ALU.add, MODC[:, j:j + 1]).then_inc(S["mod_used"], 1)
            dve.wait_ge(S["par_in"], 16)
            dve.wait_ge(S["mod_used"], 16)
            dve.wait_ge(S["ctx_sum"], len(BY_POOL))
            link(dve.tensor_tensor(MOD[:, 0:16], MOD[:, 0:16], par("modb", 0, 16), ALU.add))
            link(dve.tensor_tensor(MODC[:, :], MODC[:, :], par("modb", 0, 16), ALU.add))
            for row, m in ((0, MOD), (2, MODC)):
                link(dve.scalar_tensor_tensor(AB[:, row, :], m[:, 8:16], 1.0, par("gmix", 0, 8), ALU.add, ALU.mult))
                link(dve.tensor_copy(AB[:, row + 1, :], m[:, 0:8]))
            dve.tensor_copy(SC[:, 2:3], ONES[:, 0:1]).then_inc(S["ab"], 1)
            norm("x0", X, HH, HL, L, RTA, TA, TB)
            norm("ctx", CTX, HCH, HCL, LC, RTA, TA, TB)
            dve.wait_ge(S["stat"], 2)
            for j in range(4):
                dve.wait_ge(S["cq_sq"], j + 1)
                if j == 0:
                    ins = dve.tensor_copy(SSQA[:, 0:L], MX[0][:, 0:L])
                else:
                    dve.wait_ge(S["cq_add"], j)
                    ins = dve.tensor_tensor(SSQA[:, 0:L], SSQA[:, 0:L], MX[j % 2][:, 0:L], ALU.add)
                ins.then_inc(S["cq_add"] if j < 3 else S["ssq"], 1)
            norm("cq", C32, CQH, CQL, L, RTA, TA, TB)
            filter_layer(1)
            dve.wait_ge(S["ckv_ev"], 4)
            link(dve.tensor_tensor(SSQA[:, :], CK32[:, 0, :], CK32[:, 0, :], ALU.mult))
            link(dve.tensor_tensor(RTA[:, :], CK32[:, 1, :], CK32[:, 1, :], ALU.mult))
            link(dve.tensor_tensor(SSQA[:, :], SSQA[:, :], RTA[:, :], ALU.add))
            dve.tensor_copy(SC[:, 3:4], ONES[:, 0:1]).then_inc(S["ssq"], 1)
            hi = slice(P // 2, P)
            dve.wait_ge(S["tab_in"], 48)
            dve.wait_ge(S["fsin"], 3)
            dve.wait_ge(S["kv_x"], 3)
            b = OBASE["kv"] + 4
            dve.tensor_tensor(K1[hi, :], PS[0:P // 2, b % 2, :], KCOS[:, :], ALU.mult).then_inc(S["krot"], 1)
            dve.tensor_tensor(C32[hi, 0, :], PS[hi, b % 2, :], KSIN[hi, :], ALU.mult).then_inc(S["krot"], 1)
            dve.wait_ge(S["krot"], 2)
            for hb in range(2):
                dve.tensor_tensor(KP[hb][hi, 0:L], K1[hi, :], C32[hi, 0, :], ALU.add).then_inc(S["krot"], 1)
            dve.wait_ge(tile_done, FIRST_TILE["kv"] + 3)
            for hb in range(2):
                dve.tensor_copy(KP[hb][hi, L:LK], PS[0:P // 2, (b + 1) % 2, 0:LC]).then_inc(S["krot"], 1)
            norm("ckx", CK32, CKH, CKL, L, RTA, TA, TB)
            dve.tensor_copy(SC[:, 4:5], ONES[:, 0:1]).then_inc(S["ssq"], 1)
            norm("ckc", CK32, CKH, CKL, LC, RTA, TA, TB, shift=L)

            def mod_rows(j, i=0, per=0, column=0):
                dve.wait_ge(S[f"mod_in{j % 2}"], i * (8 * per) + 16 * (j // 2 + 1))
                dve.tensor_tensor_reduce(MR[j % 2][:, :], MR[j % 2][:, :], CB[:, :], 1.0, 0.0,
                                         ALU.mult, ALU.add, MACC[:, column:column + 1]
                                         ).then_inc(S["mod_used"], 1)

            def mod_store(j, n, i=0, per=0):
                dve.wait_ge(S["mod_used"], i * per + (16 + j + n))
                dve.tensor_copy(MOD[:, ds(i * per + (16 + j), n)], MACC[:, 0:n]).then_inc(S["modx"], 1)

            def queries(p, i=0, per=0):
                for hb in range(2):
                    dve.wait_ge(S["proj"], i * (3 * per) + (10 + 3 * p + 1 + hb))
                    dve.tensor_tensor(Q[hb][:, :], bank(4 + hb), QTAB[:, :], ALU.mult).then_inc(S["qready"], 1)

            def maxes(h, i=0, per=0, between=None):
                for qt in range(4):
                    dve.wait_ge(S["s_ready"], i * (4 * per) + (4 * h + qt + 1))
                    c = (4 * h + qt) % 8
                    dve.tensor_reduce(NMX[:, c:c + 1], wide(2 * (qt % 2), LK), AX.X, ALU.max, negate=True
                                      ).then_inc(S["smax"], 1)
                    if qt == 1 and between is not None:
                        between()

            def value_copy(p, i=0, per=0):
                dve.wait_ge(S["pv"], i * (2 * per) + 2 * p + 1)
                dve.tensor_copy(VC[:, :, :], V[:, :, ds(i * (P * per) + P * p, P)]).then_inc(S["vc"], 1)

            def diagonals(h, i=0, per=0):
                dve.wait_ge(S["sexp"], i * (4 * per) + 4 * (h + 1))
                c = 4 * (h % 2)
                link(dve.reciprocal(RSUM[:, c:c + 4], SUMS[:, c:c + 4]))
                for qt in range(4):
                    dve.tensor_scalar(DG[h % 2][:, qt, :], IDENT[:, :], RSUM[:, c + qt:c + qt + 1], None, ALU.mult
                                      ).then_inc(S["diag"], 1)

            def out_lo(h, i=0, per=0):
                v = slice(VH * (h % 2), VH * (h % 2) + VH)
                at = (v, ds(i * (per // 2) + h // 2, 1), slice(None))
                dve.wait_ge(S["ohi"], i * per + (h + 1))
                dve.tensor_tensor(HL[at].rearrange("p a n -> p (a n)"), PS[v, 4 + h % 2, :],
                                  HH[at].rearrange("p a n -> p (a n)").bitcast(F32),
                                  ALU.subtract).then_inc(S["olo"], 1)

            def pair(p, i=0, per=0):
                m = 11 * p
                two = 11 * per
                value_copy(p, i, per)
                maxes(2 * p + 1, i, 2 * per, lambda: mod_rows(m, i, two, 0))
                for k in range(1, 3):
                    mod_rows(m + k, i, two, k)
                queries(p + 1, i, per)
                diagonals(2 * p + 1, i, 2 * per)
                for k in range(3, 8):
                    mod_rows(m + k, i, two, k)
                maxes(2 * p + 2, i, 2 * per, lambda: mod_rows(m + 8, i, two, 8))
                out_lo(2 * p, i, 2 * per)
                diagonals(2 * p + 2, i, 2 * per)
                for k in range(9, 11):
                    mod_rows(m + k, i, two, k)
                out_lo(2 * p + 1, i, 2 * per)
                mod_store(m, 11, i, two)
                dve.wait_ge(S["modx"], i * per + (p + 1))

            queries(0)
            maxes(0)
            diagonals(0)
            with repeat(dve, 3, (own, 4)) as i:
                pair(0, i, 2)
                pair(1, i, 2)
            pair(6)
            value_copy(7)
            maxes(15)
            diagonals(15)
            out_lo(14)
            out_lo(15)
            for n in range(3):
                mod_rows(77 + n, column=n)
            mod_store(77, 3)
            dve.wait_ge(S["modx"], 8)
            link(dve.tensor_tensor(MOD[:, 16:96], MOD[:, 16:96], par("modb", 16, 80), ALU.add))

            def residual(stage, j, layer, i=0, per=0, tiles=1, gate=2):
                n = RBASE[stage] + j
                t = FIRST_TILE[stage] + j * tiles + tiles - 1
                xt = X[:, ds(i * per + j, 1), :].rearrange("p a n -> p (a n)")
                dve.wait_ge(tile_done, i * (per * tiles) + (t + 1))
                dve.scalar_tensor_tensor(xt, bank((OBASE[stage] + j) % 2),
                                         MOD[:, ds(i * per + (48 * layer + KD * gate + j), 1)], xt,
                                         ALU.mult, ALU.add).then_inc(S["resid"], 1)
                add_squares(n, j, i, per)

            def add_squares(n, j, i, per):
                dve.wait_ge(S["rsq"], i * per + (n + 1))
                if n or per:
                    dve.wait_ge(S["radd"], i * per + n)
                dve.tensor_tensor(SSQ[:, :], SSQ[:, :], SQ[j % 2][:, :], ALU.add).then_inc(S["radd"], 1)

            def conv_side(buf, bk, w0, w2, z, zwait, i):
                dve.wait_ge(S["za"], zwait)
                link(dve.scalar_tensor_tensor(buf[:, 1:L], bank(bk)[:, 0:L - 1], w0, buf[:, 1:L],
                                              ALU.mult, ALU.add))
                dve.scalar_tensor_tensor(buf[:, 0:L - 1], bank(bk)[:, 1:L], w2, buf[:, 0:L - 1],
                                         ALU.mult, ALU.add).then_inc(S["zc"], 1)

            def ffn_up(l, i):
                n = KF * l
                for half, buf in ((0, ZA), (1, ZG)):
                    c = l * 3 * NUP + KF * half
                    conv_side(buf, (OBASE[f"up{l}"] + half) % 2, par_at("fcw", i + c),
                              par_at("fcw", i + (c + 2 * NUP)), None, i * 2 + (2 * n + half + 1), i)
                dve.wait_ge(S["silu"], i + (n + 1))
                dve.wait_ge(S["zc"], i * 2 + (2 * n + 2))
                dve.tensor_tensor(HID[:, :], ZG[:, :], ZA[:, :], ALU.mult).then_inc(S["hid"], 1)
                dve.wait_ge(S["hidh"], i + (n + 1))
                dve.tensor_tensor(HIDL[:, ds(i, 1), :].rearrange("p a n -> p (a n)"), HID[:, :],
                                  HIDH[:, ds(i, 1), :].rearrange("p a n -> p (a n)").bitcast(F32),
                                  ALU.subtract).then_inc(S["hidl"], 1)

            def columns(layer, mix):
                k = 0 if mix else 3
                g = par("gmix" if mix else "gffn", KD * layer, KD)
                link(dve.scalar_tensor_tensor(AB[:, 0, :], mod(layer, k + 1), 1.0, g, ALU.add, ALU.mult))
                dve.tensor_copy(AB[:, 1, :], mod(layer, k)).then_inc(S["ab"], 1)

            def sums_ready():
                dve.tensor_copy(SC[:, 3:4], ONES[:, 0:1]).then_inc(S["ssq"], 1)

            link(dve.memset(SSQ[:, :], 0.0))
            columns(0, False)
            for j in range(2):
                residual("wo", j, 0)
            with dve.Fori(0, 3) as i:
                for j in range(2):
                    residual("wo", 2 + j, 0, i, 2)
            dve.wait_ge(S["radd"], 8)
            sums_ready()
            for l in range(2):
                if l == 1:
                    dve_hyena(dve, norm, link, own, columns, sums_ready, add_squares)
                norm(f"ffn{l}", X, HH, HL, L, RT, TN, TM)
                link(dve.memset(SSQ[:, :], 0.0))
                with repeat(dve, KF, (own, 2)) as i:
                    ffn_up(l, i)
                with dve.Fori(0, 4) as i:
                    for j in range(2):
                        residual(f"down{l}", j, l, i, 2, tiles=2, gate=5)
                dve.wait_ge(S["radd"], RBASE[f"down{l}"] + 8)
                sums_ready()
                if l == 0:
                    columns(1, True)
            dve_second(dve, norm, link, own, reduce_angle, add_squares, sums_ready)


def constants():
    f4 = np.float32
    t = np.linspace(0.0, 1.0, L, dtype=f4)
    w = (f4(TWO_PI) * np.arange(L, dtype=f4) / f4(L)).astype(f4)
    f = np.linspace(1e-4, HY_BANDS - 1, HY_BANDS, dtype=f4)
    wf = (w[:, None] * f).astype(f4).astype(np.float64)
    zt = np.concatenate([t[:, None], np.cos(wf), -np.sin(wf)], axis=1).T.astype(f4)
    half = ROPE // 2
    inv = (10000.0 ** (-np.arange(0, half, 2, dtype=np.float64) / half)).astype(f4)
    row = np.repeat(np.arange(L // GRID_W, dtype=f4), GRID_W)
    col = np.tile(np.arange(GRID_W, dtype=f4), L // GRID_W)
    ar, ac = row[:, None] * inv, col[:, None] * inv
    ang = np.concatenate([ar, ar, ac, ac], axis=1).astype(np.float64).T
    q = ROPE // 4
    sign = np.repeat([-1.0, 1.0, -1.0, 1.0], q)[:, None]
    cos, sin = np.cos(ang), np.sin(ang) * sign
    qtab = np.concatenate([np.ones((NOPE, L)), cos, sin]) / math.sqrt(NOPE + ROPE)
    kcos = np.concatenate([cos, cos])
    ksin = np.concatenate([sin, sin])
    tt, ff = np.arange(L), np.arange(L)
    turn = (tt[:, None] * (2 * ff[None, :] + 1)) % (4 * L)
    th = np.pi * turn / (2 * L)
    c, s = np.cos(th), np.sin(th)
    fwd = np.stack([c, s]).reshape(2, 4, P, 4, P).transpose(3, 2, 0, 1, 4)
    inv_t = np.stack([c.T, s.T]).reshape(2, 4, P, L).transpose(2, 0, 1, 3) / L
    tvec = np.broadcast_to(np.arange(L, dtype=f4), (P, L))
    asf = lambda x: np.ascontiguousarray(x, dtype=f4)
    pos = np.arange(16)
    invc = np.stack([1.0 / np.minimum(pos + 1, win) for win in (2, 4, 8, 16)])
    return dict(zt=asf(zt), qtab=asf(qtab), kcos=asf(kcos), ksin=asf(ksin), dft=asf(fwd.reshape(4, P, 8 * P)),
                idft=asf(inv_t.reshape(P, 8, L)), tvec=asf(tvec)), asf(-t.reshape(4, P).T), asf(
                    np.broadcast_to(invc.reshape(1, 64), (P, 64)))


def tiles(w):
    k, n = w.shape
    return w.reshape(k // P, P, n // P, P).transpose(2, 1, 0, 3).reshape(n // P, P, k)


def cols(v):
    return v.reshape(-1, P).T


def lay_out(x):
    g = {}
    g["x"] = x["x"][0].T.reshape(KD, P, L).transpose(1, 0, 2)
    g["ctx"] = x["ctx"][0].T.reshape(KD, P, LC).transpose(1, 0, 2)
    g["c"] = x["c"].reshape(D)
    g["cc"] = x["c_ctx"].reshape(D)
    g["modw"] = x["mod_w"].transpose(0, 2, 1).reshape(96, P, D)
    g["wdq"] = tiles(x["mla_w_dq"][0])
    dkv = x["mla_w_dkv"][0]
    q = ROPE // 4
    perm = np.concatenate([np.arange(q, 2 * q), np.arange(q), np.arange(3 * q, 4 * q), np.arange(2 * q, 3 * q)])
    kr = dkv[:, KVL:]
    g["wdkv"] = tiles(np.concatenate([dkv[:, :KVL], kr, kr, kr[:, perm], kr[:, perm]], axis=1))
    g["wuv"] = x["mla_w_uv"][0].reshape(2, P, 2, 512).transpose(2, 1, 0, 3).reshape(2, P, 1024)
    uq = x["mla_w_uq"][0].reshape(QL, HEADS, NOPE + ROPE)
    uq = np.concatenate([uq, uq[:, :, NOPE:][:, :, perm]], axis=2).reshape(QL, HEADS * P)
    uq = tiles(uq).reshape(HEADS // 2, 2, P, 4 * P).transpose(0, 2, 1, 3).reshape(HEADS // 2, P, 8 * P)
    g["whead"] = np.concatenate([uq, tiles(x["mla_w_uk"][0])], axis=2)
    g["wo"] = tiles(x["mla_w_o"][0])
    for l in range(2):
        up = tiles(x["ffn_w_up"][l])
        g[f"wup{l}"] = up.reshape(2, KF, P, D).transpose(1, 0, 2, 3).reshape(NUP, P, D)
        dn = tiles(x["ffn_w_down"][l])
        g[f"wdn{l}"] = dn.reshape(8, P, 2, 11 * P).transpose(0, 2, 1, 3).reshape(16, P, 11 * P)
    hy = tiles(x["hy_w_in"][0]).reshape(3, KD, P, D)
    g["whin"] = hy[[1, 2, 0]].transpose(1, 0, 2, 3).reshape(24, P, D)
    g["whout"] = tiles(x["hy_w_out"][0])
    g["fw1"], g["fw2"] = x["hy_f_w1"][0], x["hy_f_w2"][0]
    g["fw3"] = x["hy_f_w3"][0].reshape(HID_F, 2, D).transpose(1, 0, 2).reshape(P, D)
    g["fpar"] = np.stack([x["hy_f_b1"][0], x["hy_f_freq1"][0], x["hy_f_b2"][0], x["hy_f_freq2"][0]], axis=1)
    g["decay"] = x["hy_decay"].reshape(D)
    w2 = tiles(x["w_in_2"][0])
    g["win2a"] = np.concatenate([w2[8:12], w2[0:4]])
    za, zb, ga, gb = w2[4:8], w2[12:16], w2[16:24].reshape(4, 2, P, D), w2[24:32].reshape(4, 2, P, D)
    g["win2b"] = np.concatenate([za[:, None], zb[:, None], ga, gb], axis=1).reshape(24, P, D)
    g["wglu"] = tiles(x["ssm_w_glu_2"][0])
    g["wpool"] = x["pool_w_2"][0].transpose(1, 0, 2).reshape(1, P, 4 * P)
    g["wbr"] = np.concatenate([tiles(x["w_branch_a_2"][0]), tiles(x["w_branch_b_2"][0])], axis=2)
    g["wout2"] = tiles(x["w_out_2"][0])
    b = [x[n].reshape(NM, P, GC) for n in ("ssm_b_re_2", "ssm_b_im_2")]
    c = [x[n].reshape(NM, 2, GC, ST).transpose(0, 1, 3, 2).reshape(NM, P, GC) for n in ("ssm_c_re_2", "ssm_c_im_2")]
    g["s5bc"] = np.stack(b + c).transpose(2, 0, 1, 3)
    consts, tcol, invc = constants()
    g.update(consts)
    packed = dict(
        modb=cols(x["mod_b"]), gmix=cols(x["norm_mix_g"]), gffn=cols(x["norm_ffn_g"]), gq=cols(x["mla_g_q"]),
        gkv=cols(x["mla_g_kv"]), hbin=cols(x["hy_b_in"]), hcw=cols(x["hy_conv_w"]), hcb=cols(x["hy_conv_b"]),
        hdb=cols(x["hy_d_bias"]), hbo=cols(x["hy_b_out"]), fcw=cols(x["ffn_conv_w"]), fcb=cols(x["ffn_conv_b"]),
        gfin=cols(x["final_g"]), g2=cols(x["norm_g_2"]), bin2=cols(x["b_in_2"]), sd=cols(x["ssm_d_2"]),
        bglu=cols(x["ssm_b_glu_2"]), pscale=cols(x["pool_scale_2"]), gfin2=cols(x["final_norm_g_2"]),
        logdt=cols(np.repeat(x["ssm_log_dt_2"].reshape(GROUPS, 1), ST, axis=1)), lre=cols(x["ssm_lam_re_2"]),
        lim=cols(x["ssm_lam_im_2"]), tcol=tcol, invc=invc)
    g["par"] = np.concatenate([packed[n] for n, _ in PARAMS], axis=1)
    return {n: np.ascontiguousarray(v) for n, v in g.items()}


def kernel(**inputs):
    import concourse.bacc as bacc
    from concourse.bass_utils import run_bass_kernel_spmd

    nc = bacc.Bacc("TRN2", target_bir_lowering=False, num_devices=1)
    arrays = lay_out({n: np.asarray(v) for n, v in inputs.items()})
    aps = {n: nc.dram_tensor(f"in_{n}", v.shape, F32, kind="ExternalInput").ap() for n, v in arrays.items()}
    aps["out"] = nc.dram_tensor("out_y", (P, KD, L), F32, kind="ExternalOutput").ap()
    build(nc, aps)
    r = run_bass_kernel_spmd(nc, [{f"in_{n}": v for n, v in arrays.items()}], core_ids=[0])
    y = r.results[0]["out_y"]
    return y.transpose(1, 0, 2).reshape(D, L).T[None]
```
